# Optimizing a Trainium2 kernel written in Bass

```python
import jax, jax.numpy as jnp
from jax import lax
import numpy as np

D_MODEL = 1024
BATCH = 1
SEQ = 512
DEPTH = 1

PLE_DIM = 256
NORM_EPS = 1e-6
RW_HEADS = 8
RW_HEAD_DIM = 64
RW_WIDTH = RW_HEADS * RW_HEAD_DIM
DECAY_LORA = 64
AAA_LORA = 64
GATE_LORA = 160
RW_COLS = 3 * RW_WIDTH + DECAY_LORA + AAA_LORA + GATE_LORA
RW_LN_EPS = 64e-5
ATT_GROUPS = ((128, 1), (512, 4), (2048, 16))
ATT_HEADS_PER_GROUP = 4
ATT_HEADS = ATT_HEADS_PER_GROUP * len(ATT_GROUPS)
ATT_HEAD_DIM = 64
ATT_WIDTH = ATT_HEADS * ATT_HEAD_DIM
ATT_OUT = ATT_HEADS_PER_GROUP * ATT_HEAD_DIM
ATT_COLS = 3 * ATT_WIDTH
IN_COLS = RW_COLS + ATT_COLS
D_FF = 3 * D_MODEL
CONV_WIDTH = 3

kernel_name = "hybrid_rwkv7_dilated_alibi_convglu"

def rms_norm(x, g):
    xf = x.astype(jnp.float32)
    y = xf * lax.rsqrt(jnp.mean(xf * xf, axis=-1, keepdims=True) + NORM_EPS)
    return (y * g.astype(jnp.float32)).astype(x.dtype)

def shift_right(u, n):
    if n == 0:
        return u
    return jnp.pad(u, ((0, 0), (n, 0), (0, 0)))[:, :-n]

def alibi_slopes(n):
    return jnp.asarray(np.array([2.0 ** (-8.0 * (h + 1) / n) for h in range(n)], dtype=np.float32))

def rwkv7_time_mix(P, mu, w0, w_up, a0, a_up, g_up, k_k, k_a, r_k, ln_g, ln_b):
    B, T, _ = P.shape
    H, N = RW_HEADS, RW_HEAD_DIM
    Pm = P + (shift_right(P, 1) - P) * mu
    cuts = list(np.cumsum([RW_WIDTH, RW_WIDTH, RW_WIDTH, DECAY_LORA, AAA_LORA]))
    r, k, v, xw, xa, xg = jnp.split(Pm, cuts, axis=-1)
    w = -jax.nn.softplus(-(w0 + jnp.tanh(xw) @ w_up)) - 0.5
    decay = jnp.exp(-jnp.exp(w.astype(jnp.float32)))
    a = jax.nn.sigmoid(a0 + xa @ a_up)
    g = jax.nn.sigmoid(xg) @ g_up
    hs = lambda z: z.astype(jnp.float32).reshape(B, T, H, N)
    r, k, v, a, decay = hs(r), hs(k), hs(v), hs(a), hs(decay)
    kk = k * k_k.reshape(H, N)
    kk = kk / jnp.maximum(jnp.linalg.norm(kk, axis=-1, keepdims=True), 1e-12)
    k = k * (1.0 + (a - 1.0) * k_a.reshape(H, N))
    a_vec = -kk
    b_vec = kk * a

    def step(S, inp):
        r_t, w_t, k_t, v_t, a_t, b_t = inp
        Sa = jnp.einsum("bhvk,bhk->bhv", S, a_t)
        S = S * w_t[:, :, None, :] + Sa[..., None] * b_t[:, :, None, :] + v_t[..., None] * k_t[:, :, None, :]
        y = jnp.einsum("bhvk,bhk->bhv", S, r_t)
        return S, y

    tm = lambda z: jnp.swapaxes(z, 0, 1)
    S0 = jnp.zeros((B, H, N, N), jnp.float32)
    _, y = lax.scan(step, S0, (tm(r), tm(decay), tm(k), tm(v), tm(a_vec), tm(b_vec)))
    y = jnp.swapaxes(y, 0, 1)
    mean = jnp.mean(y, axis=-1, keepdims=True)
    var = jnp.mean(jnp.square(y - mean), axis=-1, keepdims=True)
    y = ((y - mean) * lax.rsqrt(var + RW_LN_EPS)).reshape(B, T, RW_WIDTH) * ln_g + ln_b
    bonus = (jnp.sum(r * k * r_k, axis=-1, keepdims=True) * v).reshape(B, T, RW_WIDTH)
    return ((y + bonus) * g).astype(P.dtype)

def dilated_group_attention(q, k, v, window, dilation, slopes):
    B, T, H, E = q.shape
    L = window // dilation
    span = L * dilation
    Tp = -(-T // span) * span
    pad = Tp - T
    nb = Tp // span

    def to_blocks(z):
        z = jnp.pad(z, ((0, 0), (0, pad), (0, 0), (0, 0)))
        return z.reshape(B, nb, L, dilation, H, E)

    def with_prev(z):
        zp = jnp.pad(z, ((0, 0), (1, 0), (0, 0), (0, 0), (0, 0), (0, 0)))[:, :-1]
        return jnp.concatenate([zp, z], axis=2)

    qb = to_blocks(q)
    kc = with_prev(to_blocks(k))
    vc = with_prev(to_blocks(v))
    s = jnp.einsum("bnqrhe,bnkrhe->bnrhqk", qb, kc).astype(jnp.float32) * (E ** -0.5)
    qi = jnp.arange(L)[:, None]
    kj = jnp.arange(2 * L)[None, :]
    steps = qi + L - kj
    blk = jnp.arange(nb)[:, None, None]
    valid = (steps >= 0) & (steps <= L) & (blk * L - L + kj >= 0)
    bias = -slopes[:, None, None] * (dilation * steps).astype(jnp.float32)[None]
    logits = jnp.where(valid[None, :, None, None], s + bias, -jnp.inf)
    lse = jax.nn.logsumexp(logits, axis=-1)
    prob = jnp.exp(logits - lse[..., None])
    o = jnp.einsum("bnrhqk,bnkrhe->bnqrhe", prob.astype(v.dtype), vc)
    o = o.reshape(B, Tp, H, E)[:, :T]
    lse = jnp.moveaxis(lse, 4, 2).reshape(B, Tp, H)[:, :T]
    return o, lse

def dilated_mixture_attention(P, slopes):
    B, T, _ = P.shape
    q, k, v = [z.reshape(B, T, ATT_HEADS, ATT_HEAD_DIM) for z in jnp.split(P, 3, axis=-1)]
    outs, lses = [], []
    for gi, (window, dilation) in enumerate(ATT_GROUPS):
        hsl = slice(gi * ATT_HEADS_PER_GROUP, (gi + 1) * ATT_HEADS_PER_GROUP)
        o, l = dilated_group_attention(q[:, :, hsl], k[:, :, hsl], v[:, :, hsl], window, dilation, slopes[hsl])
        outs.append(o.astype(jnp.float32))
        lses.append(l)
    wts = jax.nn.softmax(jnp.stack(lses, axis=0), axis=0)
    o = jnp.sum(wts[..., None] * jnp.stack(outs, axis=0), axis=0)
    return o.reshape(B, T, ATT_OUT).astype(P.dtype)

def conv_glu_ffn(h, w_up, conv_w, conv_b, w_down):
    u = h @ w_up
    u = conv_b + sum(conv_w[j] * shift_right(u, j) for j in range(CONV_WIDTH))
    gate, val = jnp.split(u, 2, axis=-1)
    return (jax.nn.gelu(gate, approximate=True) * val) @ w_down

def setup_inputs(seed: int = 0) -> dict:
    key = jax.random.key(seed)
    ks = jax.random.split(key, 32)
    Ld = DEPTH
    nrm = lambda kk, shape, fan: jax.random.normal(kk, shape, jnp.float32) * (fan ** -0.5)
    gain = lambda kk, n: 1.0 + 0.1 * jax.random.normal(kk, (Ld, n), jnp.float32)
    small = lambda kk, shape, s: s * jax.random.normal(kk, shape, jnp.float32)
    conv_w = jnp.array([1.0, 0.0, 0.0], jnp.float32)[None, :, None] + small(ks[22], (Ld, CONV_WIDTH, 2 * D_FF), 0.2)
    return {
        "x": jax.random.normal(ks[0], (BATCH, SEQ, D_MODEL), jnp.float32),
        "p": jax.random.normal(ks[1], (DEPTH, BATCH, SEQ, PLE_DIM), jnp.float32),
        "g_mix": gain(ks[2], D_MODEL),
        "w_in": nrm(ks[3], (Ld, D_MODEL, IN_COLS), D_MODEL),
        "rw_mu": jax.random.uniform(ks[4], (Ld, RW_COLS), jnp.float32),
        "rw_w0": jax.random.uniform(ks[5], (Ld, RW_WIDTH), jnp.float32, minval=-6.5, maxval=-1.5),
        "rw_w_up": 0.1 * nrm(ks[6], (Ld, DECAY_LORA, RW_WIDTH), DECAY_LORA),
        "rw_a0": small(ks[7], (Ld, RW_WIDTH), 0.1),
        "rw_a_up": nrm(ks[8], (Ld, AAA_LORA, RW_WIDTH), AAA_LORA),
        "rw_g_up": nrm(ks[9], (Ld, GATE_LORA, RW_WIDTH), GATE_LORA),
        "rw_k_k": 0.85 + small(ks[10], (Ld, RW_WIDTH), 0.05),
        "rw_k_a": 1.0 + small(ks[11], (Ld, RW_WIDTH), 0.05),
        "rw_r_k": small(ks[12], (Ld, RW_HEADS, RW_HEAD_DIM), 0.1),
        "rw_ln_g": gain(ks[13], RW_WIDTH),
        "rw_ln_b": small(ks[14], (Ld, RW_WIDTH), 0.01),
        "w_branch_a": nrm(ks[15], (Ld, RW_WIDTH, D_MODEL), RW_WIDTH),
        "w_branch_b": nrm(ks[16], (Ld, ATT_OUT, D_MODEL), ATT_OUT),
        "w_gate": nrm(ks[17], (Ld, D_MODEL, 2 * D_MODEL), D_MODEL),
        "b_gate": small(ks[18], (Ld, 2 * D_MODEL), 0.01),
        "w_out": nrm(ks[19], (Ld, D_MODEL, D_MODEL), D_MODEL),
        "g_ffn": gain(ks[20], D_MODEL),
        "w_up": nrm(ks[21], (Ld, D_MODEL, 2 * D_FF), D_MODEL),
        "conv_w": conv_w,
        "conv_b": small(ks[23], (Ld, 2 * D_FF), 0.01),
        "w_down": nrm(ks[24], (Ld, D_FF, D_MODEL), D_FF),
        "g_ple": gain(ks[25], D_MODEL),
        "w_ple_gate": nrm(ks[26], (Ld, D_MODEL, D_MODEL), D_MODEL),
        "w_ple": nrm(ks[27], (Ld, PLE_DIM, D_MODEL), PLE_DIM),
        "g_final": 1.0 + 0.1 * jax.random.normal(ks[28], (D_MODEL,), jnp.float32),
    }

def reference(x, p, g_mix, w_in, rw_mu, rw_w0, rw_w_up, rw_a0, rw_a_up, rw_g_up, rw_k_k, rw_k_a, rw_r_k,
              rw_ln_g, rw_ln_b, w_branch_a, w_branch_b, w_gate, b_gate, w_out, g_ffn, w_up, conv_w, conv_b,
              w_down, g_ple, w_ple_gate, w_ple, g_final):
    slopes = alibi_slopes(ATT_HEADS)
    for i in range(DEPTH):
        h = rms_norm(x, g_mix[i])
        proj = h @ w_in[i]
        y_a = rwkv7_time_mix(proj[..., :RW_COLS], rw_mu[i], rw_w0[i], rw_w_up[i], rw_a0[i], rw_a_up[i],
                             rw_g_up[i], rw_k_k[i], rw_k_a[i], rw_r_k[i], rw_ln_g[i], rw_ln_b[i])
        y_b = dilated_mixture_attention(proj[..., RW_COLS:], slopes)
        gate_a, gate_b = jnp.split(jax.nn.sigmoid(h @ w_gate[i] + b_gate[i]), 2, axis=-1)
        merged = gate_a * (y_a @ w_branch_a[i]) + gate_b * (y_b @ w_branch_b[i])
        x = x + merged @ w_out[i]
        x = x + conv_glu_ffn(rms_norm(x, g_ffn[i]), w_up[i], conv_w[i], conv_b[i], w_down[i])
        ple_gate = jax.nn.sigmoid(rms_norm(x, g_ple[i]) @ w_ple_gate[i])
        x = x + ple_gate * (p[i] @ w_ple[i])
    return rms_norm(x, g_final)


_drawn_inputs = setup_inputs


def setup_inputs(seed=0):
    import zlib

    import numpy as np

    out = dict(_drawn_inputs(seed))
    spreads = {}
    factors = {'rw_w_up': 41.298,
     'rw_a0': 4.867,
     'rw_k_k': 12.119,
     'rw_k_a': 3.251,
     'rw_ln_b': 8.0,
     'b_gate': 39.386,
     'conv_b': 7.849,
     'g_ple': 3.734}
    for name, (base, spread) in spreads.items():
        noise = np.random.default_rng([zlib.crc32(name.encode()), seed]).standard_normal(out[name].shape)
        drawn = base * np.exp(spread * noise) if base else spread * noise
        out[name] = __import__('jax').numpy.asarray(drawn.astype(out[name].dtype))
    for name, factor in factors.items():
        out[name] = (out[name] * factor).astype(out[name].dtype)
    return out
```

```python
from contextlib import ExitStack

import numpy as np

import concourse.bass as bass
from concourse import mybir

P = 128
F32 = mybir.dt.float32
F32R = mybir.dt.float32r
ALU = mybir.AluOpType
ACT = mybir.ActivationFunctionType
AX_X = mybir.AxisListType.X

SEQ, DM, PLE = 512, 1024, 256
NH, HD = 8, 64
RW = NH * HD
ATT_H, ATT_HG = 12, 4
ATT_W = ATT_H * HD
DFF = 3 * DM
NT = SEQ // P
KD = DM // P
NPAIR = RW // P
CH = 64
NCH = SEQ // CH
NF = DFF // P
NORM_EPS, LN_EPS = 1e-6, 64e-5
DECAY = float(np.exp(-0.5))
UNIT = 1024
RAW_SLOTS, W_SLOTS, BANKS = 3, 2, 8
GROUPS = ((128, 1), (512, 4), (2048, 16))
SLOPES = [2.0 ** (-8.0 * (h + 1) / ATT_H) for h in range(ATT_H)]
FAR = 1e30

PARAM_ROWS = [("rw_mu", 15), ("rw_w0", 4), ("rw_a0", 4), ("rw_k_k", 4), ("rw_k_a", 4), ("rw_r_k", 4),
              ("rw_ln_g", 4), ("rw_ln_b", 4), ("g_mix", 8), ("g_ffn", 8), ("g_ple", 8), ("b_gate", 16)]
PARAM_COL, _n = {}, 0
for _name, _rows in PARAM_ROWS:
    PARAM_COL[_name] = _n
    _n += _rows
PARAM_USED = [_n, 96, 96]
PARAM_COL["conv_w0"], PARAM_COL["conv_w1"] = P, P + 48
PARAM_COL["conv_w2"], PARAM_COL["conv_b"] = 2 * P, 2 * P + 48

CONST_NAMES = ["ident", "heads", "strict_st", "incl_st", "strict_ts", "off1_st", "off1_ts",
               "off2", "off4", "off8", "off16", "off32"]


def shape_constants():
    i = np.arange(P)
    same = (i[:, None] // CH) == (i[None, :] // CH)
    r, c = i[:, None] % CH, i[None, :] % CH

    def off(b):
        return same & (r // (2 * b) == c // (2 * b)) & (r % (2 * b) < b) & (c % (2 * b) >= b)

    parts = {"ident": r * 0 + (i[:, None] == i[None, :]), "heads": same, "strict_st": same & (r < c),
             "incl_st": same & (r <= c), "strict_ts": same & (r > c), "off1_st": off(1),
             "off1_ts": off(1).T}
    for b in (2, 4, 8, 16, 32):
        parts[f"off{b}"] = off(b)
    reset = np.broadcast_to((np.arange(SEQ) % CH != 0)[None, :], (P, SEQ))
    consts = np.concatenate([np.asarray(parts[n], np.float32) for n in CONST_NAMES] + [reset.astype(np.float32)], 1)
    dist = []
    for (window, dilation), width in zip(GROUPS, (2 * P, SEQ, SEQ)):
        d = i[:, None] + (width - P) - np.arange(width)[None, :]
        ok = (d >= 0) & (d <= window) & (d % dilation == 0)
        dist.append(np.where(ok, d, FAR).astype(np.float32))
    return np.ascontiguousarray(consts), np.ascontiguousarray(np.concatenate(dist, 1))


SIGNALS = [
    "act_Bt", "act_E", "act_Kt", "act_U", "act_U1", "act_Vt", "act_chain", "act_exp", "act_fill", "act_g_hi",
    "act_gate", "act_gelu", "act_gn_sd", "act_gn_sq", "act_hi", "act_kk_sq", "act_kn", "act_la", "act_lg",
    "act_lora_act", "act_lw", "act_mg_hi", "act_own", "act_pg", "act_pp", "act_pt", "act_qk", "act_rms", "act_tap0",
    "act_vt0", "act_vt1", "act_y", "act_ya_hi", "act_yb_hi", "dve_Ak", "dve_L", "dve_P", "dve_Rb", "dve_Rk", "dve_Wp",
    "dve_X", "dve_Z", "dve_chain", "dve_derived", "dve_fill", "dve_final", "dve_g", "dve_g_lo", "dve_gn_d",
    "dve_hT_lo", "dve_kkr", "dve_max", "dve_merged", "dve_mg_lo", "dve_pT_lo", "dve_params", "dve_preC",
    "dve_psum_read", "dve_rk", "dve_shift", "dve_taps", "dve_x_nb", "dve_x_nc", "dve_x_ple", "dve_xn_a", "dve_xn_b",
    "dve_xn_c", "dve_y_a", "dve_ya_lo", "dve_yb_lo", "pe_A", "pe_AT", "pe_Ak", "pe_Bt", "pe_Kt", "pe_Rb", "pe_Rk",
    "pe_Vt", "pe_W", "pe_XTW", "pe_XW", "pe_bn", "pe_chain", "pe_dn", "pe_kn", "pe_la", "pe_lg", "pe_lw", "pe_mu",
    "pe_na", "pe_nb", "pe_nc", "pe_np", "pe_o", "pe_op", "pe_pa", "pe_par", "pe_pb", "pe_pg", "pe_pp", "pe_s", "pe_t",
    "pe_u1", "pe_u2", "pe_unit", "pe_var", "pe_vt0", "pe_vt1", "pe_y", "pe_z", "pool_chain", "pool_cleared",
    "pool_eps", "pool_lo", "pool_stage",
]


def weight_units():
    u = []
    for i in (12, 13, 14, 0, 1, 2, 3, 4, 5, 6, 7, 8, 9, 10, 11):
        u.append((("rw", i), "w_in", 0, 8, P * i, P))
    base = 1824
    for i in range(12):
        u.append((("qk", i), "w_in", 0, 8, base + P * i, P))
    for s in range(4):
        u.append((("v0", s), "w_in", 2 * P * s, 2, base + 2 * ATT_W, 512))
    for s in range(2):
        u.append((("v1", s), "w_in", 4 * P * s, 4, base + 2 * ATT_W + 512, 256))
    for i in range(16):
        u.append((("gate", i), "w_gate", 0, 8, P * i, P))
    for i in range(0, 8, 4):
        u.append((("bb", i), "w_branch_b", 0, 2, P * i, 512))
        u.append((("ba", i), "w_branch_a", 0, 4, P * i, 256))
        u.append((("ba", i + 2), "w_branch_a", 0, 4, P * (i + 2), 256))
    for h in range(2):
        for s in range(4):
            u.append((("out", h, s), "w_out", 2 * P * s, 2, 512 * h, 512))
    for i in range(NF):
        u.append((("up", i), "w_up", 0, 8, P * i, P))
        u.append((("up", NF + i), "w_up", 0, 8, DFF + P * i, P))
    for h in range(2):
        for s in range(NF // 2):
            u.append((("down", h, s), "w_down", 2 * P * s, 2, 512 * h, 512))
    for h in range(2):
        u.append((("ple", h), "w_ple", 0, 2, 512 * h, 512))
    for h in range(2):
        for s in range(4):
            u.append((("pleg", h, s), "w_ple_gate", 2 * P * s, 2, 512 * h, 512))
    return u


UNITS = weight_units()
UIDX = {x[0]: n for n, x in enumerate(UNITS)}


def build(nc, ins, out, known):
    W = {}
    for name in ("w_in", "w_gate", "w_branch_a", "w_branch_b", "w_out", "w_up", "w_down", "w_ple_gate", "w_ple"):
        W[name] = ins[name].rearrange("l k n -> (l k) n")
    x_d = ins["x"].rearrange("b (m p) d -> p (b m) d", p=P)
    out_d = out.rearrange("b (m p) d -> p (b m) d", p=P)
    p_d = ins["p"].rearrange("l b (m p) d -> p (l b m) d", p=P)

    with ExitStack() as ctx:
        def sem(name):
            return ctx.enter_context(nc.semaphore(name))

        base = -(-nc.sbuf_base // 64) * 64
        top = [base]

        def sb_at(name, shape, dt, offset):
            return nc.alloc_sbuf_tensor_at(name, shape, dt, offset=offset)

        def sb(name, words, shape=None, dt=F32):
            t = sb_at(name, shape or [P, words], dt, top[0])
            top[0] += 4 * words
            return t

        consts = sb("consts", 2048)
        params = sb("params", 3 * P)
        stat = sb("stat", 256)
        hT_hi = sb("hT_hi", 4096, [P, KD, SEQ], F32R)
        hT_lo = sb("hT_lo", 4096, [P, KD, SEQ], F32R)
        raw = sb("raw", RAW_SLOTS * UNIT, [P, RAW_SLOTS, UNIT])
        w_hi = sb("w_hi", W_SLOTS * UNIT, [P, W_SLOTS, UNIT], F32R)
        w_lo = sb("w_lo", W_SLOTS * UNIT, [P, W_SLOTS, UNIT], F32R)
        yb_hi = sb("yb_hi", 1024, [P, 2, SEQ], F32R)
        yb_lo = sb("yb_lo", 1024, [P, 2, SEQ], F32R)
        R0 = top[0]
        KB = 1024
        assert R0 + 128 * KB <= nc.sbuf_usable_end, (R0, nc.sbuf_usable_end)

        def at(name, kb, shape, dt=F32):
            return sb_at(name, shape, dt, R0 + int(kb * KB))

        xs = at("xs", 56, [P, NT, DM])
        xn_a = at("xn_a", 72, [P, NT, DM])
        stage = at("stage", 88, [P, 3, P])
        Rr, Kk, Aa, KK, Vv, Gg, Bo = [at(n, 8 * i, [P, NPAIR, SEQ]) for i, n in
                                      enumerate(("Rr", "Kk", "Aa", "KK", "Vv", "Gg", "Bo"))]
        qk = at("qk", 56, [P, 12, SEQ])
        vtok = at("vtok", 80, [P, NT, ATT_W])
        dist = at("dist", 92, [P, 2 * P + 2 * SEQ])
        Sx = at("Sx", 97, [P, 2, 1280])
        PT = at("PT", 107, [P, 10, P])
        names = ["Bf", "Kf", "Vf", "Xx", "XT", "Am", "Ak", "Rb", "Rk", "Vt", "Bt", "Kt"]
        CM = {n: at(n, 56 + 4 * i, [P, 2, 512]) for i, n in enumerate(names)}
        At = at("At", 104, [P, 4, 512])
        Rt = at("Rt", 120, [P, 4, 512])
        Zs = at("Zs", 112, [P, 2, 512])
        Wp = at("Wp", 116, [P, 2, 512])
        lora_x = at("lora_x", 112, [P, 3, SEQ])
        lora_w = at("lora_w", 118, [P, 3, RW])
        Lt, Et, Ei, Sc = [at(n, 112 + 4 * i, [P, 2, SEQ]) for i, n in enumerate(("Lt", "Et", "Ei", "Sc"))]
        sig = at("sig", 56, [P, 16, SEQ])
        ya_hi = at("ya_hi", 88, [P, NPAIR, SEQ], F32R)
        ya_lo = at("ya_lo", 96, [P, NPAIR, SEQ], F32R)
        gn = at("gn", 104, [P, NPAIR, SEQ])
        mg_hi = at("mg_hi", 0, [P, KD, SEQ], F32R)
        mg_lo = at("mg_lo", 16, [P, KD, SEQ], F32R)
        xr = at("xr", 112, [P, NT, DM])
        xn_b = at("xn_b", 32, [P, NT, DM])
        g_hi = at("g_hi", 0, [P, NF, SEQ], F32R)
        g_lo = at("g_lo", 48, [P, NF, SEQ], F32R)
        cbuf = at("cbuf", 96, [P, 2, 4, SEQ])
        p_raw = at("p_raw", 96, [P, NT, PLE])
        pT_hi = at("pT_hi", 100, [P, 2, SEQ], F32R)
        pT_lo = at("pT_lo", 104, [P, 2, SEQ], F32R)
        xn_c = at("xn_c", 0, [P, NT, DM])
        psig = at("psig", 16, [P, NT, 512])
        gfin = at("gfin", 24, [P, DM])
        pple = at("pple", 28, [P, NT, DM])
        junk = at("junk", 44, [P, DM])

        def cst(n):
            k = CONST_NAMES.index(n)
            return consts[:, k * P:(k + 1) * P]

        def cst4(n):
            return cst(n).unsqueeze(1).broadcast_to([P, NPAIR, P])

        reset = consts[:, len(CONST_NAMES) * P:len(CONST_NAMES) * P + SEQ]
        ident = cst("ident")

        def par(name, i, lo=0, hi=P):
            c = PARAM_COL[name] + i
            return params[lo:hi, c:c + 1]

        omm, omka, ec, ss, rstd = 0, 16, 32, 96, 100
        negmax, den, rden, epsc = 112, 128, 144, 160

        bank = [ctx.enter_context(nc.psum_tensor(f"bank{i}", [P, 512], F32)) for i in range(BANKS)]

        x_in, par_in, cst_in, dist_in, lora_in, xr_in, p_in, gf_in, out_done = [
            sem(n) for n in ("x_in", "par_in", "cst_in", "dist_in", "lora_in", "xr_in", "p_in", "gf_in", "out_done")]
        landed = [sem(f"landed{i}") for i in range(RAW_SLOTS)]
        signal = {name: sem(name) for name in SIGNALS}

        count = {name: 0 for name in signal}
        latest, steps, readers, turn = {}, {}, {}, {}
        earlier = known or {"steps": {}, "readers": {}, "turn": {}}

        def step(who, *labels):
            name = f"{who}_{labels[0][0]}" if labels else f"{who}_chain"
            count[name] += 1
            latest[who] = (name, count[name])
            for label in labels:
                steps[(who,) + label] = latest[who]
            return signal[name], 1

        def frees(who, bank_label, *labels):
            got = step(who, *(labels or (("psum_read",),)))
            readers[bank_label] = latest[who]
            return got

        def done(who, *label):
            name, n = earlier["steps"].get((who,) + label, (f"{who}_chain", 1))
            return signal[name], n

        def previous(who):
            name, n = latest[who]
            return signal[name], n

        def psum(label):
            return bank[earlier["turn"].get(label, 0) % BANKS]

        order = []
        block = ctx.enter_context(nc.Block())
        n_par = len(PARAM_ROWS) + 1 + 4

        def fill_blocks(who, copy, gr, parts):
            for n, (dst, slot, src) in enumerate(parts):
                for q in range(2):
                    r = slice(CH * q, CH * q + CH)
                    for s in range(2):
                        c = 2 * gr + s
                        d = dst[r, slot + s, :].rearrange("p (h two t) -> p h two t", two=2, t=CH)[:, :, q, :]
                        last = (("fill", gr),) if n == len(parts) - 1 and q == 1 and s == 1 else ()
                        copy(d, src[r, :, c * CH:(c + 1) * CH]).then_inc(*step(who, *last))

        @block.sync
        def _(sp):
            sp.dma_start(xs[:, 0:2, :], x_d[:, 0:2, :]).then_inc(x_in, 16)
            sp.dma_start(xs[:, 2:4, :], x_d[:, 2:4, :]).then_inc(x_in, 16)
            for n, (label, name, r0, t, c0, w) in enumerate(UNITS):
                if n >= RAW_SLOTS:
                    sp.wait_ge(*done("pool", "lo", n - RAW_SLOTS))
                src = W[name][r0:r0 + t * P, c0:c0 + w].rearrange("(t p) n -> p t n", p=P)
                dst = raw[:, n % RAW_SLOTS, :].rearrange("p (t n) -> p t n", t=t)
                sp.dma_start(dst, src).then_inc(landed[n % RAW_SLOTS], 16)
                if label == ("out", 0, 1):
                    sp.wait_ge(*done("act", "ya_hi", NPAIR - 1))
                    sp.dma_start(xr[:, :, :], x_d).then_inc(xr_in, 16)
                if label == ("down", 0, 4):
                    sp.wait_ge(*done("dve", "g_lo", NF - 1))
                    sp.dma_start(p_raw[:, :, :], p_d).then_inc(p_in, 16)
                if label == ("pleg", 0, 3):
                    sp.wait_ge(*done("pe", "dn", 1, NT - 1))
                    sp.dma_start(gfin[:, :], ins["g_final"].partition_broadcast(P)).then_inc(gf_in, 16)
            for m in range(NT):
                sp.wait_ge(*done("dve", "final", m))
                sp.dma_start(out_d[:, m, :], xr[:, m, :]).then_inc(out_done, 16)
            sp.wait_ge(out_done, 16 * NT)

        @block.gpsimd
        def _(gp):
            nc.gpsimd.memset(stage[:, :, :], 0.0).then_inc(*step("pool", ("stage",)))
            nc.gpsimd.memset(stat[:, epsc:epsc + 1], NORM_EPS).then_inc(*step("pool"))
            nc.gpsimd.memset(stat[:, epsc + 1:epsc + 2], LN_EPS).then_inc(*step("pool", ("eps",)))
            gp.wait_ge(*done("pool", "stage"))
            for name, rows in PARAM_ROWS:
                c = PARAM_COL[name]
                src = ins[name].rearrange("l a b -> l (a b)") if name == "rw_r_k" else ins[name]
                full = src.shape[1] // P
                gp.dma_start(stage[c:c + full, 0, :], src[0, 0:full * P].rearrange("(r n) -> r n", n=P)).then_inc(par_in, 16)
                if full < rows:
                    gp.dma_start(stage[c + full:c + rows, 0, 0:src.shape[1] - full * P],
                                 src[:, full * P:]).then_inc(par_in, 16)
            for b, r, src in ((1, 0, ins["conv_w"][0, 0]), (1, 48, ins["conv_w"][0, 1]),
                              (2, 0, ins["conv_w"][0, 2]), (2, 48, ins["conv_b"][0])):
                gp.dma_start(stage[r:r + 48, b, :], src.rearrange("(r n) -> r n", n=P)).then_inc(par_in, 16)

            def clear_chunks():
                gp.wait_ge(*done("pe", "o", 15))
                gp.wait_ge(*done("dve", "preC", NPAIR - 1))
                for n in ("Bf", "Kf", "Vf"):
                    nc.gpsimd.memset(CM[n][:, :, :], 0.0).then_inc(*step("pool"))
                nc.gpsimd.memset(At[:, :, :], 0.0).then_inc(*step("pool"))
                nc.gpsimd.memset(Rt[:, :, :], 0.0).then_inc(*step("pool"))
                nc.gpsimd.memset(Zs[:, 0, :], 0.0).then_inc(*step("pool", ("cleared",)))

            for n in range(len(UNITS)):
                if n == UIDX[("gate", 0)] + 1:
                    clear_chunks()
                gp.wait_ge(*done("act", "hi", n))
                nc.gpsimd.tensor_tensor(w_lo[:, n % W_SLOTS, :], raw[:, n % RAW_SLOTS, :],
                    w_hi[:, n % W_SLOTS, :].bitcast(F32), ALU.subtract).then_inc(*step("pool", ("lo", n)))

        @block.tensor
        def _(pe):
            def begin(*label):
                n = len(order)
                order.append(label)
                turn[label] = n
                if n >= BANKS:
                    name, at_ = earlier["readers"].get(order[n - BANKS], ("dve_psum_read", 1))
                    pe.wait_ge(signal[name], at_)
                return bank[n % BANKS]

            def split3(o, wh, wl, ah, al, first, last):
                nc.tensor.matmul(o, wh, ah, start=first, stop=False)
                nc.tensor.matmul(o, wh, al, start=False, stop=False)
                return nc.tensor.matmul(o, wl, ah, start=False, stop=last)

            def feature_unit(label, *bank_label):
                n = UIDX[label]
                o = begin(*bank_label)
                pe.wait_ge(*done("pool", "lo", n))
                for t in range(KD):
                    k = slice(t * P, (t + 1) * P)
                    mm = split3(o[:, :], w_hi[:, n % W_SLOTS, k], w_lo[:, n % W_SLOTS, k],
                                hT_hi[:, t, :], hT_lo[:, t, :], t == 0, t == KD - 1)
                mm.then_inc(*step("pe", ("unit", n), bank_label))

            def token_units(labels, outs, a_hi, a_lo, kts, cols):
                bs = [begin(*o) for o in outs]
                for s, label in enumerate(labels):
                    n = UIDX[label]
                    pe.wait_ge(*done("pool", "lo", n))
                    for m in range(NT):
                        for j in range(kts):
                            k = s * kts + j
                            c = slice(j * cols, (j + 1) * cols)
                            tok = slice(m * P, (m + 1) * P)
                            first, last = k == 0, k == kts * len(labels) - 1
                            o = bs[m][:, 0:cols]
                            nc.tensor.matmul(o, a_hi[:, k, tok], w_hi[:, n % W_SLOTS, c], start=first, stop=False)
                            nc.tensor.matmul(o, a_hi[:, k, tok], w_lo[:, n % W_SLOTS, c], start=False, stop=False)
                            mm = nc.tensor.matmul(o, a_lo[:, k, tok], w_hi[:, n % W_SLOTS, c], start=False, stop=last)
                        marks = ([outs[m]] if last else []) + ([("unit", n)] if m == NT - 1 else [])
                        if marks:
                            mm.then_inc(*step("pe", *marks))

            def transposed(tag, src, tiles):
                for k in range(tiles):
                    o = begin(tag, k)
                    for m in range(NT):
                        mm = nc.tensor.transpose(o[:, m * P:(m + 1) * P], src[:, m, k * P:(k + 1) * P], ident)
                    mm.then_inc(*step("pe", (tag, k)))

            pe.wait_ge(cst_in, 16)
            pe.wait_ge(par_in, 16 * n_par)
            for b, rows in enumerate(PARAM_USED):
                o = begin("par", b)
                nc.tensor.transpose(o[:, 0:rows], stage[0:rows, b, :], ident[0:rows, 0:rows]) \
                    .then_inc(*step("pe", ("par", b)))
            for m in range(NT):
                pe.wait_ge(*done("dve", "xn_a", m))
            transposed("na", xn_a, KD)
            pe.wait_ge(*done("dve", "hT_lo", "na", KD - 1))

            for i in (12, 13, 14, 0, 1, 2, 3, 4, 5, 6, 7):
                feature_unit(("rw", i), "rw", i)
            pe.wait_ge(lora_in, 64)
            pe.wait_ge(*done("act", "lora_act"))
            for i in range(NPAIR):
                c = slice(i * P, (i + 1) * P)
                o = begin("lw", i)
                nc.tensor.matmul(o[:, :], lora_w[0:64, 0, c], lora_x[0:64, 0, :], start=True, stop=True) \
                    .then_inc(*step("pe", ("lw", i)))
                o = begin("la", i)
                nc.tensor.matmul(o[:, :], lora_w[64:128, 0, c], lora_x[64:128, 0, :], start=True, stop=True) \
                    .then_inc(*step("pe", ("la", i)))
                o = begin("lg", i)
                nc.tensor.matmul(o[:, :], lora_w[:, 1, c], lora_x[:, 1, :], start=True, stop=False)
                nc.tensor.matmul(o[:, :], lora_w[0:32, 2, c], lora_x[0:32, 2, :], start=False, stop=True) \
                    .then_inc(*step("pe", ("lg", i)))
            for i in range(8, 12):
                feature_unit(("rw", i), "rw", i)

            def head_sums(tag, src, p):
                o = begin(tag, p)
                nc.tensor.matmul(o[:, :], cst("heads"), src, start=True, stop=True).then_inc(*step("pe", (tag, p)))

            def key_norm(p):
                pe.wait_ge(*done("act", "kk_sq", p))
                head_sums("kn", Sc[:, p % 2, :], p)

            def bonus_sum(p):
                pe.wait_ge(*done("dve", "rk", p))
                head_sums("bn", Sc[:, p % 2, :], p)

            for i in range(12):
                feature_unit(("qk", i), "qk", i)
                if i % 3 == 2:
                    key_norm(i // 3)
                    if i // 3 >= 1:
                        bonus_sum(i // 3 - 1)
            token_units([("v0", s) for s in range(4)], [("vt0", m) for m in range(NT)], hT_hi, hT_lo, 2, 512)
            bonus_sum(NPAIR - 1)
            token_units([("v1", s) for s in range(2)], [("vt1", m) for m in range(NT)], hT_hi, hT_lo, 4, 256)

            def scores(it):
                j, qt = it // NT, it % NT
                for g in range(3):
                    h = ATT_HG * g + j
                    r = slice(HD * (h % 2), HD * (h % 2) + HD)
                    k0 = max(0, qt - 1) if g == 0 else 0
                    n = (qt + 1 - k0) * P
                    o = begin("s", it, g)
                    nc.tensor.matmul(o[:, 0:n], qk[r, h // 2, qt * P:(qt + 1) * P],
                        qk[r, 6 + h // 2, k0 * P:(qt + 1) * P], start=True, stop=True).then_inc(*step("pe", ("s", it, g)))

            pe.wait_ge(*done("act", "vt1", NT - 1))
            scores(0)
            for it in range(16):
                if it + 1 < 16:
                    scores(it + 1)
                j, qt = it // NT, it % NT
                tiles = att_tiles(j, qt)
                pe.wait_ge(*done("dve", "P", it))
                for c in range(0, len(tiles), 4):
                    o = begin("t", it, c)
                    for x in range(c, min(c + 4, len(tiles))):
                        mm = nc.tensor.transpose(o[:, (x - c) * P:(x - c + 1) * P], Sx[:, it % 2, x * P:(x + 1) * P], ident)
                    mm.then_inc(*step("pe", ("t", it, c), ("tall", it)))
                r = slice(HD * (j % 2), HD * (j % 2) + HD)
                o = begin("o", it)
                for x, (h, kt) in enumerate(tiles):
                    if x % 4 == 0:
                        pe.wait_ge(*done("act", "pt", it, x))
                    mm = nc.tensor.matmul(o[r, 0:P], vtok[:, kt, HD * h:HD * (h + 1)], PT[:, x, :],
                                          start=(x == 0), stop=(x == len(tiles) - 1))
                mm.then_inc(*step("pe", ("o", it)))

            def four(label, pairs):
                o = begin(*label)
                for p in range(NPAIR):
                    c = slice(p * P, (p + 1) * P)
                    for x, (a, b) in enumerate(pairs):
                        mm = nc.tensor.matmul(o[:, c], a[:, c], b[:, c], start=(x == 0), stop=(x == len(pairs) - 1))
                mm.then_inc(*step("pe", label))

            def four_t(label, src):
                o = begin(*label)
                for p in range(NPAIR):
                    c = slice(p * P, (p + 1) * P)
                    mm = nc.tensor.transpose(o[:, c], src[:, c], ident)
                mm.then_inc(*step("pe", label))

            for gr in range(NCH // 2):
                pe.wait_ge(*done("dve", "fill", gr))
                pe.wait_ge(*done("act", "fill", gr))

                def side(kind, s):
                    B, K, V = (CM[n][:, s, :] for n in ("Bf", "Kf", "Vf"))
                    A, R = At[:, 2 * (gr % 2) + s, :], Rt[:, 2 * (gr % 2) + s, :]
                    c = 2 * gr + s
                    if kind == "Vt":
                        four_t(("Vt", c), V)
                    if kind == "Bt":
                        four_t(("Bt", c), B)
                    if kind == "Kt":
                        four_t(("Kt", c), K)
                    if kind == "Ak":
                        four(("Ak", c), [(K, A)])
                    if kind == "Rb":
                        four(("Rb", c), [(B, R)])
                    if kind == "Rk":
                        four(("Rk", c), [(K, R)])

                for s in range(2):
                    B, A = CM["Bf"][:, s, :], At[:, 2 * (gr % 2) + s, :]
                    four(("AT", 2 * gr + s), [(B, A)])
                    four(("A", 2 * gr + s), [(A, B)])
                for lv in range(5):
                    for s in range(2):
                        c = 2 * gr + s
                        pe.wait_ge(*done("dve", "X", c, lv))
                        four(("W", c, lv), [(CM["Am"][:, s, :], CM["Xx"][:, s, :])])
                    for kind in (("Vt", "Ak"), ("Bt",), ("Kt",), ("Rb",), ("Rk",))[lv]:
                        for s in range(2):
                            side(kind, s)
                    for s in range(2):
                        c = 2 * gr + s
                        pe.wait_ge(*done("dve", "Wp", c, lv))
                        four(("XW", c, lv), [(CM["XT"][:, s, :], Wp[:, s, :])])
                        if lv < 4:
                            four(("XTW", c, lv), [(Wp[:, s, :], CM["XT"][:, s, :])])
                for s in range(2):
                    c = 2 * gr + s
                    Z = Zs[:, c % 2, :]
                    A, R = At[:, 2 * (gr % 2) + s, :], Rt[:, 2 * (gr % 2) + s, :]
                    U1, U = CM["XT"][:, s, :], CM["Am"][:, s, :]
                    pe.wait_ge(*done("act", "Kt", c))
                    pe.wait_ge(*done("dve", "Rk", c))
                    pe.wait_ge(*done("dve", "X", c, 5))
                    if c == 0:
                        pe.wait_ge(*done("pool", "cleared"))
                    else:
                        pe.wait_ge(*done("dve", "Z", c))
                    four(("u1", c), [(A, Z), (CM["Ak"][:, s, :], CM["Vt"][:, s, :])])
                    pe.wait_ge(*done("act", "U1", c))
                    four(("u2", c), [(CM["Xx"][:, s, :], U1)])
                    pe.wait_ge(*done("act", "U", c))
                    if c + 1 < NCH:
                        four(("z", c), [(CM["Bt"][:, s, :], U), (CM["Kt"][:, s, :], CM["Vt"][:, s, :])])
                    four(("y", c), [(Z, R), (U, CM["Rb"][:, s, :]), (CM["Vt"][:, s, :], CM["Rk"][:, s, :])])

            pe.wait_ge(*done("act", "y", NCH - 1))
            for p in range(NPAIR):
                head_sums("mu", KK[:, p, :], p)
            feature_unit(("gate", 0), "gate", 0)
            for p in range(NPAIR):
                pe.wait_ge(*done("act", "gn_sq", p))
                head_sums("var", gn[:, p, :], p)
            for i in range(1, 16):
                feature_unit(("gate", i), "gate", i)

            def branch(label, tag, outs, kts, a_hi, a_lo):
                n = UIDX[label]
                pe.wait_ge(*done("pool", "lo", n))
                w = UNIT // kts
                for x, i in enumerate(outs):
                    o = begin(tag, i)
                    for k in range(kts):
                        c = slice(k * w + x * P, k * w + (x + 1) * P)
                        mm = split3(o[:, :], w_hi[:, n % W_SLOTS, c], w_lo[:, n % W_SLOTS, c],
                                    a_hi[:, k, :], a_lo[:, k, :], k == 0, k == kts - 1)
                    mm.then_inc(*step("pe", (tag, i), ("unit", n)))

            pe.wait_ge(*done("dve", "ya_lo", NPAIR - 1))
            for i in range(0, KD, 4):
                branch(("bb", i), "pb", range(i, i + 4), 2, yb_hi, yb_lo)
                branch(("ba", i), "pa", range(i, i + 2), 4, ya_hi, ya_lo)
                branch(("ba", i + 2), "pa", range(i + 2, i + 4), 4, ya_hi, ya_lo)

            pe.wait_ge(*done("dve", "mg_lo", KD - 1))
            for h in range(2):
                token_units([("out", h, s) for s in range(4)], [("op", h, m) for m in range(NT)], mg_hi, mg_lo, 2, 512)
            for m in range(NT):
                pe.wait_ge(*done("dve", "xn_b", m))
            transposed("nb", xn_b, KD)
            pe.wait_ge(*done("dve", "hT_lo", "nb", KD - 1))

            for i in range(NF):
                feature_unit(("up", i), "up", i)
                feature_unit(("up", NF + i), "up", NF + i)
            for h in range(2):
                pe.wait_ge(*done("dve", "g_lo", NF - 1))
                token_units([("down", h, s) for s in range(NF // 2)], [("dn", h, m) for m in range(NT)], g_hi, g_lo, 2, 512)
                if h == 0:
                    pe.wait_ge(p_in, 16)
                    transposed("np", p_raw, 2)
            pe.wait_ge(*done("dve", "pT_lo", 1))
            for h in range(2):
                token_units([("ple", h)], [("pp", h, m) for m in range(NT)], pT_hi, pT_lo, 2, 512)
            for m in range(NT):
                pe.wait_ge(*done("dve", "xn_c", m))
            transposed("nc", xn_c, KD)
            pe.wait_ge(*done("dve", "hT_lo", "nc", KD - 1))
            for h in range(2):
                token_units([("pleg", h, s) for s in range(4)], [("pg", h, m) for m in range(NT)], hT_hi, hT_lo, 2, 512)

        @block.scalar
        def _(act):
            act.dma_start(consts[:, :], ins["consts"]).then_inc(cst_in, 16)
            act.dma_start(dist[:, :], ins["dist"]).then_inc(dist_in, 16)
            act.dma_start(lora_w[0:64, 0, :], ins["rw_w_up"][0]).then_inc(lora_in, 16)
            act.dma_start(lora_w[64:128, 0, :], ins["rw_a_up"][0]).then_inc(lora_in, 16)
            act.dma_start(lora_w[:, 1, :], ins["rw_g_up"][0, 0:P, :]).then_inc(lora_in, 16)
            act.dma_start(lora_w[0:32, 2, :], ins["rw_g_up"][0, P:, :]).then_inc(lora_in, 16)
            nxt = [0]

            def hi_upto(n):
                while nxt[0] <= min(n, len(UNITS) - 1):
                    u = nxt[0]
                    act.wait_ge(landed[u % RAW_SLOTS], 16 * (u // RAW_SLOTS + 1))
                    if u >= W_SLOTS:
                        act.wait_ge(*done("pe", "unit", u - W_SLOTS))
                        act.wait_ge(*done("pool", "lo", u - W_SLOTS))
                    nc.scalar.activation(w_hi[:, u % W_SLOTS, :], raw[:, u % RAW_SLOTS, :], ACT.Copy) \
                        .then_inc(*step("act", ("hi", u)))
                    nxt[0] += 1

            def before(label):
                hi_upto(UIDX[label] + 1)


            def norm_stats(tag, src, scratch, m0=0, m1=NT):
                for m in range(m0, m1):
                    if tag == "na":
                        act.wait_ge(x_in, 32)
                    else:
                        act.wait_ge(*done("dve", "x_" + tag, m))
                    if m > m0:
                        act.wait_ge(*previous("act"))
                    nc.scalar.activation(scratch, src[:, m, :], ACT.Square, accum_out=stat[:, ss + m:ss + m + 1]) \
                        .then_inc(*step("act"))
                act.wait_ge(*previous("act"))
                nc.scalar.activation(stat[:, ss + m0:ss + m1], stat[:, ss + m0:ss + m1], ACT.Sqrt,
                    scale=1.0 / DM, bias=stat[:, epsc:epsc + 1]).then_inc(*step("act", ("rms", tag, m0)))

            def gained_hi(tag, gain, tiles, dst):
                for k in range(tiles):
                    act.wait_ge(*done("pe", tag, k))
                    scale = par(gain, k) if gain else 1.0
                    nc.scalar.activation(dst[:, k, :], psum((tag, k))[:, :], ACT.Copy, scale=scale) \
                        .then_inc(*step("act", ("hi", tag, k)))

            act.wait_ge(*done("pool", "eps"))
            norm_stats("na", xs, Rr[:, 0:2, :].rearrange("p a b -> p (a b)"))
            hi_upto(0)
            act.wait_ge(*done("dve", "params"))
            gained_hi("na", "g_mix", KD, hT_hi)

            dsts = {12: lora_x[:, 0, :], 13: lora_x[:, 1, :], 14: lora_x[:, 2, :]}
            for i in range(4):
                dsts[i], dsts[4 + i], dsts[8 + i] = Rr[:, i, :], Kk[:, i, :], Vv[:, i, :]

            def shift_own(i):
                before(("rw", i))
                act.wait_ge(*done("pe", "rw", i))
                rows = 32 if i == 14 else P
                nc.scalar.activation(dsts[i][0:rows, :], psum(("rw", i))[0:rows, :], ACT.Copy,
                    scale=stat[0:rows, omm + i:omm + i + 1]).then_inc(*step("act", ("own", i)))

            act.wait_ge(*done("dve", "derived"))
            for i in (12, 13, 14, 0, 1, 2):
                shift_own(i)
            act.wait_ge(*done("dve", "shift", 14))
            nc.scalar.activation(lora_x[0:64, 0, :], lora_x[0:64, 0, :], ACT.Tanh).then_inc(*step("act"))
            nc.scalar.activation(lora_x[:, 1, :], lora_x[:, 1, :], ACT.Sigmoid).then_inc(*step("act"))
            nc.scalar.activation(lora_x[0:32, 2, :], lora_x[0:32, 2, :], ACT.Sigmoid).then_inc(*step("act", ("lora_act",)))
            for i in (3, 4, 5, 6, 7):
                shift_own(i)
            hi_upto(UIDX[("rw", 8)] + 0)
            for i in range(NPAIR):
                act.wait_ge(*done("pe", "lw", i))
                nc.scalar.activation(Bo[:, i, :], psum(("lw", i))[:, :], ACT.Sigmoid, bias=par("rw_w0", i)) \
                    .then_inc(*frees("act", ("lw", i), ("lw", i)))
                act.wait_ge(*done("pe", "la", i))
                nc.scalar.activation(Aa[:, i, :], psum(("la", i))[:, :], ACT.Sigmoid, bias=par("rw_a0", i)) \
                    .then_inc(*frees("act", ("la", i), ("la", i)))
                act.wait_ge(*done("pe", "lg", i))
                nc.scalar.activation(Gg[:, i, :], psum(("lg", i))[:, :], ACT.Copy) \
                    .then_inc(*frees("act", ("lg", i), ("lg", i)))
            for i in range(8, 12):
                shift_own(i)

            def pre_a(p):
                q = p % 2
                act.wait_ge(*done("dve", "L", p))
                if p >= 2:
                    act.wait_ge(*done("dve", "preC", p - 2))
                nc.scalar.activation(Et[:, q, :], Lt[:, q, :], ACT.Exp, scale=-DECAY).then_inc(*step("act"))
                nc.scalar.activation(Ei[:, q, :], Lt[:, q, :], ACT.Exp, scale=DECAY).then_inc(*step("act", ("E", p)))
                act.wait_ge(*done("dve", "kkr", p))
                nc.scalar.activation(Sc[:, q, :], KK[:, p, :], ACT.Square).then_inc(*step("act", ("kk_sq", p)))

            for i in range(12):
                if i % 3 == 0:
                    pre_a(i // 3)
                before(("qk", i))
                act.wait_ge(*done("pe", "qk", i))
                nc.scalar.activation(qk[:, i, :], psum(("qk", i))[:, :], ACT.Copy,
                    scale=HD ** -0.5 if i < 6 else 1.0).then_inc(*frees("act", ("qk", i), ("qk", i)))
                if i % 3 == 2:
                    p = i // 3
                    act.wait_ge(*done("pe", "kn", p))
                    nc.scalar.activation(Sc[:, p % 2, :], psum(("kn", p))[:, :], ACT.Sqrt) \
                        .then_inc(*frees("act", ("kn", p), ("kn", p)))
            for c, w, n in ((0, 512, 4), (512, 256, 2)):
                tag = "vt0" if c == 0 else "vt1"
                for s in range(n):
                    before(("v0" if c == 0 else "v1", s))
                for m in range(NT):
                    act.wait_ge(*done("pe", tag, m))
                    nc.scalar.activation(vtok[:, m, c:c + w], psum((tag, m))[:, 0:w], ACT.Copy) \
                        .then_inc(*frees("act", (tag, m), (tag, m)))

            def expo(it):
                act.wait_ge(*done("dve", "max", it))
                n = len(att_tiles(it // NT, it % NT)) * P
                nc.scalar.activation(Sx[:, it % 2, 0:n], Sx[:, it % 2, 0:n], ACT.Exp,
                    bias=stat[:, negmax + it:negmax + it + 1],
                    accum_out=stat[:, den + it:den + it + 1]).then_inc(*step("act", ("exp", it)))

            expo(0)
            for it in range(16):
                if it + 1 < 16:
                    expo(it + 1)
                j, qt = it // NT, it % NT
                n = len(att_tiles(j, qt))
                for c in range(0, n, 4):
                    w = min(4, n - c)
                    act.wait_ge(*done("pe", "t", it, c))
                    if it:
                        act.wait_ge(*done("pe", "o", it - 1))
                    nc.scalar.activation(PT[:, c:c + w, :].rearrange("p a b -> p (a b)"),
                        psum(("t", it, c))[:, 0:w * P], ACT.Copy).then_inc(*frees("act", ("t", it, c), ("pt", it, c)))
                r = slice(HD * (j % 2), HD * (j % 2) + HD)
                act.wait_ge(*done("pe", "o", it))
                nc.scalar.activation(yb_hi[r, j // 2, qt * P:(qt + 1) * P], psum(("o", it))[r, 0:P], ACT.Copy) \
                    .then_inc(*step("act", ("yb_hi", it)))

            def fill(gr):
                if gr == 0:
                    act.wait_ge(*done("pool", "cleared"))
                    act.wait_ge(*done("dve", "preC", NPAIR - 1))
                else:
                    for s in range(2):
                        for k in ("Kt", "Vt", "Rk"):
                            act.wait_ge(*done("pe", k, 2 * (gr - 1) + s))
                    if gr >= 2:
                        act.wait_ge(*done("pe", "y", 2 * gr - 3))
                fill_blocks("act", nc.scalar.copy, gr, ((CM["Kf"], 0, Kk), (CM["Vf"], 0, Vv), (Rt, 2 * (gr % 2), Rr)))

            fill(0)
            for gr in range(NCH // 2):
                for kind in ("Vt", "Bt", "Kt"):
                    for s in range(2):
                        c = 2 * gr + s
                        act.wait_ge(*done("pe", kind, c))
                        if c >= 2:
                            act.wait_ge(*done("pe", "y", c - 2))
                        nc.scalar.activation(CM[kind][:, s, :], psum((kind, c))[:, :], ACT.Copy) \
                            .then_inc(*frees("act", (kind, c), (kind, c)))
                if gr + 1 < NCH // 2:
                    fill(gr + 1)
                for s in range(2):
                    c = 2 * gr + s
                    act.wait_ge(*done("pe", "u1", c))
                    nc.scalar.activation(CM["XT"][:, s, :], psum(("u1", c))[:, :], ACT.Copy) \
                        .then_inc(*frees("act", ("u1", c), ("U1", c)))
                    act.wait_ge(*done("pe", "u2", c))
                    nc.scalar.activation(CM["Am"][:, s, :], psum(("u2", c))[:, :], ACT.Copy) \
                        .then_inc(*frees("act", ("u2", c), ("U", c)))
                    act.wait_ge(*done("pe", "y", c))
                    if s == 0 and gr == 0:
                        act.wait_ge(*done("dve", "fill", 0))
                    for q in range(2):
                        r = slice(CH * q, CH * q + CH)
                        y = psum(("y", c))[r, :].rearrange("p (h two t) -> p h two t", two=2, t=CH)[:, :, q, :]
                        ins_ = nc.scalar.activation(KK[r, :, c * CH:(c + 1) * CH], y, ACT.Copy)
                        if q == 0:
                            ins_.then_inc(*step("act"))
                    ins_.then_inc(*frees("act", ("y", c), ("y", c)))

            def gate(i):
                before(("gate", i))
                act.wait_ge(*done("pe", "gate", i))
                nc.scalar.activation(sig[:, i, :], psum(("gate", i))[:, :], ACT.Sigmoid, bias=par("b_gate", i)) \
                    .then_inc(*frees("act", ("gate", i), ("gate", i)))

            hi_upto(UIDX[("gate", 0)] + 1)
            for p in range(NPAIR):
                act.wait_ge(*done("dve", "gn_d", p))
                nc.scalar.activation(gn[:, p, :], KK[:, p, :], ACT.Square).then_inc(*step("act", ("gn_sq", p)))
            gate(0)
            for p in range(NPAIR):
                act.wait_ge(*done("pe", "var", p))
                nc.scalar.activation(gn[:, p, :], psum(("var", p))[:, :], ACT.Sqrt, scale=1.0 / HD,
                    bias=stat[:, epsc + 1:epsc + 2]).then_inc(*frees("act", ("var", p), ("gn_sd", p)))
            for i in range(1, 16):
                gate(i)
                if i >= 6 and i % 2 == 0 and (i - 6) // 2 < NPAIR:
                    p = (i - 6) // 2
                    act.wait_ge(*done("dve", "y_a", p))
                    nc.scalar.activation(ya_hi[:, p, :], KK[:, p, :], ACT.Copy).then_inc(*step("act", ("ya_hi", p)))
            before(("bb", 0))
            for i in range(KD):
                before(("bb" if i % 4 == 0 else "ba", i - i % 4 if i % 4 < 2 else i - i % 4 + 2))
                if i % 4 == 0:
                    before(("ba", i))
                act.wait_ge(*done("dve", "merged", i))
                nc.scalar.activation(mg_hi[:, i, :], sig[:, i, :], ACT.Copy).then_inc(*step("act", ("mg_hi", i)))
            for h in range(2):
                for s in range(4):
                    before(("out", h, s))
            norm_stats("nb", xr, cbuf[:, 0, 0:2, :].rearrange("p a b -> p (a b)"))
            gained_hi("nb", "g_ffn", KD, hT_hi)

            def g_split(i):
                act.wait_ge(*done("dve", "g", i))
                nc.scalar.activation(g_hi[:, i, :], cbuf[:, i % 2, 3, :], ACT.Copy).then_inc(*step("act", ("g_hi", i)))

            for i in range(NF):
                if i:
                    g_split(i - 1)
                for z, u in ((0, i), (1, NF + i)):
                    before(("up", u))
                    act.wait_ge(*done("pe", "up", u))
                    if i >= 2:
                        act.wait_ge(*done("dve", "g_lo", i - 2))
                    nc.scalar.activation(cbuf[:, i % 2, z, :], psum(("up", u))[:, :], ACT.Identity,
                        scale=par("conv_w0", u), bias=par("conv_b", u)).then_inc(*step("act", ("tap0", u)))
                act.wait_ge(*done("dve", "taps", i))
                nc.scalar.activation(cbuf[:, i % 2, 2, :], cbuf[:, i % 2, 0, :], ACT.Gelu_apprx_tanh) \
                    .then_inc(*step("act", ("gelu", i)))
            g_split(NF - 1)
            for h in range(2):
                for s in range(NF // 2):
                    before(("down", h, s))
                if h == 0:
                    gained_hi("np", None, 2, pT_hi)
            for h in range(2):
                before(("ple", h))
                for m in range(NT):
                    act.wait_ge(*done("pe", "pp", h, m))
                    nc.scalar.activation(pple[:, m, 512 * h:512 * h + 512], psum(("pp", h, m))[:, :], ACT.Copy) \
                        .then_inc(*frees("act", ("pp", h, m), ("pp", h, m)))
            norm_stats("nc", xr, junk[:, :])
            gained_hi("nc", "g_ple", KD, hT_hi)
            for h in range(2):
                for s in range(4):
                    before(("pleg", h, s))
                for m in range(NT):
                    act.wait_ge(*done("pe", "pg", h, m))
                    if h:
                        act.wait_ge(*done("dve", "x_ple", 0, m))
                    nc.scalar.activation(psig[:, m, :], psum(("pg", h, m))[:, :], ACT.Sigmoid) \
                        .then_inc(*frees("act", ("pg", h, m), ("pg", h, m)))
            for m in range(NT):
                norm_stats("end", xr, junk[:, :], m, m + 1)

        @block.vector
        def _(dve):
            V = nc.vector


            def gained_lo(tag, gain, tiles, dst_hi, dst, name):
                for k in range(tiles):
                    dve.wait_ge(*done("act", "hi", tag, k))
                    scale = par(gain, k) if gain else 1.0
                    V.scalar_tensor_tensor(dst[:, k, :], psum((tag, k))[:, :], scale,
                        dst_hi[:, k, :].bitcast(F32), ALU.mult, ALU.subtract) \
                        .then_inc(*frees("dve", (tag, k), (name, tag, k) if name == "hT_lo" else (name, k)))

            for b, rows in enumerate(PARAM_USED):
                dve.wait_ge(*done("pe", "par", b))
                V.tensor_copy(params[:, b * P:b * P + rows], psum(("par", b))[:, 0:rows]) \
                    .then_inc(*frees("dve", ("par", b), ("params",)))
            dve.wait_ge(*previous("dve"))
            c = PARAM_COL["rw_mu"]
            V.tensor_scalar(stat[:, omm:omm + 15], params[:, c:c + 15], -1.0, 1.0, ALU.mult, ALU.add).then_inc(*step("dve"))
            c = PARAM_COL["rw_k_a"]
            V.tensor_scalar(stat[:, omka:omka + 4], params[:, c:c + 4], -1.0, 1.0, ALU.mult, ALU.add) \
                .then_inc(*step("dve", ("derived",)))
            dve.wait_ge(*done("act", "rms", "na", 0))
            V.reciprocal(stat[:, rstd:rstd + NT], stat[:, ss:ss + NT]).then_inc(*step("dve"))
            dve.wait_ge(*previous("dve"))
            for m in range(NT):
                V.tensor_scalar(xn_a[:, m, :], xs[:, m, :], stat[:, rstd + m:rstd + m + 1], None, ALU.mult) \
                    .then_inc(*step("dve", ("xn_a", m)))
            gained_lo("na", "g_mix", KD, hT_hi, hT_lo, "hT_lo")

            dsts = {12: lora_x[:, 0, :], 13: lora_x[:, 1, :], 14: lora_x[:, 2, :]}
            for i in range(4):
                dsts[i], dsts[4 + i], dsts[8 + i] = Rr[:, i, :], Kk[:, i, :], Vv[:, i, :]

            def shift(i):
                dve.wait_ge(*done("act", "own", i))
                rows = 32 if i == 14 else P
                d = dsts[i][0:rows, 1:SEQ]
                V.scalar_tensor_tensor(d, psum(("rw", i))[0:rows, 0:SEQ - 1], par("rw_mu", i, 0, rows), d,
                    ALU.mult, ALU.add).then_inc(*frees("dve", ("rw", i), ("shift", i)))

            for i in (12, 13, 14, 0, 1, 2, 3, 4, 5, 6, 7, 8, 9, 10, 11):
                shift(i)

            def pre_a(p):
                q = p % 2
                dve.wait_ge(*done("act", "lg", NPAIR - 1))
                if p == 0:
                    dve.wait_ge(*done("pe", "lg", NPAIR - 1))
                if p >= 2:
                    dve.wait_ge(*done("act", "E", p - 2))
                V.tensor_tensor_scan(Lt[:, q, :], reset, Bo[:, p, :], 0.0, ALU.mult, ALU.add) \
                    .then_inc(*step("dve", ("L", p)))
                V.tensor_scalar(KK[:, p, :], Kk[:, p, :], par("rw_k_k", p), None, ALU.mult) \
                    .then_inc(*step("dve", ("kkr", p)))

            def pre_b(p):
                sc, kk, k, a, r = Sc[:, p % 2, :], KK[:, p, :], Kk[:, p, :], Aa[:, p, :], Rr[:, p, :]
                dve.wait_ge(*done("act", "kn", p))
                V.tensor_scalar(sc, sc, 1e-12, None, ALU.max).then_inc(*step("dve"))
                dve.wait_ge(*previous("dve"))
                V.reciprocal(sc, sc).then_inc(*step("dve"))
                dve.wait_ge(*previous("dve"))
                V.tensor_tensor(kk, kk, sc, ALU.mult).then_inc(*step("dve"))
                dve.wait_ge(*previous("dve"))
                V.tensor_scalar(sc, a, par("rw_k_a", p), stat[:, omka + p:omka + p + 1], ALU.mult, ALU.add) \
                    .then_inc(*step("dve"))
                dve.wait_ge(*previous("dve"))
                V.tensor_tensor(k, k, sc, ALU.mult).then_inc(*step("dve"))
                V.tensor_tensor(a, kk, a, ALU.mult).then_inc(*step("dve"))
                dve.wait_ge(*previous("dve"))
                V.scalar_tensor_tensor(sc, r, par("rw_r_k", p), k, ALU.mult, ALU.mult).then_inc(*step("dve", ("rk", p)))

            def pre_c(p):
                q = p % 2
                kk, k, a, r = KK[:, p, :], Kk[:, p, :], Aa[:, p, :], Rr[:, p, :]
                dve.wait_ge(*done("pe", "bn", p))
                V.tensor_tensor(Bo[:, p, :], psum(("bn", p))[:, :], Vv[:, p, :], ALU.mult).then_inc(*frees("dve", ("bn", p)))
                dve.wait_ge(*done("act", "E", p))
                V.tensor_tensor(a, a, Ei[:, q, :], ALU.mult).then_inc(*step("dve"))
                V.tensor_tensor(k, k, Ei[:, q, :], ALU.mult).then_inc(*step("dve"))
                V.tensor_tensor(r, r, Et[:, q, :], ALU.mult).then_inc(*step("dve"))
                e3 = Et[:, q, :].rearrange("p (c t) -> p c t", t=CH)
                k3 = kk.rearrange("p (c t) -> p c t", t=CH)
                V.tensor_copy(stat[:, ec + 8 * p:ec + 8 * p + 8].unsqueeze(2), e3[:, :, CH - 1:CH]).then_inc(*step("dve"))
                V.scalar_tensor_tensor(k3[:, :, 1:CH], k3[:, :, 1:CH], -1.0, e3[:, :, 0:CH - 1], ALU.mult, ALU.mult) \
                    .then_inc(*step("dve"))
                V.tensor_scalar(k3[:, :, 0:1], k3[:, :, 0:1], -1.0, None, ALU.mult).then_inc(*step("dve", ("preC", p)))

            pre_a(0)
            for p in range(NPAIR):
                if p + 1 < NPAIR:
                    pre_a(p + 1)
                pre_b(p)
                if p:
                    pre_c(p - 1)
            pre_c(NPAIR - 1)

            def masked(it):
                j, qt = it // NT, it % NT
                off, base_ = 0, 0
                if it >= 2:
                    dve.wait_ge(*done("pe", "tall", it - 2))
                for g, width in enumerate((2 * P, SEQ, SEQ)):
                    k0 = max(0, qt - 1) if g == 0 else 0
                    n = (qt + 1 - k0) * P
                    dve.wait_ge(*done("pe", "s", it, g))
                    V.scalar_tensor_tensor(Sx[:, it % 2, off:off + n], dist[:, base_ + width - n:base_ + width],
                        -SLOPES[ATT_HG * g + j], psum(("s", it, g))[:, 0:n],
                        ALU.mult, ALU.add).then_inc(*frees("dve", ("s", it, g)))
                    off += n
                    base_ += width
                dve.wait_ge(*previous("dve"))
                nm = stat[:, negmax + it:negmax + it + 1]
                V.reduce_max(nm, Sx[:, it % 2, 0:off], AX_X).then_inc(*step("dve"))
                dve.wait_ge(*previous("dve"))
                V.tensor_scalar(nm, nm, -1.0, None, ALU.mult).then_inc(*step("dve", ("max", it)))

            def normalise(it):
                n = len(att_tiles(it // NT, it % NT)) * P
                dve.wait_ge(*done("act", "exp", it))
                rd = stat[:, rden + it:rden + it + 1]
                V.reciprocal(rd, stat[:, den + it:den + it + 1]).then_inc(*step("dve"))
                dve.wait_ge(*previous("dve"))
                V.tensor_scalar(Sx[:, it % 2, 0:n], Sx[:, it % 2, 0:n], rd, None, ALU.mult).then_inc(*step("dve", ("P", it)))

            def yb_rest(it):
                j, qt = it // NT, it % NT
                r, t = slice(HD * (j % 2), HD * (j % 2) + HD), slice(qt * P, (qt + 1) * P)
                dve.wait_ge(*done("act", "yb_hi", it))
                V.tensor_tensor(yb_lo[r, j // 2, t], psum(("o", it))[r, 0:P], yb_hi[r, j // 2, t].bitcast(F32),
                    ALU.subtract).then_inc(*frees("dve", ("o", it), ("yb_lo", it)))

            dve.wait_ge(dist_in, 16)
            masked(0)
            for it in range(16):
                if it + 1 < 16:
                    masked(it + 1)
                normalise(it)
                if it:
                    yb_rest(it - 1)
            yb_rest(15)

            def fill(gr):
                if gr == 0:
                    dve.wait_ge(*done("pool", "cleared"))
                else:
                    for s in range(2):
                        dve.wait_ge(*done("pe", "Bt", 2 * (gr - 1) + s))
                        dve.wait_ge(*done("pe", "Rb", 2 * (gr - 1) + s))
                    if gr >= 2:
                        dve.wait_ge(*done("pe", "y", 2 * gr - 3))
                fill_blocks("dve", nc.vector.tensor_copy, gr, ((CM["Bf"], 0, Aa), (At, 2 * (gr % 2), KK)))

            def times_mask(dst, label, mask, *marks):
                dve.wait_ge(*done("pe", *label))
                V.tensor_tensor(dst.rearrange("p (h t) -> p h t", t=P),
                    psum(label)[:, :].rearrange("p (h t) -> p h t", t=P), cst4(mask), ALU.mult) \
                    .then_inc(*frees("dve", label, *marks))

            fill(0)
            for gr in range(NCH // 2):
                for s in range(2):
                    c = 2 * gr + s
                    X, XT, A = CM["Xx"][:, s, :], CM["XT"][:, s, :], CM["Am"][:, s, :]
                    if gr:
                        dve.wait_ge(*done("pe", "y", c - 2))
                    times_mask(X, ("AT", c), "off1_st")
                    times_mask(A, ("A", c), "strict_ts")
                    dve.wait_ge(*previous("dve"))
                    x3, t3, a3 = (z.rearrange("p (h t) -> p h t", t=P) for z in (X, XT, A))
                    V.tensor_tensor(x3, x3, cst4("ident"), ALU.add).then_inc(*step("dve"))
                    V.tensor_tensor(t3, a3, cst4("off1_ts"), ALU.mult).then_inc(*step("dve"))
                    dve.wait_ge(*previous("dve"))
                    V.tensor_tensor(t3, t3, cst4("ident"), ALU.add).then_inc(*step("dve", ("X", c, 0)))
                for lv in range(5):
                    for s in range(2):
                        c = 2 * gr + s
                        times_mask(Wp[:, s, :], ("W", c, lv), f"off{2 << lv}", ("Wp", c, lv))
                    for kind, mask in {0: (("Ak", "strict_st"),), 3: (("Rb", "incl_st"),), 4: (("Rk", "incl_st"),)}.get(lv, ()):
                        for s in range(2):
                            c = 2 * gr + s
                            times_mask(CM[kind][:, s, :], (kind, c), mask, (kind, c))
                    for s in range(2):
                        c = 2 * gr + s
                        X, XT = CM["Xx"][:, s, :], CM["XT"][:, s, :]
                        dve.wait_ge(*done("pe", "XW", c, lv))
                        V.tensor_tensor(X, psum(("XW", c, lv))[:, :], X, ALU.add) \
                            .then_inc(*frees("dve", ("XW", c, lv), *([("X", c, 5)] if lv == 4 else [])))
                        if lv < 4:
                            dve.wait_ge(*done("pe", "XTW", c, lv))
                            V.tensor_tensor(XT, psum(("XTW", c, lv))[:, :], XT, ALU.add) \
                                .then_inc(*frees("dve", ("XTW", c, lv), ("X", c, lv + 1)))
                if gr + 1 < NCH // 2:
                    fill(gr + 1)
                for s in range(2):
                    c = 2 * gr + s
                    if c + 1 == NCH:
                        break
                    dve.wait_ge(*done("pe", "z", c))
                    if c:
                        dve.wait_ge(*done("pe", "y", c - 1))
                    Zn = Zs[:, (c + 1) % 2, :]
                    V.tensor_tensor(Zn, psum(("z", c))[:, :], Zs[:, c % 2, :], ALU.add).then_inc(*frees("dve", ("z", c)))
                    dve.wait_ge(*previous("dve"))
                    z3 = Zn.rearrange("p (h t) -> p h t", t=P)
                    e = stat[:, ec:ec + 32].rearrange("p (h c) -> p h c", c=NCH)[:, :, c:c + 1].broadcast_to([P, NPAIR, P])
                    V.tensor_tensor(z3, z3, e, ALU.mult).then_inc(*step("dve", ("Z", c + 1)))

            for p in range(NPAIR):
                dve.wait_ge(*done("pe", "mu", p))
                V.scalar_tensor_tensor(KK[:, p, :], psum(("mu", p))[:, :], -1.0 / HD, KK[:, p, :], ALU.mult, ALU.add) \
                    .then_inc(*frees("dve", ("mu", p), ("gn_d", p)))
            for p in range(NPAIR):
                y, sd = KK[:, p, :], gn[:, p, :]
                dve.wait_ge(*done("act", "gn_sd", p))
                V.reciprocal(sd, sd).then_inc(*step("dve"))
                dve.wait_ge(*previous("dve"))
                V.tensor_tensor(y, y, sd, ALU.mult).then_inc(*step("dve"))
                dve.wait_ge(*previous("dve"))
                V.tensor_scalar(y, y, par("rw_ln_g", p), par("rw_ln_b", p), ALU.mult, ALU.add).then_inc(*step("dve"))
                dve.wait_ge(*previous("dve"))
                V.tensor_tensor(y, y, Bo[:, p, :], ALU.add).then_inc(*step("dve"))
                dve.wait_ge(*previous("dve"))
                V.tensor_tensor(y, y, Gg[:, p, :], ALU.mult).then_inc(*step("dve", ("y_a", p)))
            for p in range(NPAIR):
                dve.wait_ge(*done("act", "ya_hi", p))
                V.tensor_tensor(ya_lo[:, p, :], KK[:, p, :], ya_hi[:, p, :].bitcast(F32), ALU.subtract) \
                    .then_inc(*step("dve", ("ya_lo", p)))

            def merged_rest(i):
                dve.wait_ge(*done("act", "mg_hi", i))
                V.tensor_tensor(mg_lo[:, i, :], sig[:, i, :], mg_hi[:, i, :].bitcast(F32), ALU.subtract) \
                    .then_inc(*step("dve", ("mg_lo", i)))

            for i in range(KD):
                if i % 4 == 0:
                    for z in range(i, i + 4):
                        dve.wait_ge(*done("pe", "pb", z))
                        dve.wait_ge(*done("act", "gate", 8 + z))
                        V.tensor_tensor(sig[:, 8 + z, :], psum(("pb", z))[:, :], sig[:, 8 + z, :], ALU.mult) \
                            .then_inc(*frees("dve", ("pb", z)))
                dve.wait_ge(*done("pe", "pa", i))
                V.tensor_tensor(sig[:, i, :], psum(("pa", i))[:, :], sig[:, i, :], ALU.mult) \
                    .then_inc(*frees("dve", ("pa", i)))
                dve.wait_ge(*previous("dve"))
                V.tensor_tensor(sig[:, i, :], sig[:, i, :], sig[:, 8 + i, :], ALU.add).then_inc(*step("dve", ("merged", i)))
                if i:
                    merged_rest(i - 1)
            merged_rest(KD - 1)

            def residual(tag, h, m, *marks):
                dve.wait_ge(*done("pe", tag, h, m))
                x = xr[:, m, 512 * h:512 * h + 512]
                V.tensor_tensor(x, psum((tag, h, m))[:, :], x, ALU.add).then_inc(*frees("dve", (tag, h, m), *marks))

            def rms_scaled(tag, dst, name):
                dve.wait_ge(*done("act", "rms", tag, 0))
                V.reciprocal(stat[:, rstd:rstd + NT], stat[:, ss:ss + NT]).then_inc(*step("dve"))
                dve.wait_ge(*previous("dve"))
                for m in range(NT):
                    V.tensor_scalar(dst[:, m, :], xr[:, m, :], stat[:, rstd + m:rstd + m + 1], None, ALU.mult) \
                        .then_inc(*step("dve", (name, m)))

            dve.wait_ge(xr_in, 16)
            for h in range(2):
                for m in range(NT):
                    residual("op", h, m, *([("x_nb", m)] if h else []))
            rms_scaled("nb", xn_b, "xn_b")
            gained_lo("nb", "g_ffn", KD, hT_hi, hT_lo, "hT_lo")

            def g_rest(i):
                dve.wait_ge(*done("act", "g_hi", i))
                V.tensor_tensor(g_lo[:, i, :], cbuf[:, i % 2, 3, :], g_hi[:, i, :].bitcast(F32), ALU.subtract) \
                    .then_inc(*step("dve", ("g_lo", i)))

            for i in range(NF):
                if i:
                    g_rest(i - 1)
                for z, u in ((0, i), (1, NF + i)):
                    dve.wait_ge(*done("act", "tap0", u))
                    cv, ps = cbuf[:, i % 2, z, :], psum(("up", u))
                    V.scalar_tensor_tensor(cv[:, 1:], ps[:, 0:SEQ - 1], par("conv_w1", u), cv[:, 1:], ALU.mult, ALU.add) \
                        .then_inc(*step("dve"))
                    dve.wait_ge(*previous("dve"))
                    V.scalar_tensor_tensor(cv[:, 2:], ps[:, 0:SEQ - 2], par("conv_w2", u), cv[:, 2:], ALU.mult, ALU.add) \
                        .then_inc(*frees("dve", ("up", u), *([("taps", i)] if z == 0 else [])))
                dve.wait_ge(*done("act", "gelu", i))
                dve.wait_ge(*previous("dve"))
                V.tensor_tensor(cbuf[:, i % 2, 3, :], cbuf[:, i % 2, 2, :], cbuf[:, i % 2, 1, :], ALU.mult) \
                    .then_inc(*step("dve", ("g", i)))
            g_rest(NF - 1)
            for h in range(2):
                for m in range(NT):
                    residual("dn", h, m, *([("x_nc", m)] if h else []))
                if h == 0:
                    gained_lo("np", None, 2, pT_hi, pT_lo, "pT_lo")
            rms_scaled("nc", xn_c, "xn_c")
            gained_lo("nc", "g_ple", KD, hT_hi, hT_lo, "hT_lo")
            for h in range(2):
                for m in range(NT):
                    dve.wait_ge(*done("act", "pg", h, m))
                    c = slice(512 * h, 512 * h + 512)
                    V.tensor_tensor(psig[:, m, :], psig[:, m, :], pple[:, m, c], ALU.mult).then_inc(*step("dve"))
                    dve.wait_ge(*previous("dve"))
                    V.tensor_tensor(xr[:, m, c], xr[:, m, c], psig[:, m, :], ALU.add) \
                        .then_inc(*step("dve", ("x_ple", h, m), *([("x_end", m)] if h else [])))
            dve.wait_ge(gf_in, 16)
            for m in range(NT):
                dve.wait_ge(*done("act", "rms", "end", m))
                V.reciprocal(stat[:, rstd + m:rstd + m + 1], stat[:, ss + m:ss + m + 1]).then_inc(*step("dve"))
                dve.wait_ge(*previous("dve"))
                V.scalar_tensor_tensor(xr[:, m, :], xr[:, m, :], stat[:, rstd + m:rstd + m + 1], gfin[:, :],
                    ALU.mult, ALU.mult).then_inc(*step("dve", ("final", m)))

    return {"steps": steps, "readers": readers, "turn": turn}


def att_tiles(j, qt):
    return [(ATT_HG * g + j, kt) for g in range(3) for kt in range(max(0, qt - 1) if g == 0 else 0, qt + 1)]


_INS = ["x", "p", "g_mix", "w_in", "rw_mu", "rw_w0", "rw_w_up", "rw_a0", "rw_a_up", "rw_g_up", "rw_k_k", "rw_k_a",
        "rw_r_k", "rw_ln_g", "rw_ln_b", "w_branch_a", "w_branch_b", "w_gate", "b_gate", "w_out", "g_ffn", "w_up",
        "conv_w", "conv_b", "w_down", "g_ple", "w_ple_gate", "w_ple", "g_final"]


def kernel(**inputs):
    import numpy as _np
    import concourse.bacc as _bacc
    from concourse import mybir as _mybir
    from concourse.bass_utils import run_bass_kernel_spmd as _run

    arrays = {name: _np.ascontiguousarray(inputs[name]) for name in _INS}
    arrays["consts"], arrays["dist"] = shape_constants()

    known = None
    for _ in range(2):
        nc = _bacc.Bacc("TRN2", target_bir_lowering=False, num_devices=1)
        ins = {name: nc.dram_tensor(f"in_{name}_dram", a.shape, _mybir.dt.from_np(a.dtype), kind="ExternalInput").ap()
               for name, a in arrays.items()}
        out = nc.dram_tensor("out_0_dram", (1, SEQ, DM), _mybir.dt.float32, kind="ExternalOutput").ap()
        known = build(nc, ins, out, known)
    r = _run(nc, [{f"in_{name}_dram": a for name, a in arrays.items()}], core_ids=[0])
    return r.results[0]["out_0_dram"]
```

```python
from contextlib import ExitStack

import numpy as np

import concourse.bass as bass
from concourse import mybir

P = 128
F32 = mybir.dt.float32
F32R = mybir.dt.float32r
ALU = mybir.AluOpType
ACT = mybir.ActivationFunctionType
AX_X = mybir.AxisListType.X

SEQ, DM, PLE = 512, 1024, 256
NH, HD = 8, 64
RW = NH * HD
ATT_H, ATT_HG = 12, 4
ATT_W = ATT_H * HD
DFF = 3 * DM
NT = SEQ // P
KD = DM // P
NPAIR = RW // P
CH = 64
NCH = SEQ // CH
NF = DFF // P
NORM_EPS, LN_EPS = 1e-6, 64e-5
DECAY = float(np.exp(-0.5))
UNIT = 1024
RAW_SLOTS, W_SLOTS, BANKS = 3, 2, 8
GROUPS = ((128, 1), (512, 4), (2048, 16))
SLOPES = [2.0 ** (-8.0 * (h + 1) / ATT_H) for h in range(ATT_H)]
FAR = 1e30

PARAM_ROWS = [("rw_mu", 15), ("rw_w0", 4), ("rw_a0", 4), ("rw_k_k", 4), ("rw_k_a", 4), ("rw_r_k", 4),
              ("rw_ln_g", 4), ("rw_ln_b", 4), ("g_mix", 8), ("g_ffn", 8), ("g_ple", 8), ("b_gate", 16)]
PARAM_COL, _n = {}, 0
for _name, _rows in PARAM_ROWS:
    PARAM_COL[_name] = _n
    _n += _rows
PARAM_USED = [_n, 96, 96]
PARAM_COL["conv_w0"], PARAM_COL["conv_w1"] = P, P + 48
PARAM_COL["conv_w2"], PARAM_COL["conv_b"] = 2 * P, 2 * P + 48

CONST_NAMES = ["ident", "heads", "strict_st", "incl_st", "strict_ts", "off1_st", "off1_ts",
               "off2", "off4", "off8", "off16", "off32"]


def shape_constants():
    i = np.arange(P)
    same = (i[:, None] // CH) == (i[None, :] // CH)
    r, c = i[:, None] % CH, i[None, :] % CH

    def off(b):
        return same & (r // (2 * b) == c // (2 * b)) & (r % (2 * b) < b) & (c % (2 * b) >= b)

    parts = {"ident": r * 0 + (i[:, None] == i[None, :]), "heads": same, "strict_st": same & (r < c),
             "incl_st": same & (r <= c), "strict_ts": same & (r > c), "off1_st": off(1),
             "off1_ts": off(1).T}
    for b in (2, 4, 8, 16, 32):
        parts[f"off{b}"] = off(b)
    reset = np.broadcast_to((np.arange(SEQ) % CH != 0)[None, :], (P, SEQ))
    consts = np.concatenate([np.asarray(parts[n], np.float32) for n in CONST_NAMES] + [reset.astype(np.float32)], 1)
    dist = []
    for (window, dilation), width in zip(GROUPS, (2 * P, SEQ, SEQ)):
        d = i[:, None] + (width - P) - np.arange(width)[None, :]
        ok = (d >= 0) & (d <= window) & (d % dilation == 0)
        dist.append(np.where(ok, d, FAR).astype(np.float32))
    return np.ascontiguousarray(consts), np.ascontiguousarray(np.concatenate(dist, 1))


SIGNALS = [
    "act_Bt", "act_E", "act_Kt", "act_U", "act_U1", "act_Vt", "act_XT", "act_chain", "act_exp", "act_fill",
    "act_g_hi", "act_gate", "act_gelu", "act_gn_sd", "act_gn_sq", "act_hi", "act_kk_sq", "act_kn", "act_la", "act_lg",
    "act_lora_act", "act_lw", "act_mg_hi", "act_own", "act_pg", "act_pp", "act_pt", "act_qk", "act_rms", "act_sq",
    "act_tap0", "act_vt0", "act_vt1", "act_y", "act_ya_hi", "act_yb_hi", "dve_Ak", "dve_L", "dve_P", "dve_Rb",
    "dve_Rk", "dve_Wp", "dve_X", "dve_Z", "dve_chain", "dve_derived", "dve_fill", "dve_final", "dve_g", "dve_g_lo",
    "dve_gn_d", "dve_hT_lo", "dve_kkr", "dve_max", "dve_merged", "dve_mg_lo", "dve_ms", "dve_pT_lo", "dve_params",
    "dve_preC", "dve_psum_read", "dve_rk", "dve_shift", "dve_stage", "dve_taps", "dve_x_end", "dve_x_nb", "dve_x_nc",
    "dve_xn_a", "dve_xn_b", "dve_xn_c", "dve_y_a", "dve_ya_lo", "dve_yb_lo", "pe_A", "pe_AT", "pe_Ak", "pe_Bt",
    "pe_Kt", "pe_Rb", "pe_Rk", "pe_Vt", "pe_W", "pe_XT", "pe_XW", "pe_bn", "pe_chain", "pe_dn", "pe_kn", "pe_la",
    "pe_lg", "pe_lw", "pe_mu", "pe_na", "pe_nb", "pe_nc", "pe_np", "pe_o", "pe_op", "pe_pa", "pe_par", "pe_pb",
    "pe_pg", "pe_pp", "pe_s", "pe_t", "pe_u1", "pe_u2", "pe_unit", "pe_var", "pe_vt0", "pe_vt1", "pe_y", "pe_z",
    "pool_chain", "pool_cleared", "pool_eps", "pool_lo",
]


GATE_ORDER = [i for c in range(NCH) for i in ((c, NCH + c // 2) if c % 2 == 0 else (c,))] + [12, 13, 14, 15]


def weight_units():
    u = []
    for i in (12, 13, 14, 0, 1, 2, 3, 4, 5, 6, 7, 8, 9, 10, 11):
        u.append((("rw", i), "w_in", 0, 8, P * i, P))
    base = 1824
    for i in range(12):
        u.append((("qk", i), "w_in", 0, 8, base + P * i, P))
    for s in range(4):
        u.append((("v0", s), "w_in", 2 * P * s, 2, base + 2 * ATT_W, 512))
    for s in range(2):
        u.append((("v1", s), "w_in", 4 * P * s, 4, base + 2 * ATT_W + 512, 256))
    for i in GATE_ORDER:
        u.append((("gate", i), "w_gate", 0, 8, P * i, P))
    for i in range(0, 8, 4):
        u.append((("bb", i), "w_branch_b", 0, 2, P * i, 512))
        u.append((("ba", i), "w_branch_a", 0, 4, P * i, 256))
        u.append((("ba", i + 2), "w_branch_a", 0, 4, P * (i + 2), 256))
    for h in range(2):
        for s in range(4):
            u.append((("out", h, s), "w_out", 2 * P * s, 2, 512 * h, 512))
    for i in range(NF):
        u.append((("up", i), "w_up", 0, 8, P * i, P))
        u.append((("up", NF + i), "w_up", 0, 8, DFF + P * i, P))
    for h in range(2):
        for s in range(NF // 2):
            u.append((("down", h, s), "w_down", 2 * P * s, 2, 512 * h, 512))
    for h in range(2):
        u.append((("ple", h), "w_ple", 0, 2, 512 * h, 512))
    for h in range(2):
        for s in range(4):
            u.append((("pleg", h, s), "w_ple_gate", 2 * P * s, 2, 512 * h, 512))
    return u


UNITS = weight_units()
UIDX = {x[0]: n for n, x in enumerate(UNITS)}


def build(nc, ins, out, known):
    W = {}
    for name in ("w_in", "w_gate", "w_branch_a", "w_branch_b", "w_out", "w_up", "w_down", "w_ple_gate", "w_ple"):
        W[name] = ins[name].rearrange("l k n -> (l k) n")
    x_d = ins["x"].rearrange("b (m p) d -> p (b m) d", p=P)
    out_d = out.rearrange("b (m p) d -> p (b m) d", p=P)
    p_d = ins["p"].rearrange("l b (m p) d -> p (l b m) d", p=P)

    with ExitStack() as ctx:
        def sem(name):
            return ctx.enter_context(nc.semaphore(name))

        base = -(-nc.sbuf_base // 64) * 64
        top = [base]

        def sb_at(name, shape, dt, offset):
            return nc.alloc_sbuf_tensor_at(name, shape, dt, offset=offset)

        def sb(name, words, shape=None, dt=F32):
            t = sb_at(name, shape or [P, words], dt, top[0])
            top[0] += 4 * words
            return t

        consts = sb("consts", 2048)
        params = sb("params", 3 * P)
        stat = sb("stat", 256)
        hT_hi = sb("hT_hi", 4096, [P, KD, SEQ], F32R)
        hT_lo = sb("hT_lo", 4096, [P, KD, SEQ], F32R)
        raw = sb("raw", RAW_SLOTS * UNIT, [P, RAW_SLOTS, UNIT])
        w_hi = sb("w_hi", W_SLOTS * UNIT, [P, W_SLOTS, UNIT], F32R)
        w_lo = sb("w_lo", W_SLOTS * UNIT, [P, W_SLOTS, UNIT], F32R)
        yb_hi = sb("yb_hi", 1024, [P, 2, SEQ], F32R)
        yb_lo = sb("yb_lo", 1024, [P, 2, SEQ], F32R)
        R0 = top[0]
        KB = 1024
        assert R0 + 128 * KB <= nc.sbuf_usable_end, (R0, nc.sbuf_usable_end)

        def at(name, kb, shape, dt=F32):
            return sb_at(name, shape, dt, R0 + int(kb * KB))

        xs = at("xs", 56, [P, NT, DM])
        xn_a = at("xn_a", 72, [P, NT, DM])
        stage = at("stage", 88, [P, 3, P])
        Rr, Kk, Aa, KK, Vv, Gg, Bo = [at(n, 8 * i, [P, NPAIR, SEQ]) for i, n in
                                      enumerate(("Rr", "Kk", "Aa", "KK", "Vv", "Gg", "Bo"))]
        qk = at("qk", 56, [P, 12, SEQ])
        vtok = at("vtok", 80, [P, NT, ATT_W])
        dist = at("dist", 92, [P, 2 * P + 2 * SEQ])
        Sx = at("Sx", 97, [P, 3, 1280])
        PT = at("PT", 112, [P, 2, 10, P])
        names = ["Bf", "Kf", "Vf", "Xx", "XT", "Am", "Ak", "Rb", "Rk", "Vt", "Bt", "Kt"]
        CM = {n: at(n, 56 + 4 * i, [P, 2, 512]) for i, n in enumerate(names)}
        At = at("At", 104, [P, 4, 512])
        Rt = at("Rt", 120, [P, 4, 512])
        Zs = at("Zs", 112, [P, 2, 512])
        Wp = at("Wp", 116, [P, 2, 512])
        lora_x = at("lora_x", 112, [P, 3, SEQ])
        lora_w = at("lora_w", 118, [P, 3, RW])
        Lt, Et, Ei, Sc = [at(n, 112 + 4 * i, [P, 2, SEQ]) for i, n in enumerate(("Lt", "Et", "Ei", "Sc"))]
        ya_hi = at("ya_hi", 88, [P, NPAIR, SEQ], F32R)
        ya_lo = at("ya_lo", 96, [P, NPAIR, SEQ], F32R)
        gn = at("gn", 104, [P, NPAIR, SEQ])
        mg_hi = at("mg_hi", 56, [P, KD, SEQ], F32R)
        mg_lo = at("mg_lo", 72, [P, KD, SEQ], F32R)
        xr = at("xr", 112, [P, NT, DM])
        xn_b = at("xn_b", 32, [P, NT, DM])
        g_hi = at("g_hi", 0, [P, NF, SEQ], F32R)
        g_lo = at("g_lo", 48, [P, NF, SEQ], F32R)
        cbuf = at("cbuf", 96, [P, 2, 4, SEQ])
        p_raw = at("p_raw", 96, [P, NT, PLE])
        pT_hi = at("pT_hi", 100, [P, 2, SEQ], F32R)
        pT_lo = at("pT_lo", 104, [P, 2, SEQ], F32R)
        xn_c = at("xn_c", 0, [P, NT, DM])
        psig = at("psig", 16, [P, NT, 512])
        gfin = at("gfin", 24, [P, DM])
        pple = at("pple", 28, [P, NT, DM])
        junk = at("junk", 44, [P, 2, 512])

        def cst(n):
            k = CONST_NAMES.index(n)
            return consts[:, k * P:(k + 1) * P]

        def cst4(n):
            return cst(n).unsqueeze(1).broadcast_to([P, NPAIR, P])

        reset = consts[:, len(CONST_NAMES) * P:len(CONST_NAMES) * P + SEQ]
        ident = cst("ident")

        def gate_at(i):
            n = GATE_ORDER.index(i)
            if n >= 12:
                return Rr[:, n - 12, :].rearrange("p (a b) -> p a b", a=4)
            return (Kk, Aa, Vv)[n % 3][:, :, (n // 3) * P:(n // 3 + 1) * P]

        def par(name, i, lo=0, hi=P):
            c = PARAM_COL[name] + i
            return params[lo:hi, c:c + 1]

        omm, omka, ec, ss, rms, rstd = 0, 16, 32, 96, 104, 108
        negmax, den, rden, epsc = 112, 128, 144, 160

        bank = [ctx.enter_context(nc.psum_tensor(f"bank{i}", [P, 512], F32)) for i in range(BANKS)]

        x_in = [sem(f"x_in{m}") for m in range(NT)]
        par_in, cst_in, dist_in, lora_in, xr_in, p_in, gf_in, out_done = [
            sem(n) for n in ("par_in", "cst_in", "dist_in", "lora_in", "xr_in", "p_in", "gf_in", "out_done")]
        landed = [sem(f"landed{i}") for i in range(RAW_SLOTS)]
        signal = {name: sem(name) for name in SIGNALS}

        count = {name: 0 for name in signal}
        latest, steps, readers, turn = {}, {}, {}, {}
        earlier = known or {"steps": {}, "readers": {}, "turn": {}}

        def step(who, *labels):
            name = f"{who}_{labels[0][0]}" if labels else f"{who}_chain"
            count[name] += 1
            latest[who] = (name, count[name])
            for label in labels:
                steps[(who,) + label] = latest[who]
            return signal[name], 1

        def frees(who, bank_label, *labels):
            got = step(who, *(labels or (("psum_read",),)))
            readers[bank_label] = latest[who]
            return got

        def done(who, *label):
            name, n = earlier["steps"].get((who,) + label, (f"{who}_chain", 1))
            return signal[name], n

        def previous(who):
            name, n = latest[who]
            return signal[name], n

        def psum(label):
            return bank[earlier["turn"].get(label, 0) % BANKS]

        order = []
        block = ctx.enter_context(nc.Block())
        n_par = len(PARAM_ROWS) + 1 + 4

        def fill_blocks(who, copy, gr, parts):
            for n, (dst, slot, src) in enumerate(parts):
                for q in range(2):
                    r = slice(CH * q, CH * q + CH)
                    for s in range(2):
                        c = 2 * gr + s
                        d = dst[r, slot + s, :].rearrange("p (h two t) -> p h two t", two=2, t=CH)[:, :, q, :]
                        last = (("fill", gr),) if n == len(parts) - 1 and q == 1 and s == 1 else ()
                        copy(d, src[r, :, c * CH:(c + 1) * CH]).then_inc(*step(who, *last))

        @block.sync
        def _(sp):
            for m in range(NT):
                sp.dma_start(xs[:, m, :], x_d[:, m, :]).then_inc(x_in[m], 16)
            sp.wait_ge(*done("dve", "stage"))
            for name, rows in PARAM_ROWS:
                c = PARAM_COL[name]
                src = ins[name].rearrange("l a b -> l (a b)") if name == "rw_r_k" else ins[name]
                full = src.shape[1] // P
                sp.dma_start(stage[c:c + full, 0, :], src[0, 0:full * P].rearrange("(r n) -> r n", n=P)).then_inc(par_in, 16)
                if full < rows:
                    sp.dma_start(stage[c + full:c + rows, 0, 0:src.shape[1] - full * P],
                                 src[:, full * P:]).then_inc(par_in, 16)
            for b, r, src in ((1, 0, ins["conv_w"][0, 0]), (1, 48, ins["conv_w"][0, 1]),
                              (2, 0, ins["conv_w"][0, 2]), (2, 48, ins["conv_b"][0])):
                sp.dma_start(stage[r:r + 48, b, :], src.rearrange("(r n) -> r n", n=P)).then_inc(par_in, 16)
            for n, (label, name, r0, t, c0, w) in enumerate(UNITS):
                if n >= RAW_SLOTS:
                    sp.wait_ge(*done("pool", "lo", n - RAW_SLOTS))
                src = W[name][r0:r0 + t * P, c0:c0 + w].rearrange("(t p) n -> p t n", p=P)
                dst = raw[:, n % RAW_SLOTS, :].rearrange("p (t n) -> p t n", t=t)
                sp.dma_start(dst, src).then_inc(landed[n % RAW_SLOTS], 16)
                if label == ("out", 0, 1):
                    sp.wait_ge(*done("act", "ya_hi", NPAIR - 1))
                    sp.dma_start(xr[:, :, :], x_d).then_inc(xr_in, 16)
                if label == ("down", 0, 4):
                    sp.wait_ge(*done("dve", "g_lo", NF - 1))
                    sp.dma_start(p_raw[:, :, :], p_d).then_inc(p_in, 16)
                if label == ("pleg", 0, 3):
                    sp.wait_ge(*done("pe", "dn", 1, NT - 1))
                    sp.dma_start(gfin[:, :], ins["g_final"].partition_broadcast(P)).then_inc(gf_in, 16)
            for m in range(NT):
                sp.wait_ge(*done("dve", "final", m))
                sp.dma_start(out_d[:, m, :], xr[:, m, :]).then_inc(out_done, 16)
            sp.wait_ge(out_done, 16 * NT)

        @block.gpsimd
        def _(gp):
            nc.gpsimd.memset(stat[:, epsc:epsc + 1], NORM_EPS).then_inc(*step("pool"))
            nc.gpsimd.memset(stat[:, epsc + 1:epsc + 2], LN_EPS).then_inc(*step("pool", ("eps",)))
            def clear_chunks():
                gp.wait_ge(*done("pe", "o", 15))
                gp.wait_ge(*done("dve", "preC", NPAIR - 1))
                for n in ("Bf", "Kf", "Vf"):
                    nc.gpsimd.memset(CM[n][:, :, :], 0.0).then_inc(*step("pool"))
                nc.gpsimd.memset(At[:, :, :], 0.0).then_inc(*step("pool"))
                nc.gpsimd.memset(Rt[:, :, :], 0.0).then_inc(*step("pool"))
                nc.gpsimd.memset(Zs[:, 0, :], 0.0).then_inc(*step("pool", ("cleared",)))

            for n in range(len(UNITS)):
                if n == UIDX[("gate", GATE_ORDER[0])] + 1:
                    clear_chunks()
                gp.wait_ge(*done("act", "hi", n))
                nc.gpsimd.tensor_tensor(w_lo[:, n % W_SLOTS, :], raw[:, n % RAW_SLOTS, :],
                    w_hi[:, n % W_SLOTS, :].bitcast(F32), ALU.subtract).then_inc(*step("pool", ("lo", n)))

        @block.tensor
        def _(pe):
            def begin(*label):
                n = len(order)
                order.append(label)
                turn[label] = n
                if n >= BANKS:
                    name, at_ = earlier["readers"].get(order[n - BANKS], ("dve_psum_read", 1))
                    pe.wait_ge(signal[name], at_)
                return bank[n % BANKS]

            def split3(o, wh, wl, ah, al, first, last):
                nc.tensor.matmul(o, wh, ah, start=first, stop=False)
                nc.tensor.matmul(o, wh, al, start=False, stop=False)
                return nc.tensor.matmul(o, wl, ah, start=False, stop=last)

            def feature_unit(label, *bank_label, fresh=None):
                n = UIDX[label]
                o = begin(*bank_label)
                pe.wait_ge(*done("pool", "lo", n))
                for t in range(KD):
                    if fresh:
                        pe.wait_ge(*done("dve", "hT_lo", fresh, t))
                    k = slice(t * P, (t + 1) * P)
                    mm = split3(o[:, :], w_hi[:, n % W_SLOTS, k], w_lo[:, n % W_SLOTS, k],
                                hT_hi[:, t, :], hT_lo[:, t, :], t == 0, t == KD - 1)
                mm.then_inc(*step("pe", ("unit", n), bank_label))

            def token_units(labels, outs, a_hi, a_lo, kts, cols, fresh=None):
                bs = [begin(*o) for o in outs]
                for s, label in enumerate(labels):
                    n = UIDX[label]
                    pe.wait_ge(*done("pool", "lo", n))
                    for m in range(NT):
                        for j in range(kts):
                            k = s * kts + j
                            if fresh and m == 0:
                                pe.wait_ge(*done("dve", *fresh, k))
                            c = slice(j * cols, (j + 1) * cols)
                            tok = slice(m * P, (m + 1) * P)
                            first, last = k == 0, k == kts * len(labels) - 1
                            o = bs[m][:, 0:cols]
                            nc.tensor.matmul(o, a_hi[:, k, tok], w_hi[:, n % W_SLOTS, c], start=first, stop=False)
                            nc.tensor.matmul(o, a_hi[:, k, tok], w_lo[:, n % W_SLOTS, c], start=False, stop=False)
                            mm = nc.tensor.matmul(o, a_lo[:, k, tok], w_hi[:, n % W_SLOTS, c], start=False, stop=last)
                        marks = ([outs[m]] if last else []) + ([("unit", n)] if m == NT - 1 else [])
                        if marks:
                            mm.then_inc(*step("pe", *marks))

            def transposed(tag, src, tiles):
                for k in range(tiles):
                    o = begin(tag, k)
                    for m in range(NT):
                        mm = nc.tensor.transpose(o[:, m * P:(m + 1) * P], src[:, m, k * P:(k + 1) * P], ident)
                    mm.then_inc(*step("pe", (tag, k)))

            pe.wait_ge(cst_in, 16)
            pe.wait_ge(par_in, 16 * n_par)
            for b, rows in enumerate(PARAM_USED):
                o = begin("par", b)
                nc.tensor.transpose(o[:, 0:rows], stage[0:rows, b, :], ident[0:rows, 0:rows]) \
                    .then_inc(*step("pe", ("par", b)))
            for m in range(NT):
                pe.wait_ge(*done("dve", "xn_a", m))
            transposed("na", xn_a, KD)

            for i in (12, 13, 14, 0, 1, 2, 3, 4, 5, 6, 7):
                feature_unit(("rw", i), "rw", i, fresh="na" if i == 12 else None)
            pe.wait_ge(lora_in, 64)
            pe.wait_ge(*done("act", "lora_act"))
            for i in range(NPAIR):
                c = slice(i * P, (i + 1) * P)
                o = begin("lw", i)
                nc.tensor.matmul(o[:, :], lora_w[0:64, 0, c], lora_x[0:64, 0, :], start=True, stop=True) \
                    .then_inc(*step("pe", ("lw", i)))
                o = begin("la", i)
                nc.tensor.matmul(o[:, :], lora_w[64:128, 0, c], lora_x[64:128, 0, :], start=True, stop=True) \
                    .then_inc(*step("pe", ("la", i)))
                o = begin("lg", i)
                nc.tensor.matmul(o[:, :], lora_w[:, 1, c], lora_x[:, 1, :], start=True, stop=False)
                nc.tensor.matmul(o[:, :], lora_w[0:32, 2, c], lora_x[0:32, 2, :], start=False, stop=True) \
                    .then_inc(*step("pe", ("lg", i)))
            for i in range(8, 12):
                feature_unit(("rw", i), "rw", i)

            def head_sums(tag, src, p):
                o = begin(tag, p)
                nc.tensor.matmul(o[:, :], cst("heads"), src, start=True, stop=True).then_inc(*step("pe", (tag, p)))

            def key_norm(p):
                pe.wait_ge(*done("act", "kk_sq", p))
                head_sums("kn", Sc[:, p % 2, :], p)

            def bonus_sum(p):
                pe.wait_ge(*done("dve", "rk", p))
                head_sums("bn", Sc[:, p % 2, :], p)

            for i in range(12):
                feature_unit(("qk", i), "qk", i)
                if i % 3 == 2:
                    key_norm(i // 3)
                    if i // 3 >= 1:
                        bonus_sum(i // 3 - 1)
            token_units([("v0", s) for s in range(4)], [("vt0", m) for m in range(NT)], hT_hi, hT_lo, 2, 512)
            bonus_sum(NPAIR - 1)
            token_units([("v1", s) for s in range(2)], [("vt1", m) for m in range(NT)], hT_hi, hT_lo, 4, 256)

            def scores(it):
                j, qt = it // NT, it % NT
                for g in range(3):
                    h = ATT_HG * g + j
                    r = slice(HD * (h % 2), HD * (h % 2) + HD)
                    k0 = max(0, qt - 1) if g == 0 else 0
                    n = (qt + 1 - k0) * P
                    o = begin("s", it, g)
                    nc.tensor.matmul(o[:, 0:n], qk[r, h // 2, qt * P:(qt + 1) * P],
                        qk[r, 6 + h // 2, k0 * P:(qt + 1) * P], start=True, stop=True).then_inc(*step("pe", ("s", it, g)))

            pe.wait_ge(*done("act", "vt1", NT - 1))
            scores(0)
            scores(1)
            for it in range(16):
                if it + 2 < 16:
                    scores(it + 2)
                j, qt = it // NT, it % NT
                tiles = att_tiles(j, qt)
                pe.wait_ge(*done("dve", "P", it))
                for c in range(0, len(tiles), 4):
                    o = begin("t", it, c)
                    for x in range(c, min(c + 4, len(tiles))):
                        mm = nc.tensor.transpose(o[:, (x - c) * P:(x - c + 1) * P], Sx[:, it % 3, x * P:(x + 1) * P], ident)
                    mm.then_inc(*step("pe", ("t", it, c), ("tall", it)))
                r = slice(HD * (j % 2), HD * (j % 2) + HD)
                o = begin("o", it)
                for x, (h, kt) in enumerate(tiles):
                    if x % 4 == 0:
                        pe.wait_ge(*done("act", "pt", it, x))
                    mm = nc.tensor.matmul(o[r, 0:P], vtok[:, kt, HD * h:HD * (h + 1)], PT[:, it % 2, x, :],
                                          start=(x == 0), stop=(x == len(tiles) - 1))
                mm.then_inc(*step("pe", ("o", it)))

            def four(label, pairs):
                o = begin(*label)
                for p in range(NPAIR):
                    c = slice(p * P, (p + 1) * P)
                    for x, (a, b) in enumerate(pairs):
                        mm = nc.tensor.matmul(o[:, c], a[:, c], b[:, c], start=(x == 0), stop=(x == len(pairs) - 1))
                mm.then_inc(*step("pe", label))

            def four_t(label, src):
                o = begin(*label)
                for p in range(NPAIR):
                    c = slice(p * P, (p + 1) * P)
                    mm = nc.tensor.transpose(o[:, c], src[:, c], ident)
                mm.then_inc(*step("pe", label))

            for gr in range(NCH // 2):
                pe.wait_ge(*done("dve", "fill", gr))
                pe.wait_ge(*done("act", "fill", gr))

                def side(kind, s):
                    B, K, V = (CM[n][:, s, :] for n in ("Bf", "Kf", "Vf"))
                    A, R = At[:, 2 * (gr % 2) + s, :], Rt[:, 2 * (gr % 2) + s, :]
                    c = 2 * gr + s
                    if kind == "Vt":
                        four_t(("Vt", c), V)
                    if kind == "Bt":
                        four_t(("Bt", c), B)
                    if kind == "Kt":
                        four_t(("Kt", c), K)
                    if kind == "Ak":
                        four(("Ak", c), [(K, A)])
                    if kind == "Rb":
                        four(("Rb", c), [(B, R)])
                    if kind == "Rk":
                        four(("Rk", c), [(K, R)])

                for s in range(2):
                    B, A = CM["Bf"][:, s, :], At[:, 2 * (gr % 2) + s, :]
                    four(("AT", 2 * gr + s), [(B, A)])
                    four(("A", 2 * gr + s), [(A, B)])
                for lv in range(5):
                    for s in range(2):
                        c = 2 * gr + s
                        pe.wait_ge(*done("dve", "X", c, lv))
                        four(("W", c, lv), [(CM["Am"][:, s, :], CM["Xx"][:, s, :])])
                    for s in range(2):
                        four_t(("XT", 2 * gr + s, lv), CM["Xx"][:, s, :])
                    for kind in (("Vt", "Ak"), ("Bt",), ("Kt",), ("Rb",), ("Rk",))[lv]:
                        for s in range(2):
                            side(kind, s)
                    for s in range(2):
                        c = 2 * gr + s
                        pe.wait_ge(*done("dve", "Wp", c, lv))
                        pe.wait_ge(*done("act", "XT", c, lv))
                        four(("XW", c, lv), [(CM["XT"][:, s, :], Wp[:, s, :])])
                for s in range(2):
                    c = 2 * gr + s
                    Z = Zs[:, c % 2, :]
                    A, R = At[:, 2 * (gr % 2) + s, :], Rt[:, 2 * (gr % 2) + s, :]
                    U1, U = CM["XT"][:, s, :], CM["Am"][:, s, :]
                    pe.wait_ge(*done("act", "Kt", c))
                    pe.wait_ge(*done("dve", "Rk", c))
                    pe.wait_ge(*done("dve", "X", c, 5))
                    if c == 0:
                        pe.wait_ge(*done("pool", "cleared"))
                    else:
                        pe.wait_ge(*done("dve", "Z", c))
                    four(("u1", c), [(A, Z), (CM["Ak"][:, s, :], CM["Vt"][:, s, :])])
                    y = begin("y", c)
                    for p in range(NPAIR):
                        h = slice(p * P, (p + 1) * P)
                        nc.tensor.matmul(y[:, h], Z[:, h], R[:, h], start=(p == 0), stop=False, skip_group_check=True)
                        nc.tensor.matmul(y[:, h], CM["Vt"][:, s, h], CM["Rk"][:, s, h], start=False, stop=False,
                                         skip_group_check=True)
                    pe.wait_ge(*done("act", "U1", c))
                    four(("u2", c), [(CM["Xx"][:, s, :], U1)])
                    feature_unit(("gate", c), "gate", c)
                    pe.wait_ge(*done("act", "U", c))
                    if c + 1 < NCH:
                        four(("z", c), [(CM["Bt"][:, s, :], U), (CM["Kt"][:, s, :], CM["Vt"][:, s, :])])
                    for p in range(NPAIR):
                        h = slice(p * P, (p + 1) * P)
                        mm = nc.tensor.matmul(y[:, h], U[:, h], CM["Rb"][:, s, h], start=False, stop=True,
                                              skip_group_check=True)
                    mm.then_inc(*step("pe", ("y", c)))
                    if s == 0:
                        feature_unit(("gate", NCH + gr), "gate", NCH + gr)

            pe.wait_ge(*done("act", "y", NCH - 1))
            for p in range(NPAIR):
                head_sums("mu", KK[:, p, :], p)
            feature_unit(("gate", 12), "gate", 12)
            for p in range(NPAIR):
                pe.wait_ge(*done("act", "gn_sq", p))
                head_sums("var", gn[:, p, :], p)
            for i in range(13, 16):
                feature_unit(("gate", i), "gate", i)

            def branch(label, tag, outs, kts, a_hi, a_lo):
                n = UIDX[label]
                pe.wait_ge(*done("pool", "lo", n))
                w = UNIT // kts
                for x, i in enumerate(outs):
                    o = begin(tag, i)
                    for k in range(kts):
                        c = slice(k * w + x * P, k * w + (x + 1) * P)
                        mm = split3(o[:, :], w_hi[:, n % W_SLOTS, c], w_lo[:, n % W_SLOTS, c],
                                    a_hi[:, k, :], a_lo[:, k, :], k == 0, k == kts - 1)
                    mm.then_inc(*step("pe", (tag, i), ("unit", n)))

            for i in range(0, KD, 4):
                branch(("bb", i), "pb", range(i, i + 4), 2, yb_hi, yb_lo)
                pe.wait_ge(*done("dve", "ya_lo", NPAIR - 1))
                branch(("ba", i), "pa", range(i, i + 2), 4, ya_hi, ya_lo)
                branch(("ba", i + 2), "pa", range(i + 2, i + 4), 4, ya_hi, ya_lo)

            for h in range(2):
                token_units([("out", h, s) for s in range(4)], [("op", h, m) for m in range(NT)], mg_hi, mg_lo, 2, 512,
                            fresh=("mg_lo",) if h == 0 else None)
            for m in range(NT):
                pe.wait_ge(*done("dve", "xn_b", m))
            transposed("nb", xn_b, KD)

            for i in range(NF):
                feature_unit(("up", i), "up", i, fresh="nb" if i == 0 else None)
                feature_unit(("up", NF + i), "up", NF + i)
            for h in range(2):
                token_units([("down", h, s) for s in range(NF // 2)], [("dn", h, m) for m in range(NT)], g_hi, g_lo, 2, 512,
                            fresh=("g_lo",) if h == 0 else None)
                if h == 0:
                    pe.wait_ge(p_in, 16)
                    transposed("np", p_raw, 2)
            pe.wait_ge(*done("dve", "pT_lo", 1))
            for h in range(2):
                token_units([("ple", h)], [("pp", h, m) for m in range(NT)], pT_hi, pT_lo, 2, 512)
            for m in range(NT):
                pe.wait_ge(*done("dve", "xn_c", m))
            transposed("nc", xn_c, KD)
            for h in range(2):
                token_units([("pleg", h, s) for s in range(4)], [("pg", h, m) for m in range(NT)], hT_hi, hT_lo, 2, 512,
                            fresh=("hT_lo", "nc") if h == 0 else None)

        @block.scalar
        def _(act):
            act.dma_start(consts[:, :], ins["consts"]).then_inc(cst_in, 16)
            act.dma_start(dist[:, :], ins["dist"]).then_inc(dist_in, 16)
            act.dma_start(lora_w[0:64, 0, :], ins["rw_w_up"][0]).then_inc(lora_in, 16)
            act.dma_start(lora_w[64:128, 0, :], ins["rw_a_up"][0]).then_inc(lora_in, 16)
            act.dma_start(lora_w[:, 1, :], ins["rw_g_up"][0, 0:P, :]).then_inc(lora_in, 16)
            act.dma_start(lora_w[0:32, 2, :], ins["rw_g_up"][0, P:, :]).then_inc(lora_in, 16)
            nxt = [0]

            def hi_upto(n):
                while nxt[0] <= min(n, len(UNITS) - 1):
                    u = nxt[0]
                    act.wait_ge(landed[u % RAW_SLOTS], 16 * (u // RAW_SLOTS + 1))
                    if u >= W_SLOTS:
                        act.wait_ge(*done("pe", "unit", u - W_SLOTS))
                        act.wait_ge(*done("pool", "lo", u - W_SLOTS))
                    nc.scalar.activation(w_hi[:, u % W_SLOTS, :], raw[:, u % RAW_SLOTS, :], ACT.Copy) \
                        .then_inc(*step("act", ("hi", u)))
                    nxt[0] += 1

            def before(label):
                hi_upto(UIDX[label] + W_SLOTS)


            def squares_of(tag, src, scratch, m, h):
                c = slice(512 * h, 512 * h + 512)
                if tag == "na":
                    act.wait_ge(x_in[m], 16)
                else:
                    act.wait_ge(*done("dve", "x_" + tag, h, m))
                k = ss + NT * h + m
                nc.scalar.activation(scratch[:, (NT * h + m) % 2, :], src[:, m, c], ACT.Square,
                                     accum_out=stat[:, k:k + 1]).then_inc(*step("act", ("sq", tag, h, m)))

            def root(tag, m0=0, m1=NT):
                act.wait_ge(*done("dve", "ms", tag, m0))
                nc.scalar.activation(stat[:, rms + m0:rms + m1], stat[:, rms + m0:rms + m1], ACT.Sqrt,
                                     scale=1.0 / DM, bias=stat[:, epsc:epsc + 1]).then_inc(*step("act", ("rms", tag, m0)))

            def gained_hi(tag, gain, tiles, dst):
                for k in range(tiles):
                    act.wait_ge(*done("pe", tag, k))
                    scale = par(gain, k) if gain else 1.0
                    nc.scalar.activation(dst[:, k, :], psum((tag, k))[:, :], ACT.Copy, scale=scale) \
                        .then_inc(*step("act", ("hi", tag, k)))

            act.wait_ge(*done("pool", "eps"))
            for m in range(2):
                for h in range(2):
                    if m or h:
                        act.wait_ge(*previous("act"))
                    squares_of("na", xs, Rr, m, h)
            root("na")
            hi_upto(W_SLOTS - 1)
            act.wait_ge(*done("dve", "params"))
            gained_hi("na", "g_mix", KD, hT_hi)

            dsts = {12: lora_x[:, 0, :], 13: lora_x[:, 1, :], 14: lora_x[:, 2, :]}
            for i in range(4):
                dsts[i], dsts[4 + i], dsts[8 + i] = Rr[:, i, :], Kk[:, i, :], Vv[:, i, :]

            def shift_own(i):
                before(("rw", i))
                act.wait_ge(*done("pe", "rw", i))
                rows = 32 if i == 14 else P
                nc.scalar.activation(dsts[i][0:rows, :], psum(("rw", i))[0:rows, :], ACT.Copy,
                    scale=stat[0:rows, omm + i:omm + i + 1]).then_inc(*step("act", ("own", i)))

            act.wait_ge(*done("dve", "derived"))
            for i in (12, 13, 14, 0, 1, 2):
                shift_own(i)
            act.wait_ge(*done("dve", "shift", 14))
            nc.scalar.activation(lora_x[0:64, 0, :], lora_x[0:64, 0, :], ACT.Tanh).then_inc(*step("act"))
            nc.scalar.activation(lora_x[:, 1, :], lora_x[:, 1, :], ACT.Sigmoid).then_inc(*step("act"))
            nc.scalar.activation(lora_x[0:32, 2, :], lora_x[0:32, 2, :], ACT.Sigmoid).then_inc(*step("act", ("lora_act",)))
            for i in (3, 4, 5, 6, 7):
                shift_own(i)
            for i in range(NPAIR):
                act.wait_ge(*done("pe", "lw", i))
                nc.scalar.activation(Bo[:, i, :], psum(("lw", i))[:, :], ACT.Sigmoid, bias=par("rw_w0", i)) \
                    .then_inc(*frees("act", ("lw", i), ("lw", i)))
                act.wait_ge(*done("pe", "la", i))
                nc.scalar.activation(Aa[:, i, :], psum(("la", i))[:, :], ACT.Sigmoid, bias=par("rw_a0", i)) \
                    .then_inc(*frees("act", ("la", i), ("la", i)))
                act.wait_ge(*done("pe", "lg", i))
                nc.scalar.activation(Gg[:, i, :], psum(("lg", i))[:, :], ACT.Copy) \
                    .then_inc(*frees("act", ("lg", i), ("lg", i)))
            for i in range(8, 12):
                shift_own(i)

            def squares(p):
                act.wait_ge(*done("dve", "kkr", p))
                nc.scalar.activation(Sc[:, p % 2, :], KK[:, p, :], ACT.Square).then_inc(*step("act", ("kk_sq", p)))

            def decays(p):
                q = p % 2
                act.wait_ge(*done("dve", "L", p))
                if p >= 2:
                    act.wait_ge(*done("dve", "preC", p - 2))
                nc.scalar.activation(Et[:, q, :], Lt[:, q, :], ACT.Exp, scale=-DECAY).then_inc(*step("act"))
                nc.scalar.activation(Ei[:, q, :], Lt[:, q, :], ACT.Exp, scale=DECAY).then_inc(*step("act", ("E", p)))

            for i in range(12):
                before(("qk", i))
                act.wait_ge(*done("pe", "qk", i))
                nc.scalar.activation(qk[:, i, :], psum(("qk", i))[:, :], ACT.Copy,
                    scale=HD ** -0.5 if i < 6 else 1.0).then_inc(*frees("act", ("qk", i), ("qk", i)))
                if i % 3 == 0:
                    squares(i // 3)
                if i % 3 == 1:
                    decays(i // 3)
                if i % 3 == 2:
                    p = i // 3
                    act.wait_ge(*done("pe", "kn", p))
                    nc.scalar.activation(Sc[:, p % 2, :], psum(("kn", p))[:, :], ACT.Sqrt) \
                        .then_inc(*frees("act", ("kn", p), ("kn", p)))
            for c, w, n in ((0, 512, 4), (512, 256, 2)):
                tag = "vt0" if c == 0 else "vt1"
                for s in range(n):
                    before(("v0" if c == 0 else "v1", s))
                for m in range(NT):
                    act.wait_ge(*done("pe", tag, m))
                    nc.scalar.activation(vtok[:, m, c:c + w], psum((tag, m))[:, 0:w], ACT.Copy) \
                        .then_inc(*frees("act", (tag, m), (tag, m)))

            def expo(it):
                act.wait_ge(*done("dve", "max", it))
                n = len(att_tiles(it // NT, it % NT)) * P
                nc.scalar.activation(Sx[:, it % 3, 0:n], Sx[:, it % 3, 0:n], ACT.Exp,
                    bias=stat[:, negmax + it:negmax + it + 1],
                    accum_out=stat[:, den + it:den + it + 1]).then_inc(*step("act", ("exp", it)))

            expo(0)
            for it in range(16):
                if it + 1 < 16:
                    expo(it + 1)
                j, qt = it // NT, it % NT
                n = len(att_tiles(j, qt))
                for c in range(0, n, 4):
                    w = min(4, n - c)
                    act.wait_ge(*done("pe", "t", it, c))
                    if it >= 2:
                        act.wait_ge(*done("pe", "o", it - 2))
                    nc.scalar.activation(PT[:, it % 2, c:c + w, :].rearrange("p a b -> p (a b)"),
                        psum(("t", it, c))[:, 0:w * P], ACT.Copy).then_inc(*frees("act", ("t", it, c), ("pt", it, c)))
                r = slice(HD * (j % 2), HD * (j % 2) + HD)
                act.wait_ge(*done("pe", "o", it))
                nc.scalar.activation(yb_hi[r, j // 2, qt * P:(qt + 1) * P], psum(("o", it))[r, 0:P], ACT.Copy) \
                    .then_inc(*step("act", ("yb_hi", it)))

            def gate(i):
                before(("gate", i))
                act.wait_ge(*done("pe", "gate", i))
                taken = min(GATE_ORDER.index(i) // 3, NCH // 2 - 1)
                act.wait_ge(*done("dve", "fill", taken))
                act.wait_ge(*done("act", "fill", taken))
                nc.scalar.activation(gate_at(i), psum(("gate", i))[:, :].rearrange("p (a b) -> p a b", a=4), ACT.Sigmoid,
                                     bias=par("b_gate", i)).then_inc(*frees("act", ("gate", i), ("gate", i)))

            def fill(gr):
                if gr == 0:
                    act.wait_ge(*done("pool", "cleared"))
                    act.wait_ge(*done("dve", "preC", NPAIR - 1))
                else:
                    for s in range(2):
                        for k in ("Kt", "Vt", "Rk"):
                            act.wait_ge(*done("pe", k, 2 * (gr - 1) + s))
                    if gr >= 2:
                        act.wait_ge(*done("pe", "y", 2 * gr - 3))
                fill_blocks("act", nc.scalar.copy, gr, ((CM["Kf"], 0, Kk), (CM["Vf"], 0, Vv), (Rt, 2 * (gr % 2), Rr)))

            fill(0)
            for gr in range(NCH // 2):
                for lv in range(5):
                    for s in range(2):
                        c = 2 * gr + s
                        act.wait_ge(*done("pe", "XT", c, lv))
                        nc.scalar.activation(CM["XT"][:, s, :], psum(("XT", c, lv))[:, :], ACT.Copy) \
                            .then_inc(*frees("act", ("XT", c, lv), ("XT", c, lv)))
                    if lv < 3:
                        kind = ("Vt", "Bt", "Kt")[lv]
                        for s in range(2):
                            c = 2 * gr + s
                            act.wait_ge(*done("pe", kind, c))
                            nc.scalar.activation(CM[kind][:, s, :], psum((kind, c))[:, :], ACT.Copy) \
                                .then_inc(*frees("act", (kind, c), (kind, c)))
                if gr + 1 < NCH // 2:
                    fill(gr + 1)
                for s in range(2):
                    c = 2 * gr + s
                    act.wait_ge(*done("pe", "u1", c))
                    nc.scalar.activation(CM["XT"][:, s, :], psum(("u1", c))[:, :], ACT.Copy) \
                        .then_inc(*frees("act", ("u1", c), ("U1", c)))
                    act.wait_ge(*done("pe", "u2", c))
                    nc.scalar.activation(CM["Am"][:, s, :], psum(("u2", c))[:, :], ACT.Copy) \
                        .then_inc(*frees("act", ("u2", c), ("U", c)))
                    gate(c)
                    act.wait_ge(*done("pe", "y", c))
                    if c == 0:
                        act.wait_ge(*done("dve", "fill", 0))
                    for q in range(2):
                        r = slice(CH * q, CH * q + CH)
                        y = psum(("y", c))[r, :].rearrange("p (h two t) -> p h two t", two=2, t=CH)[:, :, q, :]
                        nc.scalar.activation(KK[r, :, c * CH:(c + 1) * CH], y, ACT.Copy) \
                            .then_inc(*frees("act", ("y", c), ("y", c)))
                    if s == 0:
                        gate(NCH + gr)

            for p in range(NPAIR):
                act.wait_ge(*done("dve", "gn_d", p))
                nc.scalar.activation(gn[:, p, :], KK[:, p, :], ACT.Square).then_inc(*step("act", ("gn_sq", p)))
            gate(12)
            for p in range(NPAIR):
                act.wait_ge(*done("pe", "var", p))
                nc.scalar.activation(gn[:, p, :], psum(("var", p))[:, :], ACT.Sqrt, scale=1.0 / HD,
                    bias=stat[:, epsc + 1:epsc + 2]).then_inc(*frees("act", ("var", p), ("gn_sd", p)))
            for i in range(13, 16):
                gate(i)
            before(("bb", 0))
            for p in range(NPAIR):
                act.wait_ge(*done("dve", "y_a", p))
                nc.scalar.activation(ya_hi[:, p, :], KK[:, p, :], ACT.Copy).then_inc(*step("act", ("ya_hi", p)))
            for i in range(KD):
                before(("bb" if i % 4 == 0 else "ba", i - i % 4 if i % 4 < 2 else i - i % 4 + 2))
                if i % 4 == 0:
                    before(("ba", i))
                act.wait_ge(*done("dve", "merged", i))
                nc.scalar.activation(mg_hi[:, i, :].rearrange("p (a b) -> p a b", a=4), gate_at(i), ACT.Copy).then_inc(*step("act", ("mg_hi", i)))
            for h in range(2):
                for s in range(4):
                    before(("out", h, s))
                for m in range(NT):
                    act.wait_ge(*previous("act"))
                    squares_of("nb", xr, cbuf[:, 0, :, :], m, h)
            root("nb")
            gained_hi("nb", "g_ffn", KD, hT_hi)

            def g_split(i):
                act.wait_ge(*done("dve", "g", i))
                nc.scalar.activation(g_hi[:, i, :], cbuf[:, i % 2, 3, :], ACT.Copy).then_inc(*step("act", ("g_hi", i)))

            for i in range(NF):
                if i:
                    g_split(i - 1)
                for z, u in ((0, i), (1, NF + i)):
                    before(("up", u))
                    act.wait_ge(*done("pe", "up", u))
                    if i >= 2:
                        act.wait_ge(*done("dve", "g_lo", i - 2))
                    nc.scalar.activation(cbuf[:, i % 2, z, :], psum(("up", u))[:, :], ACT.Identity,
                        scale=par("conv_w0", u), bias=par("conv_b", u)).then_inc(*step("act", ("tap0", u)))
                act.wait_ge(*done("dve", "taps", i))
                nc.scalar.activation(cbuf[:, i % 2, 2, :], cbuf[:, i % 2, 0, :], ACT.Gelu_apprx_tanh) \
                    .then_inc(*step("act", ("gelu", i)))
            g_split(NF - 1)
            for h in range(2):
                for s in range(NF // 2):
                    before(("down", h, s))
                for m in range(NT):
                    act.wait_ge(*previous("act"))
                    squares_of("nc", xr, cbuf[:, 1, 2:4, :], m, h)
                if h == 0:
                    gained_hi("np", None, 2, pT_hi)
            root("nc")
            for h in range(2):
                before(("ple", h))
                for m in range(NT):
                    act.wait_ge(*done("pe", "pp", h, m))
                    nc.scalar.activation(pple[:, m, 512 * h:512 * h + 512], psum(("pp", h, m))[:, :], ACT.Copy) \
                        .then_inc(*frees("act", ("pp", h, m), ("pp", h, m)))
            gained_hi("nc", "g_ple", KD, hT_hi)
            for h in range(2):
                for s in range(4):
                    before(("pleg", h, s))
                for m in range(NT):
                    act.wait_ge(*done("pe", "pg", h, m))
                    if h:
                        act.wait_ge(*done("dve", "x_end", 0, m))
                    nc.scalar.activation(psig[:, m, :], psum(("pg", h, m))[:, :], ACT.Sigmoid) \
                        .then_inc(*frees("act", ("pg", h, m), ("pg", h, m)))
                for m in range(NT if h == 0 else 0):
                    act.wait_ge(*previous("act"))
                    squares_of("end", xr, junk, m, 0)
            for m in range(NT):
                act.wait_ge(*previous("act"))
                squares_of("end", xr, junk, m, 1)
                root("end", m, m + 1)

        @block.vector
        def _(dve):
            V = nc.vector


            def mean_square(tag, m0=0, m1=NT, last_m=None):
                dve.wait_ge(*done("act", "sq", tag, 1, m1 - 1 if last_m is None else last_m))
                V.tensor_tensor(stat[:, rms + m0:rms + m1], stat[:, ss + m0:ss + m1], stat[:, ss + NT + m0:ss + NT + m1],
                                ALU.add).then_inc(*step("dve", ("ms", tag, m0)))

            def gained_lo(tag, gain, tiles, dst_hi, dst, name):
                for k in range(tiles):
                    dve.wait_ge(*done("act", "hi", tag, k))
                    scale = par(gain, k) if gain else 1.0
                    V.scalar_tensor_tensor(dst[:, k, :], psum((tag, k))[:, :], scale,
                        dst_hi[:, k, :].bitcast(F32), ALU.mult, ALU.subtract) \
                        .then_inc(*frees("dve", (tag, k), (name, tag, k) if name == "hT_lo" else (name, k)))

            V.memset(stage[0:32, 0, :], 0.0).then_inc(*step("dve", ("stage",)))
            for m in (2, 3):
                for h in range(2):
                    dve.wait_ge(x_in[m], 16)
                    if m > 2 or h:
                        dve.wait_ge(*previous("dve"))
                    c, k = slice(512 * h, 512 * h + 512), ss + NT * h + m
                    V.tensor_tensor_reduce(out=Kk[:, m, :], in0=xs[:, m, c], in1=xs[:, m, c], scale=1.0, scalar=0.0,
                                           op0=ALU.mult, op1=ALU.add, accum_out=stat[:, k:k + 1]).then_inc(*step("dve"))
            dve.wait_ge(*previous("dve"))
            mean_square("na", last_m=1)
            dve.wait_ge(*done("act", "rms", "na", 0))
            V.reciprocal(stat[:, rstd:rstd + NT], stat[:, rms:rms + NT]).then_inc(*step("dve"))
            dve.wait_ge(*previous("dve"))
            for m in range(NT):
                V.tensor_scalar(xn_a[:, m, :], xs[:, m, :], stat[:, rstd + m:rstd + m + 1], None, ALU.mult) \
                    .then_inc(*step("dve", ("xn_a", m)))
            for b, rows in enumerate(PARAM_USED):
                dve.wait_ge(*done("pe", "par", b))
                V.tensor_copy(params[:, b * P:b * P + rows], psum(("par", b))[:, 0:rows]) \
                    .then_inc(*frees("dve", ("par", b), ("params",)))
            dve.wait_ge(*previous("dve"))
            c = PARAM_COL["rw_mu"]
            V.tensor_scalar(stat[:, omm:omm + 15], params[:, c:c + 15], -1.0, 1.0, ALU.mult, ALU.add).then_inc(*step("dve"))
            c = PARAM_COL["rw_k_a"]
            V.tensor_scalar(stat[:, omka:omka + 4], params[:, c:c + 4], -1.0, 1.0, ALU.mult, ALU.add) \
                .then_inc(*step("dve", ("derived",)))
            gained_lo("na", "g_mix", KD, hT_hi, hT_lo, "hT_lo")

            dsts = {12: lora_x[:, 0, :], 13: lora_x[:, 1, :], 14: lora_x[:, 2, :]}
            for i in range(4):
                dsts[i], dsts[4 + i], dsts[8 + i] = Rr[:, i, :], Kk[:, i, :], Vv[:, i, :]

            def shift(i):
                dve.wait_ge(*done("act", "own", i))
                rows = 32 if i == 14 else P
                d = dsts[i][0:rows, 1:SEQ]
                V.scalar_tensor_tensor(d, psum(("rw", i))[0:rows, 0:SEQ - 1], par("rw_mu", i, 0, rows), d,
                    ALU.mult, ALU.add).then_inc(*frees("dve", ("rw", i), ("shift", i)))

            for i in (12, 13, 14, 0, 1, 2, 3, 4, 5, 6, 7, 8, 9, 10, 11):
                shift(i)

            def pre_a(p):
                q = p % 2
                dve.wait_ge(*done("act", "lg", NPAIR - 1))
                if p == 0:
                    dve.wait_ge(*done("pe", "lg", NPAIR - 1))
                if p >= 2:
                    dve.wait_ge(*done("act", "E", p - 2))
                V.tensor_tensor_scan(Lt[:, q, :], reset, Bo[:, p, :], 0.0, ALU.mult, ALU.add) \
                    .then_inc(*step("dve", ("L", p)))
                V.tensor_scalar(KK[:, p, :], Kk[:, p, :], par("rw_k_k", p), None, ALU.mult) \
                    .then_inc(*step("dve", ("kkr", p)))

            def pre_b(p):
                sc, kk, k, a, r = Sc[:, p % 2, :], KK[:, p, :], Kk[:, p, :], Aa[:, p, :], Rr[:, p, :]
                dve.wait_ge(*done("act", "kn", p))
                V.tensor_scalar(sc, sc, 1e-12, None, ALU.max).then_inc(*step("dve"))
                dve.wait_ge(*previous("dve"))
                V.reciprocal(sc, sc).then_inc(*step("dve"))
                dve.wait_ge(*previous("dve"))
                V.tensor_tensor(kk, kk, sc, ALU.mult).then_inc(*step("dve"))
                dve.wait_ge(*previous("dve"))
                V.tensor_scalar(sc, a, par("rw_k_a", p), stat[:, omka + p:omka + p + 1], ALU.mult, ALU.add) \
                    .then_inc(*step("dve"))
                dve.wait_ge(*previous("dve"))
                V.tensor_tensor(k, k, sc, ALU.mult).then_inc(*step("dve"))
                V.tensor_tensor(a, kk, a, ALU.mult).then_inc(*step("dve"))
                dve.wait_ge(*previous("dve"))
                V.scalar_tensor_tensor(sc, r, par("rw_r_k", p), k, ALU.mult, ALU.mult).then_inc(*step("dve", ("rk", p)))

            def pre_c(p):
                q = p % 2
                kk, k, a, r = KK[:, p, :], Kk[:, p, :], Aa[:, p, :], Rr[:, p, :]
                dve.wait_ge(*done("pe", "bn", p))
                V.tensor_tensor(Bo[:, p, :], psum(("bn", p))[:, :], Vv[:, p, :], ALU.mult).then_inc(*frees("dve", ("bn", p)))
                dve.wait_ge(*done("act", "E", p))
                V.tensor_tensor(a, a, Ei[:, q, :], ALU.mult).then_inc(*step("dve"))
                V.tensor_tensor(k, k, Ei[:, q, :], ALU.mult).then_inc(*step("dve"))
                V.tensor_tensor(r, r, Et[:, q, :], ALU.mult).then_inc(*step("dve"))
                e3 = Et[:, q, :].rearrange("p (c t) -> p c t", t=CH)
                k3 = kk.rearrange("p (c t) -> p c t", t=CH)
                V.tensor_copy(stat[:, ec + 8 * p:ec + 8 * p + 8].unsqueeze(2), e3[:, :, CH - 1:CH]).then_inc(*step("dve"))
                V.scalar_tensor_tensor(k3[:, :, 1:CH], k3[:, :, 1:CH], -1.0, e3[:, :, 0:CH - 1], ALU.mult, ALU.mult) \
                    .then_inc(*step("dve"))
                V.tensor_scalar(k3[:, :, 0:1], k3[:, :, 0:1], -1.0, None, ALU.mult).then_inc(*step("dve", ("preC", p)))

            pre_a(0)
            for p in range(NPAIR):
                if p + 1 < NPAIR:
                    pre_a(p + 1)
                pre_b(p)
                if p:
                    pre_c(p - 1)
            pre_c(NPAIR - 1)

            def masked(it):
                j, qt = it // NT, it % NT
                off, base_ = 0, 0
                if it >= 3:
                    dve.wait_ge(*done("pe", "tall", it - 3))
                for g, width in enumerate((2 * P, SEQ, SEQ)):
                    k0 = max(0, qt - 1) if g == 0 else 0
                    n = (qt + 1 - k0) * P
                    dve.wait_ge(*done("pe", "s", it, g))
                    V.scalar_tensor_tensor(Sx[:, it % 3, off:off + n], dist[:, base_ + width - n:base_ + width],
                        -SLOPES[ATT_HG * g + j], psum(("s", it, g))[:, 0:n],
                        ALU.mult, ALU.add).then_inc(*frees("dve", ("s", it, g)))
                    off += n
                    base_ += width
                dve.wait_ge(*previous("dve"))
                nm = stat[:, negmax + it:negmax + it + 1]
                V.reduce_max(nm, Sx[:, it % 3, 0:off], AX_X).then_inc(*step("dve"))
                dve.wait_ge(*previous("dve"))
                V.tensor_scalar(nm, nm, -1.0, None, ALU.mult).then_inc(*step("dve", ("max", it)))

            def normalise(it):
                n = len(att_tiles(it // NT, it % NT)) * P
                dve.wait_ge(*done("act", "exp", it))
                rd = stat[:, rden + it:rden + it + 1]
                V.reciprocal(rd, stat[:, den + it:den + it + 1]).then_inc(*step("dve"))
                dve.wait_ge(*previous("dve"))
                V.tensor_scalar(Sx[:, it % 3, 0:n], Sx[:, it % 3, 0:n], rd, None, ALU.mult).then_inc(*step("dve", ("P", it)))

            def yb_rest(it):
                j, qt = it // NT, it % NT
                r, t = slice(HD * (j % 2), HD * (j % 2) + HD), slice(qt * P, (qt + 1) * P)
                dve.wait_ge(*done("act", "yb_hi", it))
                V.tensor_tensor(yb_lo[r, j // 2, t], psum(("o", it))[r, 0:P], yb_hi[r, j // 2, t].bitcast(F32),
                    ALU.subtract).then_inc(*frees("dve", ("o", it), ("yb_lo", it)))

            dve.wait_ge(dist_in, 16)
            masked(0)
            for it in range(16):
                if it + 1 < 16:
                    masked(it + 1)
                normalise(it)
                if it:
                    yb_rest(it - 1)
            yb_rest(15)

            def fill(gr):
                if gr == 0:
                    dve.wait_ge(*done("pool", "cleared"))
                else:
                    for s in range(2):
                        dve.wait_ge(*done("pe", "Bt", 2 * (gr - 1) + s))
                        dve.wait_ge(*done("pe", "Rb", 2 * (gr - 1) + s))
                    if gr >= 2:
                        dve.wait_ge(*done("pe", "y", 2 * gr - 3))
                fill_blocks("dve", nc.vector.tensor_copy, gr, ((CM["Bf"], 0, Aa), (At, 2 * (gr % 2), KK)))

            def times_mask(dst, label, mask, *marks):
                dve.wait_ge(*done("pe", *label))
                V.tensor_tensor(dst.rearrange("p (h t) -> p h t", t=P),
                    psum(label)[:, :].rearrange("p (h t) -> p h t", t=P), cst4(mask), ALU.mult) \
                    .then_inc(*frees("dve", label, *marks))

            fill(0)
            for gr in range(NCH // 2):
                for s in range(2):
                    c = 2 * gr + s
                    X, A = CM["Xx"][:, s, :], CM["Am"][:, s, :]
                    if gr:
                        dve.wait_ge(*done("pe", "y", c - 2))
                    times_mask(X, ("AT", c), "off1_st")
                    times_mask(A, ("A", c), "strict_ts")
                    dve.wait_ge(*previous("dve"))
                    x3 = X.rearrange("p (h t) -> p h t", t=P)
                    V.tensor_tensor(x3, x3, cst4("ident"), ALU.add).then_inc(*step("dve", ("X", c, 0)))
                for lv in range(5):
                    for s in range(2):
                        c = 2 * gr + s
                        times_mask(Wp[:, s, :], ("W", c, lv), f"off{2 << lv}", ("Wp", c, lv))
                    for kind, mask in {0: (("Ak", "strict_st"),), 3: (("Rb", "incl_st"),), 4: (("Rk", "incl_st"),)}.get(lv, ()):
                        for s in range(2):
                            c = 2 * gr + s
                            times_mask(CM[kind][:, s, :], (kind, c), mask, (kind, c))
                    for s in range(2):
                        c = 2 * gr + s
                        X = CM["Xx"][:, s, :]
                        dve.wait_ge(*done("pe", "XW", c, lv))
                        V.tensor_tensor(X, psum(("XW", c, lv))[:, :], X, ALU.add) \
                            .then_inc(*frees("dve", ("XW", c, lv), ("X", c, lv + 1)))
                if gr + 1 < NCH // 2:
                    fill(gr + 1)
                for s in range(2):
                    c = 2 * gr + s
                    if c + 1 == NCH:
                        break
                    dve.wait_ge(*done("pe", "z", c))
                    if c:
                        dve.wait_ge(*done("pe", "y", c - 1))
                    Zn = Zs[:, (c + 1) % 2, :]
                    V.tensor_tensor(Zn, psum(("z", c))[:, :], Zs[:, c % 2, :], ALU.add).then_inc(*frees("dve", ("z", c)))
                    dve.wait_ge(*previous("dve"))
                    z3 = Zn.rearrange("p (h t) -> p h t", t=P)
                    e = stat[:, ec:ec + 32].rearrange("p (h c) -> p h c", c=NCH)[:, :, c:c + 1].broadcast_to([P, NPAIR, P])
                    V.tensor_tensor(z3, z3, e, ALU.mult).then_inc(*step("dve", ("Z", c + 1)))

            for p in range(NPAIR):
                dve.wait_ge(*done("pe", "mu", p))
                V.scalar_tensor_tensor(KK[:, p, :], psum(("mu", p))[:, :], -1.0 / HD, KK[:, p, :], ALU.mult, ALU.add) \
                    .then_inc(*frees("dve", ("mu", p), ("gn_d", p)))
            for p in range(NPAIR):
                y, sd = KK[:, p, :], gn[:, p, :]
                dve.wait_ge(*done("act", "gn_sd", p))
                V.reciprocal(sd, sd).then_inc(*step("dve"))
                dve.wait_ge(*previous("dve"))
                V.tensor_tensor(y, y, sd, ALU.mult).then_inc(*step("dve"))
                dve.wait_ge(*previous("dve"))
                V.tensor_scalar(y, y, par("rw_ln_g", p), par("rw_ln_b", p), ALU.mult, ALU.add).then_inc(*step("dve"))
                dve.wait_ge(*previous("dve"))
                V.tensor_tensor(y, y, Bo[:, p, :], ALU.add).then_inc(*step("dve"))
                dve.wait_ge(*previous("dve"))
                V.tensor_tensor(y, y, Gg[:, p, :], ALU.mult).then_inc(*step("dve", ("y_a", p)))
            for p in range(NPAIR):
                dve.wait_ge(*done("act", "ya_hi", p))
                V.tensor_tensor(ya_lo[:, p, :], KK[:, p, :], ya_hi[:, p, :].bitcast(F32), ALU.subtract) \
                    .then_inc(*step("dve", ("ya_lo", p)))

            def tile4(t):
                return t.rearrange("p (a b) -> p a b", a=4)

            def merged_rest(i):
                dve.wait_ge(*done("act", "mg_hi", i))
                V.tensor_tensor(tile4(mg_lo[:, i, :]), gate_at(i), tile4(mg_hi[:, i, :].bitcast(F32)), ALU.subtract) \
                    .then_inc(*step("dve", ("mg_lo", i)))

            for i in range(KD):
                if i % 4 == 0:
                    for z in range(i, i + 4):
                        dve.wait_ge(*done("pe", "pb", z))
                        dve.wait_ge(*done("act", "gate", 8 + z))
                        V.tensor_tensor(gate_at(8 + z), tile4(psum(("pb", z))[:, :]), gate_at(8 + z), ALU.mult) \
                            .then_inc(*frees("dve", ("pb", z)))
                dve.wait_ge(*done("pe", "pa", i))
                dve.wait_ge(*done("act", "gate", i))
                V.tensor_tensor(gate_at(i), tile4(psum(("pa", i))[:, :]), gate_at(i), ALU.mult).then_inc(*frees("dve", ("pa", i)))
                dve.wait_ge(*previous("dve"))
                V.tensor_tensor(gate_at(i), gate_at(i), gate_at(8 + i), ALU.add).then_inc(*step("dve", ("merged", i)))
                if i:
                    merged_rest(i - 1)
            merged_rest(KD - 1)

            def residual(tag, h, m, *marks):
                dve.wait_ge(*done("pe", tag, h, m))
                x = xr[:, m, 512 * h:512 * h + 512]
                V.tensor_tensor(x, psum((tag, h, m))[:, :], x, ALU.add).then_inc(*frees("dve", (tag, h, m), *marks))

            def rms_scaled(tag, dst, name):
                mean_square(tag)
                dve.wait_ge(*done("act", "rms", tag, 0))
                V.reciprocal(stat[:, rstd:rstd + NT], stat[:, rms:rms + NT]).then_inc(*step("dve"))
                dve.wait_ge(*previous("dve"))
                for m in range(NT):
                    V.tensor_scalar(dst[:, m, :], xr[:, m, :], stat[:, rstd + m:rstd + m + 1], None, ALU.mult) \
                        .then_inc(*step("dve", (name, m)))

            dve.wait_ge(xr_in, 16)
            for h in range(2):
                for m in range(NT):
                    residual("op", h, m, ("x_nb", h, m))
            rms_scaled("nb", xn_b, "xn_b")
            gained_lo("nb", "g_ffn", KD, hT_hi, hT_lo, "hT_lo")

            def g_rest(i):
                dve.wait_ge(*done("act", "g_hi", i))
                V.tensor_tensor(g_lo[:, i, :], cbuf[:, i % 2, 3, :], g_hi[:, i, :].bitcast(F32), ALU.subtract) \
                    .then_inc(*step("dve", ("g_lo", i)))

            for i in range(NF):
                if i:
                    g_rest(i - 1)
                for z, u in ((0, i), (1, NF + i)):
                    dve.wait_ge(*done("act", "tap0", u))
                    cv, ps = cbuf[:, i % 2, z, :], psum(("up", u))
                    V.scalar_tensor_tensor(cv[:, 1:], ps[:, 0:SEQ - 1], par("conv_w1", u), cv[:, 1:], ALU.mult, ALU.add) \
                        .then_inc(*step("dve"))
                    dve.wait_ge(*previous("dve"))
                    V.scalar_tensor_tensor(cv[:, 2:], ps[:, 0:SEQ - 2], par("conv_w2", u), cv[:, 2:], ALU.mult, ALU.add) \
                        .then_inc(*frees("dve", ("up", u), *([("taps", i)] if z == 0 else [])))
                dve.wait_ge(*done("act", "gelu", i))
                dve.wait_ge(*previous("dve"))
                V.tensor_tensor(cbuf[:, i % 2, 3, :], cbuf[:, i % 2, 2, :], cbuf[:, i % 2, 1, :], ALU.mult) \
                    .then_inc(*step("dve", ("g", i)))
            g_rest(NF - 1)
            for h in range(2):
                for m in range(NT):
                    residual("dn", h, m, ("x_nc", h, m))
                if h == 0:
                    gained_lo("np", None, 2, pT_hi, pT_lo, "pT_lo")
            rms_scaled("nc", xn_c, "xn_c")
            gained_lo("nc", "g_ple", KD, hT_hi, hT_lo, "hT_lo")
            for h in range(2):
                for m in range(NT):
                    dve.wait_ge(*done("act", "pg", h, m))
                    c = slice(512 * h, 512 * h + 512)
                    V.tensor_tensor(psig[:, m, :], psig[:, m, :], pple[:, m, c], ALU.mult).then_inc(*step("dve"))
                    dve.wait_ge(*previous("dve"))
                    V.tensor_tensor(xr[:, m, c], xr[:, m, c], psig[:, m, :], ALU.add) \
                        .then_inc(*step("dve", ("x_end", h, m)))
            dve.wait_ge(gf_in, 16)
            for m in range(NT):
                mean_square("end", m, m + 1)
                dve.wait_ge(*done("act", "rms", "end", m))
                V.reciprocal(stat[:, rstd + m:rstd + m + 1], stat[:, rms + m:rms + m + 1]).then_inc(*step("dve"))
                dve.wait_ge(*previous("dve"))
                V.scalar_tensor_tensor(xr[:, m, :], xr[:, m, :], stat[:, rstd + m:rstd + m + 1], gfin[:, :],
                    ALU.mult, ALU.mult).then_inc(*step("dve", ("final", m)))

    return {"steps": steps, "readers": readers, "turn": turn}


def att_tiles(j, qt):
    return [(ATT_HG * g + j, kt) for g in range(3) for kt in range(max(0, qt - 1) if g == 0 else 0, qt + 1)]


_INS = ["x", "p", "g_mix", "w_in", "rw_mu", "rw_w0", "rw_w_up", "rw_a0", "rw_a_up", "rw_g_up", "rw_k_k", "rw_k_a",
        "rw_r_k", "rw_ln_g", "rw_ln_b", "w_branch_a", "w_branch_b", "w_gate", "b_gate", "w_out", "g_ffn", "w_up",
        "conv_w", "conv_b", "w_down", "g_ple", "w_ple_gate", "w_ple", "g_final"]


def kernel(**inputs):
    import numpy as _np
    import concourse.bacc as _bacc
    from concourse import mybir as _mybir
    from concourse.bass_utils import run_bass_kernel_spmd as _run

    arrays = {name: _np.ascontiguousarray(inputs[name]) for name in _INS}
    arrays["consts"], arrays["dist"] = shape_constants()

    known = None
    for _ in range(2):
        nc = _bacc.Bacc("TRN2", target_bir_lowering=False, num_devices=1)
        ins = {name: nc.dram_tensor(f"in_{name}_dram", a.shape, _mybir.dt.from_np(a.dtype), kind="ExternalInput").ap()
               for name, a in arrays.items()}
        out = nc.dram_tensor("out_0_dram", (1, SEQ, DM), _mybir.dt.float32, kind="ExternalOutput").ap()
        known = build(nc, ins, out, known)
    r = _run(nc, [{f"in_{name}_dram": a for name, a in arrays.items()}], core_ids=[0])
    return r.results[0]["out_0_dram"]
```

```python
from contextlib import ExitStack

import numpy as np

import concourse.bass as bass
from concourse import mybir

P = 128
F32 = mybir.dt.float32
F32R = mybir.dt.float32r
ALU = mybir.AluOpType
ACT = mybir.ActivationFunctionType
AX_X = mybir.AxisListType.X

SEQ, DM, PLE = 512, 1024, 256
NH, HD = 8, 64
RW = NH * HD
ATT_H, ATT_HG = 12, 4
ATT_W = ATT_H * HD
DFF = 3 * DM
NT = SEQ // P
KD = DM // P
NPAIR = RW // P
CH = 64
NCH = SEQ // CH
NF = DFF // P
NORM_EPS, LN_EPS = 1e-6, 64e-5
DECAY = float(np.exp(-0.5))
UNIT = 1024
RAW_SLOTS, W_SLOTS, BANKS = 3, 2, 8
GROUPS = ((128, 1), (512, 4), (2048, 16))
SLOPES = [2.0 ** (-8.0 * (h + 1) / ATT_H) for h in range(ATT_H)]
FAR = 1e30

PARAM_ROWS = [("rw_mu", 15), ("rw_w0", 4), ("rw_a0", 4), ("rw_k_k", 4), ("rw_k_a", 4), ("rw_r_k", 4),
              ("rw_ln_g", 4), ("rw_ln_b", 4), ("g_mix", 8), ("g_ffn", 8), ("g_ple", 8), ("b_gate", 16)]
PARAM_COL, _n = {}, 0
for _name, _rows in PARAM_ROWS:
    PARAM_COL[_name] = _n
    _n += _rows
PARAM_USED = [_n, 96, 96]
PARAM_COL["conv_w0"], PARAM_COL["conv_w1"] = P, P + 48
PARAM_COL["conv_w2"], PARAM_COL["conv_b"] = 2 * P, 2 * P + 48

CONST_NAMES = ["ident", "heads", "strict_st", "incl_st", "strict_ts"]
STACKED = ["ident64", "off1", "off2", "off4", "off8", "off16", "off32"]


def shape_constants():
    i = np.arange(P)
    same = (i[:, None] // CH) == (i[None, :] // CH)
    r, c = i[:, None] % CH, i[None, :] % CH

    def off(b):
        return ((r // (2 * b) == c // (2 * b)) & (r % (2 * b) < b) & (c % (2 * b) >= b))[:, 0:CH]

    parts = {"ident": r * 0 + (i[:, None] == i[None, :]), "heads": same, "strict_st": same & (r < c),
             "incl_st": same & (r <= c), "strict_ts": same & (r > c),
             "ident64": (r == c)[:, 0:CH]}
    for b in (1, 2, 4, 8, 16, 32):
        parts[f"off{b}"] = off(b)
    reset = np.broadcast_to((np.arange(SEQ) % CH != 0)[None, :], (P, SEQ))
    consts = np.concatenate([np.asarray(parts[n], np.float32) for n in CONST_NAMES + STACKED] + [reset.astype(np.float32)], 1)
    dist = []
    for (window, dilation), width in zip(GROUPS, (2 * P, SEQ, SEQ)):
        d = i[:, None] + (width - P) - np.arange(width)[None, :]
        ok = (d >= 0) & (d <= window) & (d % dilation == 0)
        dist.append(np.where(ok, d, FAR).astype(np.float32))
    return np.ascontiguousarray(consts), np.ascontiguousarray(np.concatenate(dist, 1))


SIGNALS = [
    "act_Bt", "act_E", "act_Kt", "act_U", "act_U1", "act_XT", "act_chain", "act_exp", "act_fill", "act_g_hi",
    "act_gate", "act_gelu", "act_gn_sd", "act_hi", "act_kk_sq", "act_kn", "act_la", "act_lg", "act_lora_act",
    "act_lw", "act_mg_hi", "act_own", "act_pg", "act_pp", "act_psum_read", "act_pt", "act_qk", "act_rms", "act_sq",
    "act_tap0", "act_vt0", "act_vt1", "act_yT", "act_ya_hi", "act_yb_hi", "dve_L", "dve_P", "dve_Rb", "dve_Rk",
    "dve_Wp", "dve_X", "dve_Z", "dve_chain", "dve_derived", "dve_fill", "dve_final", "dve_g", "dve_g_lo", "dve_gn_d",
    "dve_gn_var", "dve_hT_lo", "dve_kkr", "dve_max", "dve_merged", "dve_mg_lo", "dve_ms", "dve_pT_lo", "dve_params",
    "dve_preC", "dve_psum_read", "dve_rk", "dve_shift", "dve_stage", "dve_taps", "dve_x_end", "dve_x_nb", "dve_x_nc",
    "dve_xn_a", "dve_xn_b", "dve_xn_c", "dve_y_a", "dve_ya_lo", "dve_yb_lo", "dve_yn", "pe_A", "pe_BRA", "pe_Bt",
    "pe_KRA", "pe_Kt", "pe_Vt", "pe_W", "pe_XT", "pe_XW", "pe_bn", "pe_chain", "pe_dn", "pe_kn", "pe_la", "pe_lg",
    "pe_lw", "pe_na", "pe_nb", "pe_nc", "pe_np", "pe_o", "pe_op", "pe_pa", "pe_par", "pe_pb", "pe_pg", "pe_pp",
    "pe_s", "pe_t", "pe_u1", "pe_u2", "pe_unit", "pe_vt0", "pe_vt1", "pe_y", "pe_yT", "pe_z", "pool_chain",
    "pool_cleared", "pool_cleared_Bt", "pool_cleared_Kt", "pool_cleared_XT", "pool_cleared_second", "pool_eps",
    "pool_lo",
]


GATE_ORDER = list(range(16))
PARTS_AT = [(1, 1, 1, 1, 1), (1, 1, 1, 1, 1), (2, 2), (3, 3), (3, 1)]


def weight_units():
    u = []
    for i in (12, 13, 14, 0, 1, 2, 3, 4, 5, 6, 7, 8, 9, 10, 11):
        u.append((("rw", i), "w_in", 0, 8, P * i, P))
    base = 1824
    for i in range(12):
        u.append((("qk", i), "w_in", 0, 8, base + P * i, P))
    for s in range(4):
        u.append((("v0", s), "w_in", 2 * P * s, 2, base + 2 * ATT_W, 512))
    for s in range(2):
        u.append((("v1", s), "w_in", 4 * P * s, 4, base + 2 * ATT_W + 512, 256))
    for i in GATE_ORDER:
        u.append((("gate", i), "w_gate", 0, 8, P * i, P))
    for i in range(0, 8, 4):
        u.append((("bb", i), "w_branch_b", 0, 2, P * i, 512))
        u.append((("ba", i), "w_branch_a", 0, 4, P * i, 256))
        u.append((("ba", i + 2), "w_branch_a", 0, 4, P * (i + 2), 256))
    for h in range(2):
        for s in range(4):
            u.append((("out", h, s), "w_out", 2 * P * s, 2, 512 * h, 512))
    for i in range(NF):
        u.append((("up", i), "w_up", 0, 8, P * i, P))
        u.append((("up", NF + i), "w_up", 0, 8, DFF + P * i, P))
    for h in range(2):
        for s in range(NF // 2):
            u.append((("down", h, s), "w_down", 2 * P * s, 2, 512 * h, 512))
    for h in range(2):
        u.append((("ple", h), "w_ple", 0, 2, 512 * h, 512))
    for h in range(2):
        for s in range(4):
            u.append((("pleg", h, s), "w_ple_gate", 2 * P * s, 2, 512 * h, 512))
    return u


UNITS = weight_units()
UIDX = {x[0]: n for n, x in enumerate(UNITS)}


def build(nc, ins, out, known):
    W = {}
    for name in ("w_in", "w_gate", "w_branch_a", "w_branch_b", "w_out", "w_up", "w_down", "w_ple_gate", "w_ple"):
        W[name] = ins[name].rearrange("l k n -> (l k) n")
    x_d = ins["x"].rearrange("b (m p) d -> p (b m) d", p=P)
    out_d = out.rearrange("b (m p) d -> p (b m) d", p=P)
    p_d = ins["p"].rearrange("l b (m p) d -> p (l b m) d", p=P)

    with ExitStack() as ctx:
        def sem(name):
            return ctx.enter_context(nc.semaphore(name))

        base = -(-nc.sbuf_base // 64) * 64
        top = [base]

        def sb_at(name, shape, dt, offset):
            return nc.alloc_sbuf_tensor_at(name, shape, dt, offset=offset)

        def sb(name, words, shape=None, dt=F32):
            t = sb_at(name, shape or [P, words], dt, top[0])
            top[0] += 4 * words
            return t

        consts = sb("consts", len(CONST_NAMES) * P + len(STACKED) * CH + SEQ)
        gn_sq = sb("gn_sq", 256, [P, NPAIR, CH])
        params = sb("params", 3 * P)
        stat = sb("stat", 256)
        hT_hi = sb("hT_hi", 4096, [P, KD, SEQ], F32R)
        hT_lo = sb("hT_lo", 4096, [P, KD, SEQ], F32R)
        raw = sb("raw", RAW_SLOTS * UNIT, [P, RAW_SLOTS, UNIT])
        w_hi = sb("w_hi", W_SLOTS * UNIT, [P, W_SLOTS, UNIT], F32R)
        w_lo = sb("w_lo", W_SLOTS * UNIT, [P, W_SLOTS, UNIT], F32R)
        yb_hi = sb("yb_hi", 1024, [P, 2, SEQ], F32R)
        yb_lo = sb("yb_lo", 1024, [P, 2, SEQ], F32R)
        R0 = top[0]
        KB = 1024
        assert R0 + 128 * KB <= nc.sbuf_usable_end, (R0, nc.sbuf_usable_end)

        def at(name, kb, shape, dt=F32):
            return sb_at(name, shape, dt, R0 + int(kb * KB))

        xs = at("xs", 56, [P, NT, DM])
        xn_a = at("xn_a", 72, [P, NT, DM])
        stage = at("stage", 88, [P, 3, P])
        RA = at("RA", 0, [P, 2, NPAIR, SEQ])
        Rr, KK = RA[:, 0, :, :], RA[:, 1, :, :]
        Kk, Aa, Vv, Gg, Bo = [at(n, 16 + 8 * i, [P, NPAIR, SEQ]) for i, n in enumerate(("Kk", "Aa", "Vv", "Gg", "Bo"))]
        qk = at("qk", 56, [P, 12, SEQ])
        vtok = at("vtok", 80, [P, NT, ATT_W])
        dist = at("dist", 92, [P, 2 * P + 2 * SEQ])
        Sx = at("Sx", 97, [P, 3, 1280])
        PT = at("PT", 112, [P, 2, 10, P])
        def full(name, kb):
            return at(name, kb, [P, 2, 512])

        def stacked(name, kb):
            return at(name, kb, [P, 2, NPAIR, CH])

        Bf, Kf = [full("Bf0", 56), full("Bf1", 68)], [full("Kf0", 60), full("Kf1", 72)]
        At, Rt = [full("At0", 64), full("At1", 76)], [full("Rt0", 122), full("Rt1", 80)]
        XT, Am, Ak, Rb, Rk, Bt, Kt = [full(n, 84 + 4 * i) for i, n in enumerate(("XT", "Am", "Ak", "Rb", "Rk", "Bt", "Kt"))]
        Xx = at("Xx", 112, [P, NPAIR, 2, CH])
        Wp, Vt, U1, Uu = [stacked(n, 114 + 2 * i) for i, n in enumerate(("Wp", "Vt", "U1", "Uu"))]
        Zs = stacked("Zs", 126)
        lora_x = at("lora_x", 112, [P, 3, SEQ])
        lora_w = at("lora_w", 118, [P, 3, RW])
        Lt, Et, Ei, Sc = [at(n, 112 + 4 * i, [P, 2, SEQ]) for i, n in enumerate(("Lt", "Et", "Ei", "Sc"))]
        ya_hi = at("ya_hi", 88, [P, NPAIR, SEQ], F32R)
        ya_lo = at("ya_lo", 96, [P, NPAIR, SEQ], F32R)
        mg_hi = at("mg_hi", 56, [P, KD, SEQ], F32R)
        mg_lo = at("mg_lo", 72, [P, KD, SEQ], F32R)
        yT = at("yT", 104, [P, NPAIR, SEQ])
        xr = at("xr", 112, [P, NT, DM])
        xn_b = at("xn_b", 32, [P, NT, DM])
        g_hi = at("g_hi", 0, [P, NF, SEQ], F32R)
        g_lo = at("g_lo", 48, [P, NF, SEQ], F32R)
        cbuf = at("cbuf", 96, [P, 2, 4, SEQ])
        p_raw = at("p_raw", 96, [P, NT, PLE])
        pT_hi = at("pT_hi", 100, [P, 2, SEQ], F32R)
        pT_lo = at("pT_lo", 104, [P, 2, SEQ], F32R)
        xn_c = at("xn_c", 0, [P, NT, DM])
        psig = at("psig", 16, [P, NT, 512])
        gfin = at("gfin", 24, [P, DM])
        pple = at("pple", 28, [P, NT, DM])
        junk = at("junk", 44, [P, 2, 512])

        def cst(n):
            k = CONST_NAMES.index(n)
            return consts[:, k * P:(k + 1) * P]

        def cst4(n):
            k = len(CONST_NAMES) * P + STACKED.index(n) * CH
            return consts[:, k:k + CH].unsqueeze(1).broadcast_to([P, NPAIR, CH])

        def cst4_full(n):
            return cst(n).rearrange("p (two t) -> p two t", t=CH).unsqueeze(1).broadcast_to([P, NPAIR, 2, CH])

        reset = consts[:, len(CONST_NAMES) * P + len(STACKED) * CH:len(CONST_NAMES) * P + len(STACKED) * CH + SEQ]
        ident = cst("ident")

        def gate_at(i):
            n = GATE_ORDER.index(i)
            if n >= 12:
                return Rr[:, n - 12, :].rearrange("p (a b) -> p a b", a=4)
            return (Kk, Aa, Vv)[n % 3][:, :, (n // 3) * P:(n // 3 + 1) * P]

        def qk_at(i):
            return qk[:, (i % 2) * 6 + i // 2, :]

        def par(name, i, lo=0, hi=P):
            c = PARAM_COL[name] + i
            return params[lo:hi, c:c + 1]

        omm, omka, ec, ss, rms, rstd = 0, 16, 32, 96, 104, 108
        negmax, den, rden, epsc, gn_mu, gn_var = 112, 128, 144, 160, 164, 168

        bank = [ctx.enter_context(nc.psum_tensor(f"bank{i}", [P, 512], F32)) for i in range(BANKS)]

        x_in = [sem(f"x_in{m}") for m in range(NT)]
        par_in, cst_in, dist_in, lora_in, xr_in, p_in, gf_in, out_done = [
            sem(n) for n in ("par_in", "cst_in", "dist_in", "lora_in", "xr_in", "p_in", "gf_in", "out_done")]
        landed = [sem(f"landed{i}") for i in range(RAW_SLOTS)]
        signal = {name: sem(name) for name in SIGNALS}

        count = {name: 0 for name in signal}
        latest, steps, readers, turn = {}, {}, {}, {}
        earlier = known or {"steps": {}, "readers": {}, "turn": {}}

        def step(who, *labels):
            name = f"{who}_{labels[0][0]}" if labels else f"{who}_chain"
            count[name] += 1
            latest[who] = (name, count[name])
            for label in labels:
                steps[(who,) + label] = latest[who]
            return signal[name], 1

        def frees(who, bank_label, *labels):
            got = step(who, *(labels or (("psum_read",),)))
            readers[bank_label] = latest[who]
            return got

        def done(who, *label):
            name, n = earlier["steps"].get((who,) + label, (f"{who}_chain", 1))
            return signal[name], n

        def previous(who):
            name, n = latest[who]
            return signal[name], n

        def psum(label):
            return bank[earlier["turn"].get(label, 0)]

        RING, CHUNK_RING, GATE_RING = range(BANKS), range(BANKS - 2), range(BANKS - 2, BANKS)
        ring, given, holder = [RING], {RING: 0, CHUNK_RING: 0, GATE_RING: 0}, {}
        block = ctx.enter_context(nc.Block())
        n_par = len(PARAM_ROWS) + 1 + 4

        def blocks(t, q):
            return t[CH * q:CH * q + CH, :, :].rearrange("p s (h two t) -> p s h two t", two=2, t=CH)[:, :, :, q, :]

        def fill_blocks(who, copy, gr, parts):
            for n, (dst, src) in enumerate(parts):
                for q in range(2):
                    r = slice(CH * q, CH * q + CH)
                    last = (("fill", gr),) if n == len(parts) - 1 and q == 1 else ()
                    copy(blocks(dst, q), src[r, :, 2 * gr * CH:(2 * gr + 2) * CH].rearrange("p h (s t) -> p s h t", s=2)) \
                        .then_inc(*step(who, *last))

        def chunk(t, c):
            return t[:, :, c * CH:(c + 1) * CH]

        @block.sync
        def _(sp):
            for m in range(NT):
                sp.dma_start(xs[:, m, :], x_d[:, m, :]).then_inc(x_in[m], 16)
            sp.wait_ge(*done("dve", "stage"))
            for name, rows in PARAM_ROWS:
                c = PARAM_COL[name]
                src = ins[name].rearrange("l a b -> l (a b)") if name == "rw_r_k" else ins[name]
                full = src.shape[1] // P
                sp.dma_start(stage[c:c + full, 0, :], src[0, 0:full * P].rearrange("(r n) -> r n", n=P)).then_inc(par_in, 16)
                if full < rows:
                    sp.dma_start(stage[c + full:c + rows, 0, 0:src.shape[1] - full * P],
                                 src[:, full * P:]).then_inc(par_in, 16)
            for b, r, src in ((1, 0, ins["conv_w"][0, 0]), (1, 48, ins["conv_w"][0, 1]),
                              (2, 0, ins["conv_w"][0, 2]), (2, 48, ins["conv_b"][0])):
                sp.dma_start(stage[r:r + 48, b, :], src.rearrange("(r n) -> r n", n=P)).then_inc(par_in, 16)
            for n, (label, name, r0, t, c0, w) in enumerate(UNITS):
                if n >= RAW_SLOTS:
                    sp.wait_ge(*done("pool", "lo", n - RAW_SLOTS))
                src = W[name][r0:r0 + t * P, c0:c0 + w].rearrange("(t p) n -> p t n", p=P)
                dst = raw[:, n % RAW_SLOTS, :].rearrange("p (t n) -> p t n", t=t)
                sp.dma_start(dst, src).then_inc(landed[n % RAW_SLOTS], 16)
                if label == ("out", 0, 1):
                    sp.wait_ge(*done("act", "ya_hi", NPAIR - 1))
                    sp.dma_start(xr[:, :, :], x_d).then_inc(xr_in, 16)
                if label == ("down", 0, 4):
                    sp.wait_ge(*done("dve", "g_lo", NF - 1))
                    sp.dma_start(p_raw[:, :, :], p_d).then_inc(p_in, 16)
                if label == ("pleg", 0, 3):
                    sp.wait_ge(*done("pe", "dn", 1, NT - 1))
                    sp.dma_start(gfin[:, :], ins["g_final"].partition_broadcast(P)).then_inc(gf_in, 16)
            for m in range(NT):
                sp.wait_ge(*done("dve", "final", m))
                sp.dma_start(out_d[:, m, :], xr[:, m, :]).then_inc(out_done, 16)
            sp.wait_ge(out_done, 16 * NT)

        @block.gpsimd
        def _(gp):
            nc.gpsimd.memset(stat[:, epsc:epsc + 1], NORM_EPS).then_inc(*step("pool"))
            nc.gpsimd.memset(stat[:, epsc + 1:epsc + 2], LN_EPS).then_inc(*step("pool", ("eps",)))

            def clear_first():
                gp.wait_ge(*done("pe", "s", 7, 2))
                gp.wait_ge(*done("dve", "preC", NPAIR - 1))
                for t in (Bf[0], At[0], Kf[0], Rt[0]):
                    nc.gpsimd.memset(t[:, :, :], 0.0).then_inc(*step("pool"))
                nc.gpsimd.memset(Zs[:, 0, :, :], 0.0).then_inc(*step("pool", ("cleared",)))

            def clear_rest():
                gp.wait_ge(*done("pe", "o", 15))
                gp.wait_ge(*done("dve", "P", 15))
                for t, name in ((XT, "cleared_XT"), (Bt, "cleared_Bt"), (Kt, "cleared_Kt")):
                    nc.gpsimd.memset(t[:, :, :], 0.0).then_inc(*step("pool", (name,)))
                for t in (Bf[1], Kf[1], At[1]):
                    nc.gpsimd.memset(t[:, :, :], 0.0).then_inc(*step("pool"))
                nc.gpsimd.memset(Rt[1][:, :, :], 0.0).then_inc(*step("pool", ("cleared_second",)))

            for n in range(len(UNITS)):
                if n == UIDX[("gate", GATE_ORDER[0])] + 1:
                    clear_first()
                if n == UIDX[("gate", GATE_ORDER[0])] + 2:
                    clear_rest()
                gp.wait_ge(*done("act", "hi", n))
                nc.gpsimd.tensor_tensor(w_lo[:, n % W_SLOTS, :], raw[:, n % RAW_SLOTS, :],
                    w_hi[:, n % W_SLOTS, :].bitcast(F32), ALU.subtract).then_inc(*step("pool", ("lo", n)))

        @block.tensor
        def _(pe):
            def begin(*label):
                banks = GATE_RING if label[0] == "gate" and ring[0] is CHUNK_RING else ring[0]
                b = banks[given[banks] % len(banks)]
                given[banks] += 1
                turn[label] = b
                if b in holder:
                    name, at_ = earlier["readers"].get(holder[b], ("dve_psum_read", 1))
                    pe.wait_ge(signal[name], at_)
                holder[b] = label
                return bank[b]

            def split3(o, wh, wl, ah, al, first, last):
                nc.tensor.matmul(o, wh, ah, start=first, stop=False)
                nc.tensor.matmul(o, wh, al, start=False, stop=False)
                return nc.tensor.matmul(o, wl, ah, start=False, stop=last)

            def feature_unit(label, *bank_label, fresh=None):
                n = UIDX[label]
                o = begin(*bank_label)
                pe.wait_ge(*done("pool", "lo", n))
                for t in range(KD):
                    if fresh:
                        pe.wait_ge(*done("dve", "hT_lo", fresh, t))
                    k = slice(t * P, (t + 1) * P)
                    mm = split3(o[:, :], w_hi[:, n % W_SLOTS, k], w_lo[:, n % W_SLOTS, k],
                                hT_hi[:, t, :], hT_lo[:, t, :], t == 0, t == KD - 1)
                mm.then_inc(*step("pe", ("unit", n), bank_label))

            def token_units(labels, outs, a_hi, a_lo, kts, cols, fresh=None):
                bs = [begin(*o) for o in outs]
                for s, label in enumerate(labels):
                    n = UIDX[label]
                    pe.wait_ge(*done("pool", "lo", n))
                    for m in range(NT):
                        for j in range(kts):
                            k = s * kts + j
                            if fresh and m == 0:
                                pe.wait_ge(*done("dve", *fresh, k))
                            c = slice(j * cols, (j + 1) * cols)
                            tok = slice(m * P, (m + 1) * P)
                            first, last = k == 0, k == kts * len(labels) - 1
                            o = bs[m][:, 0:cols]
                            nc.tensor.matmul(o, a_hi[:, k, tok], w_hi[:, n % W_SLOTS, c], start=first, stop=False)
                            nc.tensor.matmul(o, a_hi[:, k, tok], w_lo[:, n % W_SLOTS, c], start=False, stop=False)
                            mm = nc.tensor.matmul(o, a_lo[:, k, tok], w_hi[:, n % W_SLOTS, c], start=False, stop=last)
                        marks = ([outs[m]] if last else []) + ([("unit", n)] if m == NT - 1 else [])
                        if marks:
                            mm.then_inc(*step("pe", *marks))

            def transposed(tag, src, tiles):
                for k in range(tiles):
                    o = begin(tag, k)
                    for m in range(NT):
                        mm = nc.tensor.transpose(o[:, m * P:(m + 1) * P], src[:, m, k * P:(k + 1) * P], ident)
                    mm.then_inc(*step("pe", (tag, k)))

            pe.wait_ge(cst_in, 16)
            pe.wait_ge(par_in, 16 * n_par)
            for b, rows in enumerate(PARAM_USED):
                o = begin("par", b)
                nc.tensor.transpose(o[:, 0:rows], stage[0:rows, b, :], ident[0:rows, 0:rows]) \
                    .then_inc(*step("pe", ("par", b)))
            for m in range(NT):
                pe.wait_ge(*done("dve", "xn_a", m))
            transposed("na", xn_a, KD)

            for i in (12, 13, 14, 0, 1, 2, 3, 4, 5, 6, 7):
                feature_unit(("rw", i), "rw", i, fresh="na" if i == 12 else None)
            pe.wait_ge(lora_in, 64)
            pe.wait_ge(*done("act", "lora_act"))
            for i in range(NPAIR):
                c = slice(i * P, (i + 1) * P)
                o = begin("lw", i)
                nc.tensor.matmul(o[:, :], lora_w[0:64, 0, c], lora_x[0:64, 0, :], start=True, stop=True) \
                    .then_inc(*step("pe", ("lw", i)))
                o = begin("la", i)
                nc.tensor.matmul(o[:, :], lora_w[64:128, 0, c], lora_x[64:128, 0, :], start=True, stop=True) \
                    .then_inc(*step("pe", ("la", i)))
                o = begin("lg", i)
                nc.tensor.matmul(o[:, :], lora_w[:, 1, c], lora_x[:, 1, :], start=True, stop=False)
                nc.tensor.matmul(o[:, :], lora_w[0:32, 2, c], lora_x[0:32, 2, :], start=False, stop=True) \
                    .then_inc(*step("pe", ("lg", i)))
            for i in range(8, 12):
                feature_unit(("rw", i), "rw", i)

            def head_sums(tag, src, p):
                o = begin(tag, p)
                nc.tensor.matmul(o[:, :], cst("heads"), src, start=True, stop=True).then_inc(*step("pe", (tag, p)))

            def key_norm(p):
                pe.wait_ge(*done("act", "kk_sq", p))
                head_sums("kn", Sc[:, p % 2, :], p)

            def bonus_sum(p):
                pe.wait_ge(*done("dve", "rk", p))
                head_sums("bn", Sc[:, p % 2, :], p)

            for i in range(12):
                feature_unit(("qk", i), "qk", i)
                if i % 3 == 2:
                    key_norm(i // 3)
                    if i // 3 >= 1:
                        bonus_sum(i // 3 - 1)
            token_units([("v0", s) for s in range(4)], [("vt0", m) for m in range(NT)], hT_hi, hT_lo, 2, 512)
            bonus_sum(NPAIR - 1)
            token_units([("v1", s) for s in range(2)], [("vt1", m) for m in range(NT)], hT_hi, hT_lo, 4, 256)

            def scores(it):
                j, qt = it // NT, it % NT
                for g in range(3):
                    h = ATT_HG * g + j
                    r = slice(HD * (h % 2), HD * (h % 2) + HD)
                    k0 = max(0, qt - 1) if g == 0 else 0
                    n = (qt + 1 - k0) * P
                    o = begin("s", it, g)
                    nc.tensor.matmul(o[:, 0:n], qk_at(h // 2)[r, qt * P:(qt + 1) * P],
                        qk_at(6 + h // 2)[r, k0 * P:(qt + 1) * P], start=True, stop=True).then_inc(*step("pe", ("s", it, g)))

            pe.wait_ge(*done("act", "vt1", NT - 1))
            scores(0)
            scores(1)
            for it in range(16):
                if it + 2 < 16:
                    scores(it + 2)
                j, qt = it // NT, it % NT
                tiles = att_tiles(j, qt)
                pe.wait_ge(*done("dve", "P", it))
                for c in range(0, len(tiles), 4):
                    o = begin("t", it, c)
                    for x in range(c, min(c + 4, len(tiles))):
                        mm = nc.tensor.transpose(o[:, (x - c) * P:(x - c + 1) * P], Sx[:, it % 3, x * P:(x + 1) * P], ident)
                    mm.then_inc(*step("pe", ("t", it, c), ("tall", it)))
                r = slice(HD * (j % 2), HD * (j % 2) + HD)
                o = begin("o", it)
                for x, (h, kt) in enumerate(tiles):
                    if x % 4 == 0:
                        pe.wait_ge(*done("act", "pt", it, x))
                    mm = nc.tensor.matmul(o[r, 0:P], vtok[:, kt, HD * h:HD * (h + 1)], PT[:, it % 2, x, :],
                                          start=(x == 0), stop=(x == len(tiles) - 1))
                mm.then_inc(*step("pe", ("o", it)))

            def four(label, pairs):
                o = begin(*label)
                for p in range(NPAIR):
                    for x, (a, b) in enumerate(pairs):
                        mm = nc.tensor.matmul(o[:, p * CH:(p + 1) * CH], a[:, p * P:(p + 1) * P], b[:, p, :],
                                              start=(x == 0), stop=(x == len(pairs) - 1))
                mm.then_inc(*step("pe", label))

            def with_r_and_a(label, a, c):
                o = begin(*label)
                for p in range(NPAIR):
                    mm = nc.tensor.matmul(o[:, p * P:(p + 1) * P].rearrange("p (two t) -> p two t", t=CH),
                        a[:, p * P:(p + 1) * P], RA[:, :, p, c * CH:(c + 1) * CH], start=True, stop=True)
                mm.then_inc(*step("pe", label))

            def four_t(label, src):
                o = begin(*label)
                for x in range(4):
                    mm = nc.tensor.transpose(o[:, x * P:(x + 1) * P], src(x), ident)
                mm.then_inc(*step("pe", label))

            parts = [0]

            def gate_parts(k):
                for _ in range(k):
                    i, t = GATE_ORDER[parts[0] // KD], parts[0] % KD
                    n = UIDX[("gate", i)]
                    if t == 0:
                        begin("gate", i)
                        pe.wait_ge(*done("pool", "lo", n))
                    f = slice(t * P, (t + 1) * P)
                    mm = split3(bank[turn[("gate", i)]][:, :], w_hi[:, n % W_SLOTS, f], w_lo[:, n % W_SLOTS, f],
                                hT_hi[:, t, :], hT_lo[:, t, :], t == 0, t == KD - 1)
                    if t == KD - 1:
                        mm.then_inc(*step("pe", ("unit", n), ("gate", i)))
                    parts[0] += 1

            ring[0] = CHUNK_RING
            for gr in range(NCH // 2):
                both = [(s, 2 * gr + s) for s in range(2)]
                pe.wait_ge(*done("dve", "fill", gr))
                pe.wait_ge(*done("act", "fill", gr))
                cols = slice(2 * gr * CH, (2 * gr + 2) * CH)
                B, K, A, R = Bf[gr % 2], Kf[gr % 2], At[gr % 2], Rt[gr % 2]
                for s, c in both:
                    with_r_and_a(("BRA", c), B[:, s, :], c)
                    four(("A", c), [(A[:, s, :], chunk(Aa, c))])
                for lv in range(5):
                    for s, c in both:
                        pe.wait_ge(*done("dve", "X", c, lv))
                        four(("W", c, lv), [(Am[:, s, :], Xx[:, :, s, :])])
                    four_t(("XT", gr, lv), lambda p: Xx[:, p, :, :].rearrange("p s t -> p (s t)"))
                    gate_parts(PARTS_AT[0][lv])
                    if lv == 0:
                        four_t(("Vt", gr), lambda p: Vv[:, p, cols])
                        for s, c in both:
                            with_r_and_a(("KRA", c), K[:, s, :], c)
                    if lv == 1:
                        four_t(("Bt", gr), lambda p: Aa[:, p, cols])
                    if lv == 2:
                        four_t(("Kt", gr), lambda p: Kk[:, p, cols])
                    for s, c in both:
                        pe.wait_ge(*done("dve", "Wp", c, lv))
                        pe.wait_ge(*done("act", "XT", gr, lv, s))
                        four(("XW", c, lv), [(XT[:, s, :], Wp[:, s, :, :])])
                    gate_parts(PARTS_AT[1][lv])
                for s, c in both:
                    Z = Zs[:, c % 2, :, :]
                    pe.wait_ge(*done("act", "Kt", gr, s))
                    pe.wait_ge(*done("dve", "Rk", c))
                    pe.wait_ge(*done("dve", "X", c, 5))
                    if c == 0:
                        pe.wait_ge(*done("pool", "cleared"))
                    else:
                        pe.wait_ge(*done("dve", "Z", c))
                    four(("u1", c), [(A[:, s, :], Z), (Ak[:, s, :], Vt[:, s, :, :])])
                    y = begin("y", c)
                    for p in range(NPAIR):
                        h, w = slice(p * P, (p + 1) * P), slice(p * CH, (p + 1) * CH)
                        nc.tensor.matmul(y[:, w], R[:, s, h], Z[:, p, :], start=(p == 0), stop=False, skip_group_check=True)
                        nc.tensor.matmul(y[:, w], Rk[:, s, h], Vt[:, s, p, :], start=False, stop=False,
                                         skip_group_check=True)
                    gate_parts(PARTS_AT[2][s])
                    pe.wait_ge(*done("act", "U1", c))
                    four(("u2", c), [(XT[:, s, :], U1[:, s, :, :])])
                    gate_parts(PARTS_AT[3][s])
                    pe.wait_ge(*done("act", "U", c))
                    if c + 1 < NCH:
                        four(("z", c), [(Bt[:, s, :], Uu[:, s, :, :]), (Kt[:, s, :], Vt[:, s, :, :])])
                    for p in range(NPAIR):
                        h, w = slice(p * P, (p + 1) * P), slice(p * CH, (p + 1) * CH)
                        mm = nc.tensor.matmul(y[:, w], Rb[:, s, h], Uu[:, s, p, :], start=False, stop=True,
                                              skip_group_check=True)
                    mm.then_inc(*step("pe", ("y", c)))
                    gate_parts(PARTS_AT[4][s])
            ring[0] = RING

            for i in (12, 13):
                feature_unit(("gate", i), "gate", i)
            for p in range(NPAIR):
                pe.wait_ge(*done("dve", "yn", p))
                four_t(("yT", p), lambda x: KK[:, p, x * P:(x + 1) * P])
            for i in (14, 15):
                feature_unit(("gate", i), "gate", i)

            def branch(label, tag, outs, kts, a_hi, a_lo):
                n = UIDX[label]
                pe.wait_ge(*done("pool", "lo", n))
                w = UNIT // kts
                for x, i in enumerate(outs):
                    o = begin(tag, i)
                    for k in range(kts):
                        c = slice(k * w + x * P, k * w + (x + 1) * P)
                        mm = split3(o[:, :], w_hi[:, n % W_SLOTS, c], w_lo[:, n % W_SLOTS, c],
                                    a_hi[:, k, :], a_lo[:, k, :], k == 0, k == kts - 1)
                    mm.then_inc(*step("pe", (tag, i), ("unit", n)))

            for i in range(0, KD, 4):
                branch(("bb", i), "pb", range(i, i + 4), 2, yb_hi, yb_lo)
                pe.wait_ge(*done("dve", "ya_lo", NPAIR - 1))
                branch(("ba", i), "pa", range(i, i + 2), 4, ya_hi, ya_lo)
                branch(("ba", i + 2), "pa", range(i + 2, i + 4), 4, ya_hi, ya_lo)

            for h in range(2):
                token_units([("out", h, s) for s in range(4)], [("op", h, m) for m in range(NT)], mg_hi, mg_lo, 2, 512,
                            fresh=("mg_lo",) if h == 0 else None)
            for m in range(NT):
                pe.wait_ge(*done("dve", "xn_b", m))
            transposed("nb", xn_b, KD)

            for i in range(NF):
                feature_unit(("up", i), "up", i, fresh="nb" if i == 0 else None)
                feature_unit(("up", NF + i), "up", NF + i)
            for h in range(2):
                token_units([("down", h, s) for s in range(NF // 2)], [("dn", h, m) for m in range(NT)], g_hi, g_lo, 2, 512,
                            fresh=("g_lo",) if h == 0 else None)
                if h == 0:
                    pe.wait_ge(p_in, 16)
                    transposed("np", p_raw, 2)
            pe.wait_ge(*done("dve", "pT_lo", 1))
            for h in range(2):
                token_units([("ple", h)], [("pp", h, m) for m in range(NT)], pT_hi, pT_lo, 2, 512)
            for m in range(NT):
                pe.wait_ge(*done("dve", "xn_c", m))
            transposed("nc", xn_c, KD)
            for h in range(2):
                token_units([("pleg", h, s) for s in range(4)], [("pg", h, m) for m in range(NT)], hT_hi, hT_lo, 2, 512,
                            fresh=("hT_lo", "nc") if h == 0 else None)

        @block.scalar
        def _(act):
            act.dma_start(consts[:, :], ins["consts"]).then_inc(cst_in, 16)
            act.dma_start(dist[:, :], ins["dist"]).then_inc(dist_in, 16)
            act.dma_start(lora_w[0:64, 0, :], ins["rw_w_up"][0]).then_inc(lora_in, 16)
            act.dma_start(lora_w[64:128, 0, :], ins["rw_a_up"][0]).then_inc(lora_in, 16)
            act.dma_start(lora_w[:, 1, :], ins["rw_g_up"][0, 0:P, :]).then_inc(lora_in, 16)
            act.dma_start(lora_w[0:32, 2, :], ins["rw_g_up"][0, P:, :]).then_inc(lora_in, 16)
            nxt = [0]

            def hi_upto(n):
                while nxt[0] <= min(n, len(UNITS) - 1):
                    u = nxt[0]
                    act.wait_ge(landed[u % RAW_SLOTS], 16 * (u // RAW_SLOTS + 1))
                    if u >= W_SLOTS:
                        act.wait_ge(*done("pe", "unit", u - W_SLOTS))
                        act.wait_ge(*done("pool", "lo", u - W_SLOTS))
                    nc.scalar.activation(w_hi[:, u % W_SLOTS, :], raw[:, u % RAW_SLOTS, :], ACT.Copy) \
                        .then_inc(*step("act", ("hi", u)))
                    nxt[0] += 1

            def before(label):
                hi_upto(UIDX[label] + W_SLOTS)


            def squares_of(tag, src, scratch, m, h):
                c = slice(512 * h, 512 * h + 512)
                if tag == "na":
                    act.wait_ge(x_in[m], 16)
                else:
                    act.wait_ge(*done("dve", "x_" + tag, h, m))
                k = ss + NT * h + m
                nc.scalar.activation(scratch[:, (NT * h + m) % 2, :], src[:, m, c], ACT.Square,
                                     accum_out=stat[:, k:k + 1]).then_inc(*step("act", ("sq", tag, h, m)))

            def root(tag, m0=0, m1=NT):
                act.wait_ge(*done("dve", "ms", tag, m0))
                nc.scalar.activation(stat[:, rms + m0:rms + m1], stat[:, rms + m0:rms + m1], ACT.Sqrt,
                                     scale=1.0 / DM, bias=stat[:, epsc:epsc + 1]).then_inc(*step("act", ("rms", tag, m0)))

            def gained_hi(tag, gain, tiles, dst):
                for k in range(tiles):
                    act.wait_ge(*done("pe", tag, k))
                    scale = par(gain, k) if gain else 1.0
                    nc.scalar.activation(dst[:, k, :], psum((tag, k))[:, :], ACT.Copy, scale=scale) \
                        .then_inc(*step("act", ("hi", tag, k)))

            act.wait_ge(*done("pool", "eps"))
            for m in range(2):
                for h in range(2):
                    if m or h:
                        act.wait_ge(*previous("act"))
                    squares_of("na", xs, Rr, m, h)
            root("na")
            hi_upto(W_SLOTS - 1)
            act.wait_ge(*done("dve", "params"))
            gained_hi("na", "g_mix", KD, hT_hi)

            dsts = {12: lora_x[:, 0, :], 13: lora_x[:, 1, :], 14: lora_x[:, 2, :]}
            for i in range(4):
                dsts[i], dsts[4 + i], dsts[8 + i] = Rr[:, i, :], Kk[:, i, :], Vv[:, i, :]

            def shift_own(i):
                before(("rw", i))
                act.wait_ge(*done("pe", "rw", i))
                rows = 32 if i == 14 else P
                nc.scalar.activation(dsts[i][0:rows, :], psum(("rw", i))[0:rows, :], ACT.Copy,
                    scale=stat[0:rows, omm + i:omm + i + 1]).then_inc(*step("act", ("own", i)))

            act.wait_ge(*done("dve", "derived"))
            for i in (12, 13, 14, 0, 1, 2):
                shift_own(i)
            act.wait_ge(*done("dve", "shift", 14))
            nc.scalar.activation(lora_x[0:64, 0, :], lora_x[0:64, 0, :], ACT.Tanh).then_inc(*step("act"))
            nc.scalar.activation(lora_x[:, 1, :], lora_x[:, 1, :], ACT.Sigmoid).then_inc(*step("act"))
            nc.scalar.activation(lora_x[0:32, 2, :], lora_x[0:32, 2, :], ACT.Sigmoid).then_inc(*step("act", ("lora_act",)))
            for i in (3, 4, 5, 6, 7):
                shift_own(i)
            for i in range(NPAIR):
                act.wait_ge(*done("pe", "lw", i))
                nc.scalar.activation(Bo[:, i, :], psum(("lw", i))[:, :], ACT.Sigmoid, bias=par("rw_w0", i)) \
                    .then_inc(*frees("act", ("lw", i), ("lw", i)))
                act.wait_ge(*done("pe", "la", i))
                nc.scalar.activation(Aa[:, i, :], psum(("la", i))[:, :], ACT.Sigmoid, bias=par("rw_a0", i)) \
                    .then_inc(*frees("act", ("la", i), ("la", i)))
                act.wait_ge(*done("pe", "lg", i))
                nc.scalar.activation(Gg[:, i, :], psum(("lg", i))[:, :], ACT.Copy) \
                    .then_inc(*frees("act", ("lg", i), ("lg", i)))
            for i in range(8, 12):
                shift_own(i)

            def squares(p):
                act.wait_ge(*done("dve", "kkr", p))
                nc.scalar.activation(Sc[:, p % 2, :], KK[:, p, :], ACT.Square).then_inc(*step("act", ("kk_sq", p)))

            def decays(p):
                q = p % 2
                act.wait_ge(*done("dve", "L", p))
                if p >= 2:
                    act.wait_ge(*done("dve", "preC", p - 2))
                nc.scalar.activation(Et[:, q, :], Lt[:, q, :], ACT.Exp, scale=-DECAY).then_inc(*step("act"))
                nc.scalar.activation(Ei[:, q, :], Lt[:, q, :], ACT.Exp, scale=DECAY).then_inc(*step("act", ("E", p)))

            for i in range(12):
                before(("qk", i))
                act.wait_ge(*done("pe", "qk", i))
                nc.scalar.activation(qk_at(i), psum(("qk", i))[:, :], ACT.Copy,
                    scale=HD ** -0.5 if i < 6 else 1.0).then_inc(*frees("act", ("qk", i), ("qk", i)))
                if i % 3 == 0:
                    squares(i // 3)
                if i % 3 == 1:
                    decays(i // 3)
                if i % 3 == 2:
                    p = i // 3
                    act.wait_ge(*done("pe", "kn", p))
                    nc.scalar.activation(Sc[:, p % 2, :], psum(("kn", p))[:, :], ACT.Sqrt) \
                        .then_inc(*frees("act", ("kn", p), ("kn", p)))
            for c, w, n in ((0, 512, 4), (512, 256, 2)):
                tag = "vt0" if c == 0 else "vt1"
                for s in range(n):
                    before(("v0" if c == 0 else "v1", s))
                for m in range(NT):
                    act.wait_ge(*done("pe", tag, m))
                    nc.scalar.activation(vtok[:, m, c:c + w], psum((tag, m))[:, 0:w], ACT.Copy) \
                        .then_inc(*frees("act", (tag, m), (tag, m)))

            def fill(gr):
                act.wait_ge(*done("pool", "cleared" if gr == 0 else "cleared_second"))
                if gr == 0:
                    act.wait_ge(*done("dve", "preC", NPAIR - 1))
                if gr >= 2:
                    act.wait_ge(*done("pe", "y", 2 * gr - 3))
                fill_blocks("act", nc.scalar.copy, gr, ((Kf[gr % 2], Kk), (Rt[gr % 2], Rr)))

            def expo(it):
                act.wait_ge(*done("dve", "max", it))
                n = len(att_tiles(it // NT, it % NT)) * P
                nc.scalar.activation(Sx[:, it % 3, 0:n], Sx[:, it % 3, 0:n], ACT.Exp,
                    bias=stat[:, negmax + it:negmax + it + 1],
                    accum_out=stat[:, den + it:den + it + 1]).then_inc(*step("act", ("exp", it)))

            expo(0)
            for it in range(16):
                if it + 1 < 16:
                    expo(it + 1)
                j, qt = it // NT, it % NT
                n = len(att_tiles(j, qt))
                for c in range(0, n, 4):
                    w = min(4, n - c)
                    act.wait_ge(*done("pe", "t", it, c))
                    if it >= 2:
                        act.wait_ge(*done("pe", "o", it - 2))
                    nc.scalar.activation(PT[:, it % 2, c:c + w, :].rearrange("p a b -> p (a b)"),
                        psum(("t", it, c))[:, 0:w * P], ACT.Copy).then_inc(*frees("act", ("t", it, c), ("pt", it, c)))
                r = slice(HD * (j % 2), HD * (j % 2) + HD)
                act.wait_ge(*done("pe", "o", it))
                nc.scalar.activation(yb_hi[r, j // 2, qt * P:(qt + 1) * P], psum(("o", it))[r, 0:P], ACT.Copy) \
                    .then_inc(*step("act", ("yb_hi", it)))
                if it == 13:
                    fill(0)

            def gate(i):
                before(("gate", i))
                act.wait_ge(*done("pe", "gate", i))
                taken = min(GATE_ORDER.index(i) // 3, NCH // 2 - 1)
                act.wait_ge(*done("dve", "fill", taken))
                act.wait_ge(*done("act", "fill", taken))
                nc.scalar.activation(gate_at(i), psum(("gate", i))[:, :].rearrange("p (a b) -> p a b", a=4), ACT.Sigmoid,
                                     bias=par("b_gate", i)).then_inc(*frees("act", ("gate", i), ("gate", i)))

            def head_of(label, s, q):
                return psum(label)[CH * s:CH * s + CH, :].rearrange("p (h two t) -> p h two t", two=2, t=CH)[:, :, q, :]

            def as_full(label, s, dst, cleared):
                act.wait_ge(*done("pe", *label))
                if label[1] == 0:
                    act.wait_ge(*done("pool", cleared))
                for q in range(2):
                    d = dst[CH * q:CH * q + CH, :].rearrange("p (h two t) -> p h two t", two=2, t=CH)[:, :, q, :]
                    nc.scalar.activation(d, head_of(label, s, q), ACT.Copy).then_inc(*frees("act", label, label + (s,)))

            for gr in range(NCH // 2):
                both = [(s, 2 * gr + s) for s in range(2)]
                for lv in range(5):
                    for s, c in both:
                        as_full(("XT", gr, lv), s, XT[:, s, :], "cleared_XT")
                    for s, c in both:
                        if lv == 0:
                            act.wait_ge(*done("pe", "Vt", gr))
                            for q in range(2):
                                nc.scalar.activation(Vt[CH * q:CH * q + CH, s, :, :], head_of(("Vt", gr), s, q), ACT.Copy) \
                                    .then_inc(*frees("act", ("Vt", gr)))
                        if lv == 1:
                            as_full(("Bt", gr), s, Bt[:, s, :], "cleared_Bt")
                        if lv == 2:
                            as_full(("Kt", gr), s, Kt[:, s, :], "cleared_Kt")
                    if lv == 3 and gr + 1 < NCH // 2:
                        fill(gr + 1)
                gate(3 * gr)
                for s in range(2):
                    c = 2 * gr + s
                    act.wait_ge(*done("pe", "u1", c))
                    nc.scalar.activation(U1[:, s, :, :].rearrange("p h t -> p (h t)"), psum(("u1", c))[:, 0:NPAIR * CH],
                                         ACT.Copy).then_inc(*frees("act", ("u1", c), ("U1", c)))
                    act.wait_ge(*done("pe", "u2", c))
                    nc.scalar.activation(Uu[:, s, :, :].rearrange("p h t -> p (h t)"), psum(("u2", c))[:, 0:NPAIR * CH],
                                         ACT.Copy).then_inc(*frees("act", ("u2", c), ("U", c)))
                    gate(3 * gr + 1 + s)

            act.wait_ge(*done("dve", "gn_var", NCH - 1))
            nc.scalar.activation(stat[:, gn_var:gn_var + 4 * NCH], stat[:, gn_var:gn_var + 4 * NCH], ACT.Sqrt,
                                 scale=1.0 / HD, bias=stat[:, epsc + 1:epsc + 2]).then_inc(*step("act", ("gn_sd",)))
            for i in (12, 13):
                gate(i)
            for p in range(NPAIR):
                act.wait_ge(*done("pe", "yT", p))
                if p == 0:
                    act.wait_ge(*done("pe", "y", NCH - 1))
                for s in range(2):
                    for q in range(2):
                        y = yT[CH * q:CH * q + CH, p, :].rearrange("p (g two t) -> p g two t", two=2, t=CH)[:, :, s, :]
                        nc.scalar.activation(y, head_of(("yT", p), s, q), ACT.Copy) \
                            .then_inc(*frees("act", ("yT", p), ("yT", p)))
            gate(14)
            for p in range(NPAIR):
                act.wait_ge(*done("dve", "y_a", p))
                nc.scalar.activation(ya_hi[:, p, :], yT[:, p, :], ACT.Copy).then_inc(*step("act", ("ya_hi", p)))
            gate(15)
            before(("bb", 0))
            for i in range(KD):
                before(("bb" if i % 4 == 0 else "ba", i - i % 4 if i % 4 < 2 else i - i % 4 + 2))
                if i % 4 == 0:
                    before(("ba", i))
                act.wait_ge(*done("dve", "merged", i))
                nc.scalar.activation(mg_hi[:, i, :].rearrange("p (a b) -> p a b", a=4), gate_at(i), ACT.Copy).then_inc(*step("act", ("mg_hi", i)))
            for h in range(2):
                for s in range(3):
                    before(("out", h, s))
                for m in range(NT):
                    if m == NT - 1:
                        before(("out", h, 3))
                    act.wait_ge(*previous("act"))
                    squares_of("nb", xr, cbuf[:, 0, :, :], m, h)
            root("nb")
            gained_hi("nb", "g_ffn", KD, hT_hi)

            def g_split(i):
                act.wait_ge(*done("dve", "g", i))
                nc.scalar.activation(g_hi[:, i, :], cbuf[:, i % 2, 3, :], ACT.Copy).then_inc(*step("act", ("g_hi", i)))

            for i in range(NF):
                if i:
                    g_split(i - 1)
                for z, u in ((0, i), (1, NF + i)):
                    before(("up", u))
                    act.wait_ge(*done("pe", "up", u))
                    if i >= 2:
                        act.wait_ge(*done("dve", "g_lo", i - 2))
                    nc.scalar.activation(cbuf[:, i % 2, z, :], psum(("up", u))[:, :], ACT.Identity,
                        scale=par("conv_w0", u), bias=par("conv_b", u)).then_inc(*step("act", ("tap0", u)))
                act.wait_ge(*done("dve", "taps", i))
                nc.scalar.activation(cbuf[:, i % 2, 2, :], cbuf[:, i % 2, 0, :], ACT.Gelu_apprx_tanh) \
                    .then_inc(*step("act", ("gelu", i)))
            g_split(NF - 1)
            for h in range(2):
                for s in range(NF // 2 - 1):
                    before(("down", h, s))
                for m in range(NT):
                    if m == NT - 1:
                        before(("down", h, NF // 2 - 1))
                    act.wait_ge(*previous("act"))
                    squares_of("nc", xr, cbuf[:, 1, 2:4, :], m, h)
                if h == 0:
                    gained_hi("np", None, 2, pT_hi)
            root("nc")
            for h in range(2):
                before(("ple", h))
                for m in range(NT):
                    act.wait_ge(*done("pe", "pp", h, m))
                    nc.scalar.activation(pple[:, m, 512 * h:512 * h + 512], psum(("pp", h, m))[:, :], ACT.Copy) \
                        .then_inc(*frees("act", ("pp", h, m), ("pp", h, m)))
            gained_hi("nc", "g_ple", KD, hT_hi)
            for h in range(2):
                for s in range(4):
                    before(("pleg", h, s))
                for m in range(NT):
                    act.wait_ge(*done("pe", "pg", h, m))
                    if h:
                        act.wait_ge(*done("dve", "x_end", 0, m))
                    nc.scalar.activation(psig[:, m, :], psum(("pg", h, m))[:, :], ACT.Sigmoid) \
                        .then_inc(*frees("act", ("pg", h, m), ("pg", h, m)))
                for m in range(NT if h == 0 else 0):
                    act.wait_ge(*previous("act"))
                    squares_of("end", xr, junk, m, 0)
            for m in range(NT):
                act.wait_ge(*previous("act"))
                squares_of("end", xr, junk, m, 1)
                root("end", m, m + 1)

        @block.vector
        def _(dve):
            V = nc.vector


            def mean_square(tag, m0=0, m1=NT, last_m=None):
                dve.wait_ge(*done("act", "sq", tag, 1, m1 - 1 if last_m is None else last_m))
                V.tensor_tensor(stat[:, rms + m0:rms + m1], stat[:, ss + m0:ss + m1], stat[:, ss + NT + m0:ss + NT + m1],
                                ALU.add).then_inc(*step("dve", ("ms", tag, m0)))

            def gained_lo(tag, gain, tiles, dst_hi, dst, name):
                for k in range(tiles):
                    dve.wait_ge(*done("act", "hi", tag, k))
                    scale = par(gain, k) if gain else 1.0
                    V.scalar_tensor_tensor(dst[:, k, :], psum((tag, k))[:, :], scale,
                        dst_hi[:, k, :].bitcast(F32), ALU.mult, ALU.subtract) \
                        .then_inc(*frees("dve", (tag, k), (name, tag, k) if name == "hT_lo" else (name, k)))

            V.memset(stage[0:32, 0, :], 0.0).then_inc(*step("dve", ("stage",)))
            for m in (2, 3):
                for h in range(2):
                    dve.wait_ge(x_in[m], 16)
                    if m > 2 or h:
                        dve.wait_ge(*previous("dve"))
                    c, k = slice(512 * h, 512 * h + 512), ss + NT * h + m
                    V.tensor_tensor_reduce(out=Kk[:, m, :], in0=xs[:, m, c], in1=xs[:, m, c], scale=1.0, scalar=0.0,
                                           op0=ALU.mult, op1=ALU.add, accum_out=stat[:, k:k + 1]).then_inc(*step("dve"))
            dve.wait_ge(*previous("dve"))
            mean_square("na", last_m=1)
            dve.wait_ge(*done("act", "rms", "na", 0))
            V.reciprocal(stat[:, rstd:rstd + NT], stat[:, rms:rms + NT]).then_inc(*step("dve"))
            dve.wait_ge(*previous("dve"))
            for m in range(NT):
                V.tensor_scalar(xn_a[:, m, :], xs[:, m, :], stat[:, rstd + m:rstd + m + 1], None, ALU.mult) \
                    .then_inc(*step("dve", ("xn_a", m)))
            for b, rows in enumerate(PARAM_USED):
                dve.wait_ge(*done("pe", "par", b))
                V.tensor_copy(params[:, b * P:b * P + rows], psum(("par", b))[:, 0:rows]) \
                    .then_inc(*frees("dve", ("par", b), ("params",)))
            dve.wait_ge(*previous("dve"))
            c = PARAM_COL["rw_mu"]
            V.tensor_scalar(stat[:, omm:omm + 15], params[:, c:c + 15], -1.0, 1.0, ALU.mult, ALU.add).then_inc(*step("dve"))
            c = PARAM_COL["rw_k_a"]
            V.tensor_scalar(stat[:, omka:omka + 4], params[:, c:c + 4], -1.0, 1.0, ALU.mult, ALU.add) \
                .then_inc(*step("dve", ("derived",)))
            gained_lo("na", "g_mix", KD, hT_hi, hT_lo, "hT_lo")

            dsts = {12: lora_x[:, 0, :], 13: lora_x[:, 1, :], 14: lora_x[:, 2, :]}
            for i in range(4):
                dsts[i], dsts[4 + i], dsts[8 + i] = Rr[:, i, :], Kk[:, i, :], Vv[:, i, :]

            def shift(i):
                dve.wait_ge(*done("act", "own", i))
                rows = 32 if i == 14 else P
                d = dsts[i][0:rows, 1:SEQ]
                V.scalar_tensor_tensor(d, psum(("rw", i))[0:rows, 0:SEQ - 1], par("rw_mu", i, 0, rows), d,
                    ALU.mult, ALU.add).then_inc(*frees("dve", ("rw", i), ("shift", i)))

            for i in (12, 13, 14, 0, 1, 2, 3, 4, 5, 6, 7, 8, 9, 10, 11):
                shift(i)

            def pre_a(p):
                q = p % 2
                dve.wait_ge(*done("act", "lg", NPAIR - 1))
                if p == 0:
                    dve.wait_ge(*done("pe", "lg", NPAIR - 1))
                if p >= 2:
                    dve.wait_ge(*done("act", "E", p - 2))
                V.tensor_tensor_scan(Lt[:, q, :], reset, Bo[:, p, :], 0.0, ALU.mult, ALU.add) \
                    .then_inc(*step("dve", ("L", p)))
                V.tensor_scalar(KK[:, p, :], Kk[:, p, :], par("rw_k_k", p), None, ALU.mult) \
                    .then_inc(*step("dve", ("kkr", p)))

            def pre_b(p):
                sc, kk, k, a, r = Sc[:, p % 2, :], KK[:, p, :], Kk[:, p, :], Aa[:, p, :], Rr[:, p, :]
                dve.wait_ge(*done("act", "kn", p))
                V.tensor_scalar(sc, sc, 1e-12, None, ALU.max).then_inc(*step("dve"))
                dve.wait_ge(*previous("dve"))
                V.reciprocal(sc, sc).then_inc(*step("dve"))
                dve.wait_ge(*previous("dve"))
                V.tensor_tensor(kk, kk, sc, ALU.mult).then_inc(*step("dve"))
                dve.wait_ge(*previous("dve"))
                V.tensor_scalar(sc, a, par("rw_k_a", p), stat[:, omka + p:omka + p + 1], ALU.mult, ALU.add) \
                    .then_inc(*step("dve"))
                dve.wait_ge(*previous("dve"))
                V.tensor_tensor(k, k, sc, ALU.mult).then_inc(*step("dve"))
                V.tensor_tensor(a, kk, a, ALU.mult).then_inc(*step("dve"))
                dve.wait_ge(*previous("dve"))
                V.scalar_tensor_tensor(sc, r, par("rw_r_k", p), k, ALU.mult, ALU.mult).then_inc(*step("dve", ("rk", p)))

            def pre_c(p):
                q = p % 2
                kk, k, a, r = KK[:, p, :], Kk[:, p, :], Aa[:, p, :], Rr[:, p, :]
                dve.wait_ge(*done("pe", "bn", p))
                V.tensor_tensor(Bo[:, p, :], psum(("bn", p))[:, :], Vv[:, p, :], ALU.mult).then_inc(*frees("dve", ("bn", p)))
                dve.wait_ge(*previous("dve"))
                V.tensor_scalar(Bo[:, p, :], Bo[:, p, :], par("rw_ln_b", p), None, ALU.add).then_inc(*step("dve"))
                dve.wait_ge(*done("act", "E", p))
                V.tensor_tensor(a, a, Ei[:, q, :], ALU.mult).then_inc(*step("dve"))
                V.tensor_tensor(k, k, Ei[:, q, :], ALU.mult).then_inc(*step("dve"))
                V.tensor_tensor(r, r, Et[:, q, :], ALU.mult).then_inc(*step("dve"))
                e3 = Et[:, q, :].rearrange("p (c t) -> p c t", t=CH)
                k3 = kk.rearrange("p (c t) -> p c t", t=CH)
                V.tensor_copy(stat[:, ec + 8 * p:ec + 8 * p + 8].unsqueeze(2), e3[:, :, CH - 1:CH]).then_inc(*step("dve"))
                V.scalar_tensor_tensor(k3[:, :, 1:CH], k3[:, :, 1:CH], -1.0, e3[:, :, 0:CH - 1], ALU.mult, ALU.mult) \
                    .then_inc(*step("dve"))
                V.tensor_scalar(k3[:, :, 0:1], k3[:, :, 0:1], -1.0, None, ALU.mult).then_inc(*step("dve", ("preC", p)))

            pre_a(0)
            for p in range(NPAIR):
                if p + 1 < NPAIR:
                    pre_a(p + 1)
                pre_b(p)
                if p:
                    pre_c(p - 1)
            pre_c(NPAIR - 1)

            def fill(gr):
                dve.wait_ge(*done("pool", "cleared" if gr == 0 else "cleared_second"))
                if gr >= 2:
                    dve.wait_ge(*done("pe", "y", 2 * gr - 3))
                fill_blocks("dve", nc.vector.tensor_copy, gr, ((Bf[gr % 2], Aa), (At[gr % 2], KK)))

            def masked(it):
                j, qt = it // NT, it % NT
                off, base_ = 0, 0
                if it >= 3:
                    dve.wait_ge(*done("pe", "tall", it - 3))
                for g, width in enumerate((2 * P, SEQ, SEQ)):
                    k0 = max(0, qt - 1) if g == 0 else 0
                    n = (qt + 1 - k0) * P
                    dve.wait_ge(*done("pe", "s", it, g))
                    V.scalar_tensor_tensor(Sx[:, it % 3, off:off + n], dist[:, base_ + width - n:base_ + width],
                        -SLOPES[ATT_HG * g + j], psum(("s", it, g))[:, 0:n],
                        ALU.mult, ALU.add).then_inc(*frees("dve", ("s", it, g)))
                    off += n
                    base_ += width
                dve.wait_ge(*previous("dve"))
                nm = stat[:, negmax + it:negmax + it + 1]
                V.reduce_max(nm, Sx[:, it % 3, 0:off], AX_X).then_inc(*step("dve"))
                dve.wait_ge(*previous("dve"))
                V.tensor_scalar(nm, nm, -1.0, None, ALU.mult).then_inc(*step("dve", ("max", it)))

            def normalise(it):
                n = len(att_tiles(it // NT, it % NT)) * P
                dve.wait_ge(*done("act", "exp", it))
                rd = stat[:, rden + it:rden + it + 1]
                V.reciprocal(rd, stat[:, den + it:den + it + 1]).then_inc(*step("dve"))
                dve.wait_ge(*previous("dve"))
                V.tensor_scalar(Sx[:, it % 3, 0:n], Sx[:, it % 3, 0:n], rd, None, ALU.mult).then_inc(*step("dve", ("P", it)))

            def yb_rest(it):
                j, qt = it // NT, it % NT
                r, t = slice(HD * (j % 2), HD * (j % 2) + HD), slice(qt * P, (qt + 1) * P)
                dve.wait_ge(*done("act", "yb_hi", it))
                V.tensor_tensor(yb_lo[r, j // 2, t], psum(("o", it))[r, 0:P], yb_hi[r, j // 2, t].bitcast(F32),
                    ALU.subtract).then_inc(*frees("dve", ("o", it), ("yb_lo", it)))

            dve.wait_ge(dist_in, 16)
            masked(0)
            for it in range(16):
                if it + 1 < 16:
                    masked(it + 1)
                normalise(it)
                if it:
                    yb_rest(it - 1)
                if it == 13:
                    fill(0)
            yb_rest(15)

            def product(label):
                return psum(label)[:, 0:NPAIR * CH].rearrange("p (h t) -> p h t", t=CH)

            def of_pair(label, n):
                return psum(label)[:, :].rearrange("p (h two t) -> p h two t", two=2, t=CH)[:, :, n, :]

            def masked_stacked(dst, label, mask, *marks, src=None):
                dve.wait_ge(*done("pe", *label))
                V.tensor_tensor(dst, product(label) if src is None else src, cst4(mask), ALU.mult) \
                    .then_inc(*frees("dve", label, *marks))

            def masked_full(dst, label, mask, *marks, src=None):
                dve.wait_ge(*done("pe", *label))
                V.tensor_tensor(dst.rearrange("p (h two t) -> p h two t", two=2, t=CH),
                    (product(label) if src is None else src).unsqueeze(2).broadcast_to([P, NPAIR, 2, CH]),
                    cst4_full(mask), ALU.mult) \
                    .then_inc(*frees("dve", label, *marks))

            def centred(c):
                mean = stat[:, gn_mu:gn_mu + NPAIR]
                dve.wait_ge(*done("pe", "y", c))
                V.reduce_sum(mean, product(("y", c)), AX_X).then_inc(*step("dve"))
                dve.wait_ge(*previous("dve"))
                V.tensor_scalar(mean, mean, 1.0 / HD, None, ALU.mult).then_inc(*step("dve"))
                dve.wait_ge(*previous("dve"))
                V.tensor_tensor(chunk(KK, c), product(("y", c)), mean.unsqueeze(2).broadcast_to([P, NPAIR, CH]),
                    ALU.subtract).then_inc(*frees("dve", ("y", c), ("gn_d", c)))

            def squared(c):
                dve.wait_ge(*done("dve", "gn_d", c))
                V.tensor_tensor(gn_sq[:, :, :], chunk(KK, c), chunk(KK, c), ALU.mult).then_inc(*step("dve"))
                dve.wait_ge(*previous("dve"))
                V.reduce_sum(stat[:, gn_var + 4 * c:gn_var + 4 * c + 4], gn_sq[:, :, :], AX_X) \
                    .then_inc(*step("dve", ("gn_var", c)))

            for gr in range(NCH // 2):
                for s in range(2):
                    c = 2 * gr + s
                    X = Xx[:, :, s, :]
                    masked_stacked(X, ("BRA", c), "off1", src=of_pair(("BRA", c), 1))
                    masked_full(Am[:, s, :], ("A", c), "strict_ts")
                    dve.wait_ge(*previous("dve"))
                    V.tensor_tensor(X, X, cst4("ident64"), ALU.add).then_inc(*step("dve", ("X", c, 0)))
                for lv in range(5):
                    if lv == 0:
                        masked_full(Rb[:, 0, :], ("BRA", 2 * gr), "incl_st", ("Rb", 2 * gr), src=of_pair(("BRA", 2 * gr), 0))
                    for s in range(2):
                        c = 2 * gr + s
                        masked_stacked(Wp[:, s, :, :], ("W", c, lv), f"off{2 << lv}", ("Wp", c, lv))
                    if lv == 0:
                        c = 2 * gr + 1
                        masked_full(Rb[:, 1, :], ("BRA", c), "incl_st", ("Rb", c), src=of_pair(("BRA", c), 0))
                        for c in (2 * gr, 2 * gr + 1):
                            masked_full(Ak[:, c % 2, :], ("KRA", c), "strict_st", src=of_pair(("KRA", c), 1))
                    if lv == 1 and gr:
                        squared(2 * gr - 1)
                    for s in range(2):
                        c = 2 * gr + s
                        X, label = Xx[:, :, s, :], ("XW", c, lv)
                        dve.wait_ge(*done("pe", *label))
                        if lv < 4:
                            V.tensor_tensor(X, product(label), X, ALU.add).then_inc(*frees("dve", label, ("X", c, lv + 1)))
                        else:
                            for q in range(2):
                                r = slice(CH * q, CH * q + CH)
                                d = XT[r, s, :].rearrange("p (h two t) -> p h two t", two=2, t=CH)[:, :, q, :]
                                V.tensor_tensor(d, product(label)[r, :, :], X[r, :, :], ALU.add) \
                                    .then_inc(*frees("dve", label, ("X", c, 5)))
                    if lv == 0:
                        for c in (2 * gr, 2 * gr + 1):
                            masked_full(Rk[:, c % 2, :], ("KRA", c), "incl_st", ("Rk", c), src=of_pair(("KRA", c), 0))
                if gr + 1 < NCH // 2:
                    fill(gr + 1)
                for s in range(2):
                    c = 2 * gr + s
                    if c + 1 < NCH:
                        dve.wait_ge(*done("pe", "z", c))
                        if c:
                            dve.wait_ge(*done("pe", "y", c - 1))
                        Zn = Zs[:, (c + 1) % 2, :, :]
                        V.tensor_tensor(Zn, product(("z", c)), Zs[:, c % 2, :, :], ALU.add).then_inc(*frees("dve", ("z", c)))
                        dve.wait_ge(*previous("dve"))
                        e = stat[:, ec:ec + 32].rearrange("p (h c) -> p h c", c=NCH)[:, :, c:c + 1].broadcast_to([P, NPAIR, CH])
                        V.tensor_tensor(Zn, Zn, e, ALU.mult).then_inc(*step("dve", ("Z", c + 1)))
                    centred(c)
                    if s == 0 or c + 1 == NCH:
                        squared(c)

            sd = stat[:, gn_var:gn_var + 4 * NCH]
            dve.wait_ge(*done("act", "gn_sd"))
            V.reciprocal(sd, sd).then_inc(*step("dve"))
            dve.wait_ge(*previous("dve"))
            for p in range(NPAIR):
                y = KK[:, p, :].rearrange("p (c t) -> p c t", t=CH)
                each = sd.rearrange("p (c h) -> p c h", h=NPAIR)[:, :, p:p + 1].broadcast_to([P, NCH, CH])
                V.tensor_tensor(y, y, each, ALU.mult).then_inc(*step("dve", ("yn", p)))
            for p in range(NPAIR):
                y = yT[:, p, :]
                dve.wait_ge(*done("act", "yT", p))
                V.scalar_tensor_tensor(y, y, par("rw_ln_g", p), Bo[:, p, :], ALU.mult, ALU.add).then_inc(*step("dve"))
                dve.wait_ge(*previous("dve"))
                V.tensor_tensor(y, y, Gg[:, p, :], ALU.mult).then_inc(*step("dve", ("y_a", p)))
            for p in range(NPAIR):
                dve.wait_ge(*done("act", "ya_hi", p))
                V.tensor_tensor(ya_lo[:, p, :], yT[:, p, :], ya_hi[:, p, :].bitcast(F32), ALU.subtract) \
                    .then_inc(*step("dve", ("ya_lo", p)))

            def tile4(t):
                return t.rearrange("p (a b) -> p a b", a=4)

            def merged_rest(i):
                dve.wait_ge(*done("act", "mg_hi", i))
                V.tensor_tensor(tile4(mg_lo[:, i, :]), gate_at(i), tile4(mg_hi[:, i, :].bitcast(F32)), ALU.subtract) \
                    .then_inc(*step("dve", ("mg_lo", i)))

            for i in range(KD):
                if i % 4 == 0:
                    for z in range(i, i + 4):
                        dve.wait_ge(*done("pe", "pb", z))
                        dve.wait_ge(*done("act", "gate", 8 + z))
                        V.tensor_tensor(gate_at(8 + z), tile4(psum(("pb", z))[:, :]), gate_at(8 + z), ALU.mult) \
                            .then_inc(*frees("dve", ("pb", z)))
                dve.wait_ge(*done("pe", "pa", i))
                dve.wait_ge(*done("act", "gate", i))
                V.tensor_tensor(gate_at(i), tile4(psum(("pa", i))[:, :]), gate_at(i), ALU.mult).then_inc(*frees("dve", ("pa", i)))
                dve.wait_ge(*previous("dve"))
                V.tensor_tensor(gate_at(i), gate_at(i), gate_at(8 + i), ALU.add).then_inc(*step("dve", ("merged", i)))
                if i:
                    merged_rest(i - 1)
            merged_rest(KD - 1)

            def residual(tag, h, m, *marks):
                dve.wait_ge(*done("pe", tag, h, m))
                x = xr[:, m, 512 * h:512 * h + 512]
                V.tensor_tensor(x, psum((tag, h, m))[:, :], x, ALU.add).then_inc(*frees("dve", (tag, h, m), *marks))

            def rms_scaled(tag, dst, name):
                mean_square(tag)
                dve.wait_ge(*done("act", "rms", tag, 0))
                V.reciprocal(stat[:, rstd:rstd + NT], stat[:, rms:rms + NT]).then_inc(*step("dve"))
                dve.wait_ge(*previous("dve"))
                for m in range(NT):
                    V.tensor_scalar(dst[:, m, :], xr[:, m, :], stat[:, rstd + m:rstd + m + 1], None, ALU.mult) \
                        .then_inc(*step("dve", (name, m)))

            dve.wait_ge(xr_in, 16)
            for h in range(2):
                for m in range(NT):
                    residual("op", h, m, ("x_nb", h, m))
            rms_scaled("nb", xn_b, "xn_b")
            gained_lo("nb", "g_ffn", KD, hT_hi, hT_lo, "hT_lo")

            def g_rest(i):
                dve.wait_ge(*done("act", "g_hi", i))
                V.tensor_tensor(g_lo[:, i, :], cbuf[:, i % 2, 3, :], g_hi[:, i, :].bitcast(F32), ALU.subtract) \
                    .then_inc(*step("dve", ("g_lo", i)))

            for i in range(NF):
                if i:
                    g_rest(i - 1)
                for z, u in ((0, i), (1, NF + i)):
                    dve.wait_ge(*done("act", "tap0", u))
                    cv, ps = cbuf[:, i % 2, z, :], psum(("up", u))
                    V.scalar_tensor_tensor(cv[:, 1:], ps[:, 0:SEQ - 1], par("conv_w1", u), cv[:, 1:], ALU.mult, ALU.add) \
                        .then_inc(*step("dve"))
                    dve.wait_ge(*previous("dve"))
                    V.scalar_tensor_tensor(cv[:, 2:], ps[:, 0:SEQ - 2], par("conv_w2", u), cv[:, 2:], ALU.mult, ALU.add) \
                        .then_inc(*frees("dve", ("up", u), *([("taps", i)] if z == 0 else [])))
                dve.wait_ge(*done("act", "gelu", i))
                dve.wait_ge(*previous("dve"))
                V.tensor_tensor(cbuf[:, i % 2, 3, :], cbuf[:, i % 2, 2, :], cbuf[:, i % 2, 1, :], ALU.mult) \
                    .then_inc(*step("dve", ("g", i)))
            g_rest(NF - 1)
            for h in range(2):
                for m in range(NT):
                    residual("dn", h, m, ("x_nc", h, m))
                if h == 0:
                    gained_lo("np", None, 2, pT_hi, pT_lo, "pT_lo")
            rms_scaled("nc", xn_c, "xn_c")
            gained_lo("nc", "g_ple", KD, hT_hi, hT_lo, "hT_lo")
            for h in range(2):
                for m in range(NT):
                    dve.wait_ge(*done("act", "pg", h, m))
                    c = slice(512 * h, 512 * h + 512)
                    V.tensor_tensor(psig[:, m, :], psig[:, m, :], pple[:, m, c], ALU.mult).then_inc(*step("dve"))
                    dve.wait_ge(*previous("dve"))
                    V.tensor_tensor(xr[:, m, c], xr[:, m, c], psig[:, m, :], ALU.add) \
                        .then_inc(*step("dve", ("x_end", h, m)))
            dve.wait_ge(gf_in, 16)
            for m in range(NT):
                mean_square("end", m, m + 1)
                dve.wait_ge(*done("act", "rms", "end", m))
                V.reciprocal(stat[:, rstd + m:rstd + m + 1], stat[:, rms + m:rms + m + 1]).then_inc(*step("dve"))
                dve.wait_ge(*previous("dve"))
                V.scalar_tensor_tensor(xr[:, m, :], xr[:, m, :], stat[:, rstd + m:rstd + m + 1], gfin[:, :],
                    ALU.mult, ALU.mult).then_inc(*step("dve", ("final", m)))

    return {"steps": steps, "readers": readers, "turn": turn}


def att_tiles(j, qt):
    return [(ATT_HG * g + j, kt) for g in range(3) for kt in range(max(0, qt - 1) if g == 0 else 0, qt + 1)]


_INS = ["x", "p", "g_mix", "w_in", "rw_mu", "rw_w0", "rw_w_up", "rw_a0", "rw_a_up", "rw_g_up", "rw_k_k", "rw_k_a",
        "rw_r_k", "rw_ln_g", "rw_ln_b", "w_branch_a", "w_branch_b", "w_gate", "b_gate", "w_out", "g_ffn", "w_up",
        "conv_w", "conv_b", "w_down", "g_ple", "w_ple_gate", "w_ple", "g_final"]


def kernel(**inputs):
    import numpy as _np
    import concourse.bacc as _bacc
    from concourse import mybir as _mybir
    from concourse.bass_utils import run_bass_kernel_spmd as _run

    arrays = {name: _np.ascontiguousarray(inputs[name]) for name in _INS}
    arrays["consts"], arrays["dist"] = shape_constants()

    known = None
    for _ in range(2):
        nc = _bacc.Bacc("TRN2", target_bir_lowering=False, num_devices=1)
        ins = {name: nc.dram_tensor(f"in_{name}_dram", a.shape, _mybir.dt.from_np(a.dtype), kind="ExternalInput").ap()
               for name, a in arrays.items()}
        out = nc.dram_tensor("out_0_dram", (1, SEQ, DM), _mybir.dt.float32, kind="ExternalOutput").ap()
        known = build(nc, ins, out, known)
    r = _run(nc, [{f"in_{name}_dram": a for name, a in arrays.items()}], core_ids=[0])
    return r.results[0]["out_0_dram"]
```
